# Optimizing a Trainium2 kernel written in Bass

```python
import math
import jax, jax.numpy as jnp
from jax import lax
import numpy as np

D_MODEL = 1024
BATCH = 1
SEQ = 512
DEPTH = 2

GRID_W = 64
CTX_LEN = 256
N_EVEN = (DEPTH + 1) // 2
N_ODD = DEPTH // 2
EPS = 1e-6
ADA_CHUNKS = 6

H_A = 8
Q_LORA = 256
KV_LORA = 128
NOPE_DIM = 64
ROPE_DIM = 32
QK_DIM = NOPE_DIM + ROPE_DIM
V_DIM = 64
ROPE_BASE = 10000.0
Q_BLOCK = 128

H_R = 8
DK_R = 64
DV_R = 64
RET_CHUNK = 128
RET_W = H_R * DK_R

MLA_IN = Q_LORA + KV_LORA + ROPE_DIM
IN_WIDTH = MLA_IN + 4 * RET_W
MIX_W = H_A * V_DIM + H_R * DV_R

S5_GROUP = 16
S5_GROUPS = D_MODEL // S5_GROUP
S5_STATE = 64
S5_CHUNK = 128
DT_MIN = 1e-3
DT_MAX = 1e-1

D_FF = 4 * D_MODEL


def rmsnorm(x, g):
    xf = x.astype(jnp.float32)
    y = xf * lax.rsqrt(jnp.mean(xf * xf, axis=-1, keepdims=True) + EPS)
    return (y * g.astype(jnp.float32)).astype(x.dtype)

def head_norm(o):
    mu = jnp.mean(o, axis=-1, keepdims=True)
    var = jnp.mean(jnp.square(o - mu), axis=-1, keepdims=True)
    return (o - mu) * lax.rsqrt(var + EPS)

def modulate(h, shift, scale):
    return h * (1 + scale) + shift

def apply_rotary(x, ang):
    half = x.shape[-1] // 2
    cos = jnp.cos(ang)[None, :, None, :].astype(x.dtype)
    sin = jnp.sin(ang)[None, :, None, :].astype(x.dtype)
    x1, x2 = x[..., :half], x[..., half:]
    return jnp.concatenate([x1 * cos - x2 * sin, x1 * sin + x2 * cos], axis=-1)

def axial_angles(n_tok):
    rows = n_tok // GRID_W
    r = jnp.repeat(jnp.arange(rows, dtype=jnp.float32), GRID_W)
    col = jnp.tile(jnp.arange(GRID_W, dtype=jnp.float32), rows)
    nf = ROPE_DIM // 4
    f = ROPE_BASE ** (-jnp.arange(nf, dtype=jnp.float32) / nf)
    return jnp.concatenate([r[:, None] * f, col[:, None] * f], axis=-1)

def retnet_angles(n_tok):
    nf = DK_R // 2
    theta = ROPE_BASE ** (-jnp.arange(nf, dtype=jnp.float32) / nf)
    return jnp.arange(n_tok, dtype=jnp.float32)[:, None] * theta

def squared_relu_mlp(h, w1, w2):
    return jnp.square(jax.nn.relu(h @ w1)) @ w2

def mla_heads(z, q_norm_g, w_uq, kv_norm_g, w_ukv, qn_g, kn_g, ang):
    b, t = z.shape[:2]
    cq = z[..., :Q_LORA]
    ckv = z[..., Q_LORA:Q_LORA + KV_LORA]
    kr = z[..., Q_LORA + KV_LORA:]
    q = (rmsnorm(cq, q_norm_g) @ w_uq).reshape(b, t, H_A, QK_DIM)
    kv = (rmsnorm(ckv, kv_norm_g) @ w_ukv).reshape(b, t, H_A, NOPE_DIM + V_DIM)
    k = jnp.concatenate([kv[..., :NOPE_DIM], jnp.broadcast_to(kr[:, :, None, :], (b, t, H_A, ROPE_DIM))], axis=-1)
    v = kv[..., NOPE_DIM:]
    q = rmsnorm(q, qn_g)
    k = rmsnorm(k, kn_g)
    if ang is not None:
        q = jnp.concatenate([q[..., :NOPE_DIM], apply_rotary(q[..., NOPE_DIM:], ang)], axis=-1)
        k = jnp.concatenate([k[..., :NOPE_DIM], apply_rotary(k[..., NOPE_DIM:], ang)], axis=-1)
    return q, k, v

def attend(q, k, v):
    s = jnp.einsum('bqhd,bkhd->bhqk', q, k).astype(jnp.float32) * (QK_DIM ** -0.5)
    p = jax.nn.softmax(s, axis=-1).astype(v.dtype)
    return jnp.einsum('bhqk,bkhd->bqhd', p, v)

def blocked_attend(q, k, v):
    b, n_tok = q.shape[:2]
    nb = n_tok // Q_BLOCK
    qb = q.reshape(b, nb, Q_BLOCK, H_A, QK_DIM).swapaxes(0, 1)
    o = lax.map(lambda qq: attend(qq, k, v), qb)
    return o.swapaxes(0, 1).reshape(b, n_tok, H_A * V_DIM)

def ret_heads(z, ang):
    b, t = z.shape[:2]
    rq, rk, rv, rg = jnp.split(z, 4, axis=-1)
    rq = rq.reshape(b, t, H_R, DK_R).astype(jnp.float32)
    rk = rk.reshape(b, t, H_R, DK_R).astype(jnp.float32)
    rv = rv.reshape(b, t, H_R, DV_R).astype(jnp.float32)
    if ang is not None:
        rq = apply_rotary(rq, ang)
        rk = apply_rotary(rk, ang)
    return rq, rk * (DK_R ** -0.5), rv, rg

def retention_scan(q, k, v, log_gamma, s0, strict):
    b, t, h, _ = q.shape
    dv = v.shape[-1]
    n = t // RET_CHUNK
    i = jnp.arange(RET_CHUNK, dtype=jnp.float32)
    diff = i[:, None] - i[None, :]
    mask = (diff > 0) if strict else (diff >= 0)
    intra_decay = jnp.where(mask[None], jnp.exp(jnp.where(mask, diff, 0.0)[None] * log_gamma[:, None, None]), 0.0)
    q_decay = jnp.exp((i + 1)[:, None] * log_gamma[None])
    k_decay = jnp.exp((RET_CHUNK - 1 - i)[:, None] * log_gamma[None])
    chunk_decay = jnp.exp(RET_CHUNK * log_gamma)

    def blocks(a):
        return a.reshape(b, n, RET_CHUNK, h, a.shape[-1]).swapaxes(0, 1)

    def step(s, qkv):
        qc, kc, vc = qkv
        scores = jnp.einsum('bihd,bjhd->bhij', qc, kc) * intra_decay
        o = jnp.einsum('bhij,bjhe->bihe', scores, vc) + jnp.einsum('bihd,bhde->bihe', qc, s) * q_decay[None, :, :, None]
        s = s * chunk_decay[None, :, None, None] + jnp.einsum('bjhd,bjhe->bhde', kc * k_decay[None, :, :, None], vc)
        return s, o

    s_final, o = lax.scan(step, s0, (blocks(q), blocks(k), blocks(v)))
    return o.swapaxes(0, 1).reshape(b, t, h, dv), s_final

def ret_out(o, g):
    b, t = o.shape[:2]
    return head_norm(o).reshape(b, t, H_R * DV_R).astype(g.dtype) * jax.nn.silu(g)

def mla_retention_mixer(h_c, h_l, w_in, q_norm_g, w_uq, kv_norm_g, w_ukv, qn_g, kn_g, lg_f_raw, lg_b_raw, w_out, need_ctx):
    b, n_lat = h_l.shape[:2]
    z_c = h_c @ w_in
    z_l = h_l @ w_in
    q_c, k_c, v_c = mla_heads(z_c[..., :MLA_IN], q_norm_g, w_uq, kv_norm_g, w_ukv, qn_g, kn_g, None)
    q_l, k_l, v_l = mla_heads(z_l[..., :MLA_IN], q_norm_g, w_uq, kv_norm_g, w_ukv, qn_g, kn_g, axial_angles(n_lat))
    k_all = jnp.concatenate([k_c, k_l], axis=1)
    v_all = jnp.concatenate([v_c, v_l], axis=1)
    a_l = blocked_attend(q_l, k_all, v_all)
    lg_f = jnp.log1p(-jnp.exp2(lg_f_raw.astype(jnp.float32)))
    lg_b = jnp.log1p(-jnp.exp2(lg_b_raw.astype(jnp.float32)))
    rq_c, rk_c, rv_c, rg_c = ret_heads(z_c[..., MLA_IN:], None)
    rq_l, rk_l, rv_l, rg_l = ret_heads(z_l[..., MLA_IN:], retnet_angles(n_lat))
    zero = jnp.zeros((b, H_R, DK_R, DV_R), jnp.float32)
    o_cf, s_cf = retention_scan(rq_c, rk_c, rv_c, lg_f, zero, False)
    o_cb, s_cb = retention_scan(rq_c[:, ::-1], rk_c[:, ::-1], rv_c[:, ::-1], lg_b, zero, True)
    o_lf, _ = retention_scan(rq_l, rk_l, rv_l, lg_f, s_cf, False)
    o_lb, _ = retention_scan(rq_l[:, ::-1], rk_l[:, ::-1], rv_l[:, ::-1], lg_b, s_cb, True)
    r_l = ret_out(o_lf + o_lb[:, ::-1], rg_l)
    y_l = jnp.concatenate([a_l, r_l.astype(a_l.dtype)], axis=-1) @ w_out
    if need_ctx:
        a_c = attend(q_c, k_c, v_c).reshape(b, h_c.shape[1], H_A * V_DIM)
        r_c = ret_out(o_cf + o_cb[:, ::-1], rg_c)
        y_c = jnp.concatenate([a_c, r_c.astype(a_c.dtype)], axis=-1) @ w_out
    else:
        y_c = None
    return y_c, y_l

def s5_discretize(a_re, a_im, b_re, b_im, c_re, c_im, log_dt):
    f = lambda t: t.astype(jnp.float32)
    a = lax.complex(f(a_re), f(a_im))
    dt = jnp.exp(f(log_dt))[:, None]
    a_bar = jnp.exp(dt * a)
    b_bar = ((a_bar - 1) / a)[..., None] * lax.complex(f(b_re), f(b_im))
    c_mat = lax.complex(f(c_re), f(c_im))
    return a_bar, b_bar, c_mat

def _affine_compose(e1, e2):
    a1, b1 = e1
    a2, b2 = e2
    return a1 * a2, a2 * b1 + b2

def s5_scan(u, a_bar, b_bar, c_mat, x0):
    b, t = u.shape[:2]
    n = t // S5_CHUNK
    ub = u.reshape(b, n, S5_CHUNK, S5_GROUPS, S5_GROUP).swapaxes(0, 1)

    def step(x, u_blk):
        bu = jnp.einsum('btgh,gph->btgp', u_blk.astype(jnp.complex64), b_bar)
        bu = bu.at[:, 0].add(a_bar * x)
        a = jnp.broadcast_to(a_bar, bu.shape)
        _, xs = lax.associative_scan(_affine_compose, (a, bu), axis=1)
        y = jnp.einsum('btgp,ghp->btgh', xs, c_mat).real
        return xs[:, -1], y

    x_final, ys = lax.scan(step, x0, ub)
    return ys.swapaxes(0, 1).reshape(b, t, S5_GROUPS, S5_GROUP), x_final

def s5_out(y, u, d_skip, w_glu, dtype):
    b, t = u.shape[:2]
    y = (y + d_skip.astype(jnp.float32).reshape(S5_GROUPS, S5_GROUP) * u).reshape(b, t, D_MODEL)
    z = jax.nn.gelu(y).astype(dtype) @ w_glu
    za, zb = jnp.split(z, 2, axis=-1)
    return za * jax.nn.sigmoid(zb)

def s5_mixer(h_c, h_l, p_f, p_b, d_skip, w_glu, need_ctx):
    ab_f, bb_f, c_f = s5_discretize(*p_f)
    ab_b, bb_b, c_b = s5_discretize(*p_b)
    b = h_l.shape[0]
    u_c = h_c.astype(jnp.float32).reshape(b, h_c.shape[1], S5_GROUPS, S5_GROUP)
    u_l = h_l.astype(jnp.float32).reshape(b, h_l.shape[1], S5_GROUPS, S5_GROUP)
    x0 = jnp.zeros((b, S5_GROUPS, S5_STATE), jnp.complex64)
    y_cf, x_cf = s5_scan(u_c, ab_f, bb_f, c_f, x0)
    y_cb, x_cb = s5_scan(u_c[:, ::-1], ab_b, bb_b, c_b, x0)
    y_lf, _ = s5_scan(u_l, ab_f, bb_f, c_f, x_cf)
    y_lb, _ = s5_scan(u_l[:, ::-1], ab_b, bb_b, c_b, x_cb)
    out_l = s5_out(y_lf + y_lb[:, ::-1], u_l, d_skip, w_glu, h_l.dtype)
    out_c = s5_out(y_cf + y_cb[:, ::-1], u_c, d_skip, w_glu, h_c.dtype) if need_ctx else None
    return out_c, out_l

def first_inputs(seed: int = 0) -> dict:
    key = jax.random.key(seed)
    ks = iter(jax.random.split(key, 48))
    f32 = jnp.float32

    def nrm(shape, scale=1.0):
        return jax.random.normal(next(ks), shape, f32) * scale

    def gain(shape):
        return 1.0 + nrm(shape, 0.02)

    D = D_MODEL
    G, P, Hg = S5_GROUPS, S5_STATE, S5_GROUP
    n_idx = jnp.arange(P, dtype=f32)
    decay_init = -(5.0 + jnp.arange(H_R, dtype=f32))
    inputs = {
        'x': nrm((BATCH, SEQ, D)),
        'c': nrm((BATCH, D)),
        'ctx': nrm((BATCH, CTX_LEN, D)),
        'c_ctx': nrm((D,)),
        'ada_w': nrm((DEPTH, D, ADA_CHUNKS * D), 0.5 * D ** -0.5),
        'ada_b': nrm((DEPTH, ADA_CHUNKS * D), 0.02),
        'norm1_g': gain((DEPTH, D)),
        'norm2_g': gain((DEPTH, D)),
        'mlp_w1': nrm((DEPTH, D, D_FF), D ** -0.5),
        'mlp_w2': nrm((DEPTH, D_FF, D), D_FF ** -0.5),
        'w_in': nrm((N_EVEN, D, IN_WIDTH), D ** -0.5),
        'mla_q_norm_g': gain((N_EVEN, Q_LORA)),
        'mla_w_uq': nrm((N_EVEN, Q_LORA, H_A * QK_DIM), Q_LORA ** -0.5),
        'mla_kv_norm_g': gain((N_EVEN, KV_LORA)),
        'mla_w_ukv': nrm((N_EVEN, KV_LORA, H_A * (NOPE_DIM + V_DIM)), KV_LORA ** -0.5),
        'mla_qn_g': gain((N_EVEN, QK_DIM)),
        'mla_kn_g': gain((N_EVEN, QK_DIM)),
        'ret_lg_f': decay_init + nrm((N_EVEN, H_R), 0.1),
        'ret_lg_b': decay_init + nrm((N_EVEN, H_R), 0.1),
        'w_out': nrm((N_EVEN, MIX_W, D), MIX_W ** -0.5),
    }
    for d in ('f', 'b'):
        inputs['s5_a_re_' + d] = -0.5 + nrm((N_ODD, G, P), 0.01)
        inputs['s5_a_im_' + d] = jnp.pi * n_idx + nrm((N_ODD, G, P), 0.01)
        inputs['s5_b_re_' + d] = nrm((N_ODD, G, P, Hg), (2 * Hg) ** -0.5)
        inputs['s5_b_im_' + d] = nrm((N_ODD, G, P, Hg), (2 * Hg) ** -0.5)
        inputs['s5_c_re_' + d] = nrm((N_ODD, G, Hg, P), P ** -0.5)
        inputs['s5_c_im_' + d] = nrm((N_ODD, G, Hg, P), P ** -0.5)
        inputs['s5_log_dt_' + d] = math.log(DT_MIN) + jax.random.uniform(next(ks), (N_ODD, G), f32) * (math.log(DT_MAX) - math.log(DT_MIN))
    inputs['s5_d'] = nrm((N_ODD, D))
    inputs['s5_w_glu'] = nrm((N_ODD, D, 2 * D), D ** -0.5)
    return inputs

def first_block(x, c, ctx, c_ctx, ada_w, ada_b, norm1_g, norm2_g, mlp_w1, mlp_w2, w_in, mla_q_norm_g, mla_w_uq, mla_kv_norm_g, mla_w_ukv, mla_qn_g, mla_kn_g, ret_lg_f, ret_lg_b, w_out, s5_a_re_f, s5_a_im_f, s5_b_re_f, s5_b_im_f, s5_c_re_f, s5_c_im_f, s5_log_dt_f, s5_a_re_b, s5_a_im_b, s5_b_re_b, s5_b_im_b, s5_c_re_b, s5_c_im_b, s5_log_dt_b, s5_d, s5_w_glu):
    xc = ctx
    b = x.shape[0]
    for l in range(DEPTH):
        need_ctx = l < DEPTH - 1
        mod_l = (jax.nn.silu(c) @ ada_w[l] + ada_b[l]).reshape(b, ADA_CHUNKS, 1, D_MODEL)
        mod_c = (jax.nn.silu(c_ctx) @ ada_w[l] + ada_b[l]).reshape(ADA_CHUNKS, D_MODEL)
        h_l = modulate(rmsnorm(x, norm1_g[l]), mod_l[:, 0], mod_l[:, 1])
        h_c = modulate(rmsnorm(xc, norm1_g[l]), mod_c[0], mod_c[1])
        if l % 2 == 0:
            e = l // 2
            o_c, o_l = mla_retention_mixer(h_c, h_l, w_in[e], mla_q_norm_g[e], mla_w_uq[e], mla_kv_norm_g[e], mla_w_ukv[e], mla_qn_g[e], mla_kn_g[e], ret_lg_f[e], ret_lg_b[e], w_out[e], need_ctx)
        else:
            o = l // 2
            p_f = (s5_a_re_f[o], s5_a_im_f[o], s5_b_re_f[o], s5_b_im_f[o], s5_c_re_f[o], s5_c_im_f[o], s5_log_dt_f[o])
            p_b = (s5_a_re_b[o], s5_a_im_b[o], s5_b_re_b[o], s5_b_im_b[o], s5_c_re_b[o], s5_c_im_b[o], s5_log_dt_b[o])
            o_c, o_l = s5_mixer(h_c, h_l, p_f, p_b, s5_d[o], s5_w_glu[o], need_ctx)
        x = x + mod_l[:, 2] * o_l
        h_l = modulate(rmsnorm(x, norm2_g[l]), mod_l[:, 3], mod_l[:, 4])
        x = x + mod_l[:, 5] * squared_relu_mlp(h_l, mlp_w1[l], mlp_w2[l])
        if need_ctx:
            xc = xc + mod_c[2] * o_c
            h_c = modulate(rmsnorm(xc, norm2_g[l]), mod_c[3], mod_c[4])
            xc = xc + mod_c[5] * squared_relu_mlp(h_c, mlp_w1[l], mlp_w2[l])
    return x


DEPTH_2 = 1

CHUNK = 64
MEM_LEN = 256
CONV_W = 4

GDN_HEADS = 4
GDN_DK = 128
GDN_DV = 128
GDN_QK = GDN_HEADS * GDN_DK
GDN_VD = GDN_HEADS * GDN_DV
LRU_DIM = D_MODEL // 2
LRU_BLOCKS = 8
LRU_BW = LRU_DIM // LRU_BLOCKS
LRU_C = 8.0
MIX_DIM = GDN_VD + LRU_DIM
IN_SPLITS = (3 * GDN_QK, GDN_VD, GDN_HEADS, GDN_HEADS, LRU_DIM, LRU_DIM)
IN_COLS = 3 * GDN_QK + GDN_VD + 2 * GDN_HEADS + 2 * LRU_DIM

XA_HEADS = 4
XA_DH = D_MODEL // XA_HEADS

PEER_HEADS = 8
PEER_NKEYS = 128
PEER_N = PEER_NKEYS * PEER_NKEYS
PEER_DQ = 256
PEER_DH = PEER_DQ // 2
PEER_TOPK = 16
PEER_BLOCK = 128


def rmsnorm_2(x, w):
    xf = x.astype(jnp.float32)
    y = xf * lax.rsqrt(jnp.mean(xf * xf, axis=-1, keepdims=True) + EPS)
    return (y * w.astype(jnp.float32)).astype(x.dtype)

def l2norm(x):
    return x * lax.rsqrt(jnp.sum(x * x, axis=-1, keepdims=True) + EPS)

def causal_dwconv(x, w, b=None):
    s = x.shape[1]
    xp = jnp.pad(x, ((0, 0), (CONV_W - 1, 0), (0, 0)))
    y = sum(xp[:, j:j + s] * w[j] for j in range(CONV_W))
    return y if b is None else y + b

def gated_delta_rule(q, k, v, g, beta):
    bsz, s, h, dk = q.shape
    dv = v.shape[-1]
    n = s // CHUNK
    f32 = jnp.float32
    q = l2norm(q.astype(f32)) * (dk ** -0.5)
    k = l2norm(k.astype(f32))
    v = v.astype(f32)

    def chunks(t):
        return t.reshape(bsz, n, CHUNK, h, -1).transpose(0, 3, 1, 2, 4)

    qc, kc, vc = chunks(q), chunks(k), chunks(v)
    gc = g.astype(f32).reshape(bsz, n, CHUNK, h).transpose(0, 3, 1, 2)
    bc = beta.astype(f32).reshape(bsz, n, CHUNK, h).transpose(0, 3, 1, 2)
    gcum = jnp.cumsum(gc, axis=-1)
    pos = jnp.arange(CHUNK)
    causal = pos[:, None] >= pos[None, :]
    strict = pos[:, None] > pos[None, :]
    decay = jnp.exp(jnp.where(causal, gcum[..., :, None] - gcum[..., None, :], -jnp.inf))
    kb = kc * bc[..., None]
    vb = vc * bc[..., None]
    a_mat = jnp.where(strict, jnp.einsum('bhncd,bhnsd->bhncs', kb, kc) * decay, 0.0)
    t_mat = a_mat + jnp.eye(CHUNK, dtype=f32)
    rhs = jnp.concatenate([vb, kb * jnp.exp(gcum)[..., None]], axis=-1)
    sol = lax.linalg.triangular_solve(t_mat, rhs, left_side=True, lower=True, unit_diagonal=True)
    u, w = sol[..., :dv], sol[..., dv:]
    attn = jnp.where(causal, jnp.einsum('bhncd,bhnsd->bhncs', qc, kc) * decay, 0.0)
    q_dec = qc * jnp.exp(gcum)[..., None]
    k_dec = kc * jnp.exp(gcum[..., -1:] - gcum)[..., None]
    chunk_decay = jnp.exp(gcum[..., -1])

    def step(state, xs):
        q_i, w_i, u_i, a_i, k_i, d_i = xs
        v_new = u_i - jnp.einsum('bhcd,bhdv->bhcv', w_i, state)
        o = jnp.einsum('bhcd,bhdv->bhcv', q_i, state) + jnp.einsum('bhcs,bhsv->bhcv', a_i, v_new)
        state = state * d_i[..., None, None] + jnp.einsum('bhcd,bhcv->bhdv', k_i, v_new)
        return state, o

    xs = tuple(jnp.moveaxis(t, 2, 0) for t in (q_dec, w, u, attn, k_dec, chunk_decay))
    state0 = jnp.zeros((bsz, h, dk, dv), f32)
    _, o = lax.scan(step, state0, xs)
    return o.transpose(1, 0, 3, 2, 4).reshape(bsz, s, h, dv)

def rg_lru(xr, w_a, b_a, w_x, b_x, lam):
    bsz, s, c = xr.shape
    f32 = jnp.float32
    xf = xr.astype(f32)
    xb = xf.reshape(bsz, s, LRU_BLOCKS, LRU_BW)
    r = jax.nn.sigmoid(jnp.einsum('bsgi,gij->bsgj', xb, w_a.astype(f32)).reshape(bsz, s, c) + b_a.astype(f32))
    i = jax.nn.sigmoid(jnp.einsum('bsgi,gij->bsgj', xb, w_x.astype(f32)).reshape(bsz, s, c) + b_x.astype(f32))
    log_a = -LRU_C * r * jax.nn.softplus(-lam.astype(f32))
    a = jnp.exp(log_a)
    b_term = jnp.sqrt(-jnp.expm1(2.0 * log_a)) * (i * xf)

    def combine(c1, c2):
        a1, b1 = c1
        a2, b2 = c2
        return a1 * a2, a2 * b1 + b2

    _, hs = lax.associative_scan(combine, (a, b_term), axis=1)
    return hs

def hybrid_mixer(h, w_in, conv_qkv_w, gdn_a_log, gdn_dt_bias, gdn_norm_w,
                 lru_conv_w, lru_conv_b, lru_wa, lru_ba, lru_wx, lru_bx, lru_lambda, w_out):
    bsz, s, _ = h.shape
    f32 = jnp.float32
    proj = h @ w_in
    offs = np.cumsum(IN_SPLITS)[:-1].tolist()
    qkv, z, a_in, b_in, xr, gate = jnp.split(proj, offs, axis=-1)
    qkv = jax.nn.silu(causal_dwconv(qkv, conv_qkv_w))
    q, k, v = jnp.split(qkv, [GDN_QK, 2 * GDN_QK], axis=-1)
    g = -jnp.exp(gdn_a_log.astype(f32)) * jax.nn.softplus(a_in.astype(f32) + gdn_dt_bias.astype(f32))
    beta = jax.nn.sigmoid(b_in.astype(f32))
    o = gated_delta_rule(q.reshape(bsz, s, GDN_HEADS, GDN_DK), k.reshape(bsz, s, GDN_HEADS, GDN_DK),
                         v.reshape(bsz, s, GDN_HEADS, GDN_DV), g, beta)
    o = rmsnorm_2(o, gdn_norm_w) * jax.nn.silu(z.reshape(bsz, s, GDN_HEADS, GDN_DV).astype(f32))
    y_gdn = o.reshape(bsz, s, GDN_VD).astype(h.dtype)
    xr = causal_dwconv(xr, lru_conv_w, lru_conv_b)
    y_lru = (rg_lru(xr, lru_wa, lru_ba, lru_wx, lru_bx, lru_lambda) * jax.nn.gelu(gate.astype(f32))).astype(h.dtype)
    return jnp.concatenate([y_gdn, y_lru], axis=-1) @ w_out

def memory_cross_attention(h, mem_n, wq, wkv, wo):
    bsz, s, _ = h.shape
    m = mem_n.shape[1]
    f32 = jnp.float32
    q = (h @ wq).reshape(bsz, s, XA_HEADS, XA_DH)
    kv = (mem_n @ wkv).reshape(bsz, m, 2, XA_HEADS, XA_DH)
    k, v = kv[:, :, 0], kv[:, :, 1]
    scores = jnp.einsum('bshd,bmhd->bhsm', q.astype(f32), k.astype(f32)) * (XA_DH ** -0.5)
    p = jax.nn.softmax(scores, axis=-1)
    o = jnp.einsum('bhsm,bmhd->bshd', p, v.astype(f32)).reshape(bsz, s, XA_HEADS * XA_DH).astype(h.dtype)
    return o @ wo

def peer_ffn(h, wq, subkeys, u_tab, v_tab):
    bsz, s, d = h.shape
    t = h.reshape(bsz * s, d)
    ntok = t.shape[0]
    f32 = jnp.float32
    q = (t @ wq).reshape(ntok, PEER_HEADS, 2, PEER_DH).astype(f32)
    sc = jnp.einsum('thpd,hpkd->thpk', q, subkeys.astype(f32))
    s1, i1 = lax.top_k(sc[:, :, 0], PEER_TOPK)
    s2, i2 = lax.top_k(sc[:, :, 1], PEER_TOPK)
    cand = (s1[..., :, None] + s2[..., None, :]).reshape(ntok, PEER_HEADS, PEER_TOPK * PEER_TOPK)
    best, pos = lax.top_k(cand, PEER_TOPK)
    e1 = jnp.take_along_axis(i1, pos // PEER_TOPK, axis=-1)
    e2 = jnp.take_along_axis(i2, pos % PEER_TOPK, axis=-1)
    idx = e1 * PEER_NKEYS + e2
    gate = jax.nn.softmax(best, axis=-1).astype(h.dtype)
    nb = ntok // PEER_BLOCK

    def block(args):
        tb, ib, gb = args
        act = jax.nn.gelu(jnp.einsum('phkd,pd->phk', u_tab[ib], tb)) * gb
        return jnp.einsum('phk,phkd->pd', act, v_tab[ib])

    out = lax.map(block, (t.reshape(nb, PEER_BLOCK, d),
                          idx.reshape(nb, PEER_BLOCK, PEER_HEADS, PEER_TOPK),
                          gate.reshape(nb, PEER_BLOCK, PEER_HEADS, PEER_TOPK)))
    return out.reshape(bsz, s, d)

def second_inputs(seed: int = 0) -> dict:
    key = jax.random.key(seed)
    ks = jax.random.split(key, 32)
    f32 = jnp.float32
    L = DEPTH_2

    def nrm(k, shape, scale):
        return jax.random.normal(k, shape, f32) * scale

    def gain(k, shape):
        return 1.0 + 0.05 * jax.random.normal(k, shape, f32)

    x = nrm(ks[0], (BATCH, SEQ, D_MODEL), 1.0)
    mem = nrm(ks[1], (BATCH, MEM_LEN, D_MODEL), 1.0)
    norm_mix_w = gain(ks[2], (L, D_MODEL))
    w_in = nrm(ks[3], (L, D_MODEL, IN_COLS), D_MODEL ** -0.5)
    conv_qkv_w = nrm(ks[4], (L, CONV_W, 3 * GDN_QK), 0.5)
    gdn_a_log = jnp.log(jax.random.uniform(ks[5], (L, GDN_HEADS), f32, 1.0, 16.0))
    dt = jnp.exp(jax.random.uniform(ks[6], (L, GDN_HEADS), f32, np.log(1e-3), np.log(1e-1)))
    gdn_dt_bias = dt + jnp.log(-jnp.expm1(-dt))
    gdn_norm_w = gain(ks[7], (L, GDN_DV))
    lru_conv_w = nrm(ks[8], (L, CONV_W, LRU_DIM), 0.5)
    lru_conv_b = nrm(ks[9], (L, LRU_DIM), 0.01)
    lru_wa = nrm(ks[10], (L, LRU_BLOCKS, LRU_BW, LRU_BW), LRU_BW ** -0.5)
    lru_ba = nrm(ks[11], (L, LRU_DIM), 0.01)
    lru_wx = nrm(ks[12], (L, LRU_BLOCKS, LRU_BW, LRU_BW), LRU_BW ** -0.5)
    lru_bx = nrm(ks[13], (L, LRU_DIM), 0.01)
    a0 = jax.random.uniform(ks[14], (L, LRU_DIM), f32, 0.9, 0.999)
    a_base = a0 ** (1.0 / LRU_C)
    lru_lambda = jnp.log(a_base) - jnp.log1p(-a_base)
    w_out = nrm(ks[15], (L, MIX_DIM, D_MODEL), MIX_DIM ** -0.5)
    norm_xattn_w = gain(ks[16], (L, D_MODEL))
    norm_mem_w = gain(ks[17], (L, D_MODEL))
    xattn_wq = nrm(ks[18], (L, D_MODEL, XA_HEADS * XA_DH), D_MODEL ** -0.5)
    xattn_wkv = nrm(ks[19], (L, D_MODEL, 2 * XA_HEADS * XA_DH), D_MODEL ** -0.5)
    xattn_wo = nrm(ks[20], (L, XA_HEADS * XA_DH, D_MODEL), (XA_HEADS * XA_DH) ** -0.5)
    norm_ffn_w = gain(ks[21], (L, D_MODEL))
    peer_wq = nrm(ks[22], (L, D_MODEL, PEER_HEADS * PEER_DQ), D_MODEL ** -0.5)
    peer_subkeys = nrm(ks[23], (L, PEER_HEADS, 2, PEER_NKEYS, PEER_DH), PEER_DH ** -0.5)
    peer_u = nrm(ks[24], (L, PEER_N, D_MODEL), D_MODEL ** -0.5)
    peer_v = nrm(ks[25], (L, PEER_N, D_MODEL), PEER_HEADS ** -0.5)
    norm_final_w = gain(ks[26], (D_MODEL,))
    return {'x': x, 'mem': mem, 'norm_mix_w': norm_mix_w, 'w_in': w_in, 'conv_qkv_w': conv_qkv_w,
            'gdn_a_log': gdn_a_log, 'gdn_dt_bias': gdn_dt_bias, 'gdn_norm_w': gdn_norm_w,
            'lru_conv_w': lru_conv_w, 'lru_conv_b': lru_conv_b, 'lru_wa': lru_wa, 'lru_ba': lru_ba,
            'lru_wx': lru_wx, 'lru_bx': lru_bx, 'lru_lambda': lru_lambda, 'w_out': w_out,
            'norm_xattn_w': norm_xattn_w, 'norm_mem_w': norm_mem_w, 'xattn_wq': xattn_wq,
            'xattn_wkv': xattn_wkv, 'xattn_wo': xattn_wo, 'norm_ffn_w': norm_ffn_w,
            'peer_wq': peer_wq, 'peer_subkeys': peer_subkeys, 'peer_u': peer_u, 'peer_v': peer_v,
            'norm_final_w': norm_final_w}

def second_block(x, mem, norm_mix_w, w_in, conv_qkv_w, gdn_a_log, gdn_dt_bias, gdn_norm_w,
              lru_conv_w, lru_conv_b, lru_wa, lru_ba, lru_wx, lru_bx, lru_lambda, w_out,
              norm_xattn_w, norm_mem_w, xattn_wq, xattn_wkv, xattn_wo, norm_ffn_w,
              peer_wq, peer_subkeys, peer_u, peer_v, norm_final_w):
    for l in range(DEPTH_2):
        x = x + hybrid_mixer(rmsnorm_2(x, norm_mix_w[l]), w_in[l], conv_qkv_w[l], gdn_a_log[l],
                             gdn_dt_bias[l], gdn_norm_w[l], lru_conv_w[l], lru_conv_b[l],
                             lru_wa[l], lru_ba[l], lru_wx[l], lru_bx[l], lru_lambda[l], w_out[l])
        x = x + memory_cross_attention(rmsnorm_2(x, norm_xattn_w[l]), rmsnorm_2(mem, norm_mem_w[l]),
                                       xattn_wq[l], xattn_wkv[l], xattn_wo[l])
        x = x + peer_ffn(rmsnorm_2(x, norm_ffn_w[l]), peer_wq[l], peer_subkeys[l], peer_u[l], peer_v[l])
    return rmsnorm_2(x, norm_final_w)


def setup_inputs(seed=0):
    out = dict(first_inputs(seed))
    for name, value in second_inputs(seed + 1).items():
        if name != "x":
            out[name + "_2"] = value
    return out


def reference(
    x, c, ctx, c_ctx, ada_w, ada_b, norm1_g, norm2_g, mlp_w1, mlp_w2, w_in, mla_q_norm_g,
    mla_w_uq, mla_kv_norm_g, mla_w_ukv, mla_qn_g, mla_kn_g, ret_lg_f, ret_lg_b, w_out,
    s5_a_re_f, s5_a_im_f, s5_b_re_f, s5_b_im_f, s5_c_re_f, s5_c_im_f, s5_log_dt_f, s5_a_re_b,
    s5_a_im_b, s5_b_re_b, s5_b_im_b, s5_c_re_b, s5_c_im_b, s5_log_dt_b, s5_d, s5_w_glu, mem_2,
    norm_mix_w_2, w_in_2, conv_qkv_w_2, gdn_a_log_2, gdn_dt_bias_2, gdn_norm_w_2, lru_conv_w_2,
    lru_conv_b_2, lru_wa_2, lru_ba_2, lru_wx_2, lru_bx_2, lru_lambda_2, w_out_2, norm_xattn_w_2,
    norm_mem_w_2, xattn_wq_2, xattn_wkv_2, xattn_wo_2, norm_ffn_w_2, peer_wq_2, peer_subkeys_2,
    peer_u_2, peer_v_2, norm_final_w_2,
):
    x = first_block(
        x, c, ctx, c_ctx, ada_w, ada_b, norm1_g, norm2_g, mlp_w1, mlp_w2, w_in, mla_q_norm_g,
        mla_w_uq, mla_kv_norm_g, mla_w_ukv, mla_qn_g, mla_kn_g, ret_lg_f, ret_lg_b, w_out,
        s5_a_re_f, s5_a_im_f, s5_b_re_f, s5_b_im_f, s5_c_re_f, s5_c_im_f, s5_log_dt_f,
        s5_a_re_b, s5_a_im_b, s5_b_re_b, s5_b_im_b, s5_c_re_b, s5_c_im_b, s5_log_dt_b, s5_d,
        s5_w_glu,
    )
    return second_block(
        x, mem_2, norm_mix_w_2, w_in_2, conv_qkv_w_2, gdn_a_log_2, gdn_dt_bias_2, gdn_norm_w_2,
        lru_conv_w_2, lru_conv_b_2, lru_wa_2, lru_ba_2, lru_wx_2, lru_bx_2, lru_lambda_2,
        w_out_2, norm_xattn_w_2, norm_mem_w_2, xattn_wq_2, xattn_wkv_2, xattn_wo_2,
        norm_ffn_w_2, peer_wq_2, peer_subkeys_2, peer_u_2, peer_v_2, norm_final_w_2,
    )


_drawn_inputs = setup_inputs


def setup_inputs(seed=0):
    import zlib

    import numpy as np

    out = dict(_drawn_inputs(seed))
    spreads = {}
    factors = {'norm1_g': 4.287,
     'norm2_g': 2.723,
     'mla_q_norm_g': 8.0,
     'mla_kv_norm_g': 8.0,
     'mla_qn_g': 8.0,
     'mla_kn_g': 8.0,
     's5_a_re_f': 64.0,
     's5_b_re_f': 9.093,
     's5_b_im_f': 9.342,
     's5_c_re_f': 10.834,
     's5_c_im_f': 3.247,
     's5_log_dt_f': 3.242,
     's5_a_re_b': 64.0,
     's5_a_im_b': 2.691,
     's5_b_re_b': 10.15,
     's5_b_im_b': 10.375,
     's5_c_re_b': 9.755,
     's5_c_im_b': 10.37,
     's5_log_dt_b': 3.333,
     'gdn_norm_w_2': 2.764,
     'lru_conv_b_2': 2.73,
     'lru_ba_2': 41.024,
     'lru_bx_2': 8.0,
     'norm_xattn_w_2': 6.143,
     'norm_mem_w_2': 4.678,
     'norm_ffn_w_2': 8.0}
    for name, (base, spread) in spreads.items():
        noise = np.random.default_rng([zlib.crc32(name.encode()), seed]).standard_normal(out[name].shape)
        drawn = base * np.exp(spread * noise) if base else spread * noise
        out[name] = __import__('jax').numpy.asarray(drawn.astype(out[name].dtype))
    for name, factor in factors.items():
        out[name] = (out[name] * factor).astype(out[name].dtype)
    return out
```

```python
from contextlib import ExitStack

import numpy as np

import concourse.bass as bass
from concourse import mybir

F32 = mybir.dt.float32
I32 = mybir.dt.int32
U32 = mybir.dt.uint32
ALU = mybir.AluOpType
ACT = mybir.ActivationFunctionType
AX_X = mybir.AxisListType.X

P = 128
D = 1024
KD = D // P
NL = 512
NC = 256
NT = NL + NC
TBS = ((0, NL), (NL, NT))
EPS = 1e-6
GRID_W = 64
ROPE_BASE = 10000.0
H_A, Q_LORA, KV_LORA, NOPE, ROPE, V_DIM = 8, 256, 128, 64, 32, 64
QK = NOPE + ROPE
MLA_IN = Q_LORA + KV_LORA + ROPE
H_R, DK_R = 8, 64
RET_W = H_R * DK_R
S5_CH = 8
S5_DVE_STEPS = 38
MEM = 256
GH = 4
GCH = 64
XA_H = 4
PH, PNK, PTOPK = 8, 128, 16
NBANK = 8
ARENA = 22 * 1024
NSLOT = 4
SLOT = 4096


def shape_constants():
    p = np.arange(P)
    c = {}
    c["ident"] = np.eye(P)
    c["ones"] = np.ones((P, P))
    same64 = (p[:, None] // 64) == (p[None, :] // 64)
    c["blk64"] = same64 / 64.0
    rot = np.zeros((P, P))
    for i in range(ROPE // 2):
        rot[NOPE + ROPE // 2 + i, NOPE + i] = -1.0
        rot[NOPE + i, NOPE + ROPE // 2 + i] = 1.0
    c["rot_mla"] = rot
    rot = np.zeros((P, P))
    for b in range(2):
        for i in range(DK_R // 2):
            rot[64 * b + 32 + i, 64 * b + i] = -1.0
            rot[64 * b + i, 64 * b + 32 + i] = 1.0
    c["rot_ret"] = rot
    nf = ROPE // 4
    f = (np.float32(ROPE_BASE) ** (-np.arange(nf, dtype=np.float32) / np.float32(nf))).astype(np.float32)
    t = np.arange(NL)
    ang = np.concatenate([(t // GRID_W).astype(np.float32)[:, None] * f,
                          (t % GRID_W).astype(np.float32)[:, None] * f], axis=-1).astype(np.float32)
    cm, sm = np.zeros((P, NL)), np.zeros((P, NL))
    for half in range(2):
        cm[NOPE + 16 * half:NOPE + 16 * half + 16] = np.cos(ang.astype(np.float64)).T
        sm[NOPE + 16 * half:NOPE + 16 * half + 16] = np.sin(ang.astype(np.float64)).T
    c["cos_mla"], c["sin_mla"] = cm, sm
    nf = DK_R // 2
    th = (np.float32(ROPE_BASE) ** (-np.arange(nf, dtype=np.float32) / np.float32(nf))).astype(np.float32)
    ang = (t.astype(np.float32)[:, None] * th).astype(np.float32).astype(np.float64)
    c["cos_ret"] = np.tile(np.cos(ang).T, (4, 1))
    c["sin_ret"] = np.tile(np.sin(ang).T, (4, 1))
    x = np.arange(896)
    c["ret_dist"] = x[None, :] - 384.0 - p[:, None]
    tau = p // 16
    c["s5_fwd"] = np.tile((tau[:, None] <= tau[None, :]) * 1.0, (1, 4))
    c["s5_bwd"] = np.tile((tau[:, None] >= tau[None, :]) * 1.0, (1, 4))
    same = (p[:, None] // GCH) == (p[None, :] // GCH)
    c["tri_incl"] = (same & (p[:, None] <= p[None, :])) * 1.0
    c["tri_strict"] = (same & (p[:, None] < p[None, :])) * 1.0
    c["suffix"] = (same & (p[:, None] > p[None, :])) * 1.0
    c["chunk_ind"] = ((p[:, None] // GCH) == np.arange(2)[None, :]) * 1.0
    for lv in range(6):
        s = 1 << lv
        blk = (p[:, None] // (2 * s)) == (p[None, :] // (2 * s))
        c[f"merge{lv}"] = (blk & ((p[:, None] // s) % 2 == 0) & ((p[None, :] // s) % 2 == 1)) * 1.0
    c["iota16"] = np.tile(np.arange(16.0), (P, 1))
    return {k: np.ascontiguousarray(v, dtype=np.float32) for k, v in c.items()}


CONST_COLS = {}
_at = 0
for _k, _v in shape_constants().items():
    CONST_COLS[_k] = (_at, _v.shape[1])
    _at += _v.shape[1]
CONST_W = _at


def mla_order():
    for step in ("proj", "norm", "rot"):
        yield step, 0
    for n in range(6 * H_A + 2):
        if n < 6 * H_A:
            yield "scores", n
            h = n // 6 + 1
            if h < H_A and n % 6 in (1, 3, 4):
                yield {1: "proj", 3: "norm", 4: "rot"}[n % 6], h
        if 1 <= n <= 6 * H_A:
            yield "turn", n - 1
        if n >= 2:
            yield "out", n - 2


def mla_tickets(step, n):
    lat = n % 6 < 4
    return {"proj": 4, "norm": 4, "rot": 2, "scores": 2 if lat else 1, "turn": 2 if lat else 1, "out": 1}[step]


def ret_order():
    for m in range(8 * H_R + 2):
        if m < 8 * H_R:
            yield "rscore", m
        if m >= 2:
            yield "rval", m - 2


PLAN_TICKETS = [
    ("x_in", 12),
    ("vecs", 3),
    ("ada0", 24),
    ("ada1", 24),
    ("norm_l0a", 2),
    ("z_q", 4), ("z_kv", 2), ("z_kr", 2),
    ("norm_cq", 2), ("norm_ckv", 2),
    ("v_tok", 6),
    *[(f"{step}{n}", mla_tickets(step, n)) for step, n in mla_order()],
    ("z_rq", 8), ("z_rk", 8), ("z_rv", 6), ("z_rg", 8),
    ("rrot", 8),
    *[t for step, m in ret_order() for t in ([(f"rscore{m}", 1)] if step == "rscore" else
                                             [(f"rout{m // 8}_{m % 8 // 6}", 1)] if m % 8 in (0, 6) else [])],
    ("rmean", 8), ("rvar", 8),
    ("w_out", 16),
    ("norm_l0b", 2),
    ("mlp0", 128),
    ("norm_l1a", 2),
    ("s5_prm", 2), ("s5_c", 8),
    ("s5", 8 * 24),
    ("glu", 16),
    ("norm_l1b", 1),
    ("mlp1", 64),
    ("norm_mix", 1),
    ("qkv", 12), ("zg", 4), ("ab", 1), ("xr", 4), ("gate", 4),
    ("lru_r", 4), ("lru_i", 4),
    ("gnorm", 8),
    ("ktok", 4), ("vtok", 4),
    *[t for pair in range(2) for t in (
        [(f"gpre{tt}", 5) for tt in (2 * pair, 2 * pair + 1)]
        + [(f"inv{pair}_{lv}", 6) for lv in range(6)]
        + [(f"uw{tt}", 2) for tt in (2 * pair, 2 * pair + 1)])],
    ("gscan", 24),
    ("norm_o", 4),
    ("w_out2", 8),
    ("mem_in", 4), ("norm_mem", 1), ("xk", 4), ("xv", 4),
    ("norm_xat", 1), ("xq", 8),
    *[t for n in range(18) for t in ([(f"xscore{n}", 1)] * (n < 16) + [(f"xturn{n - 1}", 1)] * (1 <= n <= 16) + [(f"xout{n - 2}", 1)] * (n >= 2))],
    ("wo", 8),
    ("subk", 4), ("norm_ffn", 1),
    *[t for j in range(4) for t in ((f"pq{j}", 4), (f"psc{j}", 4))],
    ("htok", 8), ("ffn", 8),
]

PLAN_BLOCKS = [
    ("ada0", 12, lambda j: ("ada0", 2 * j + 1)),
    ("ada1", 12, lambda j: ("ada1", 2 * j + 1)),
    ("w_in0", 1, lambda j: ("z_kr", 1)),
    ("uq", 1, lambda j: (f"proj{H_A - 1}", 1)),
    ("ukv", 1, lambda j: (f"proj{H_A - 1}", 3)),
    ("w_in_r", 4, lambda j: (("z_rq", "z_rk", "z_rv", "z_rg")[j], (7, 7, 5, 7)[j])),
    ("w_out", 2, lambda j: ("w_out", 8 * j + 7)),
    ("mlp0", 16, lambda j: ("mlp0", 32 * (j // 4) + 8 * (j % 4) + 7)),
    ("glu", 4, lambda j: ("glu", 8 * (j // 2) + 7)),
    ("mlp1", 16, lambda j: ("mlp1", 16 * (j // 4) + 4 * (j % 4) + 3)),
    ("w_in2", 4, lambda j: ("qkv", 4 * j + 3) if j < 3 else ("zg", 3)),
    ("w_ab", 1, lambda j: ("ab", 0)),
    ("w_xg", 2, lambda j: (("xr", 3), ("gate", 3))[j]),
    ("w_out2", 2, lambda j: ("w_out2", 4 * j + 3)),
    ("xkv", 4, lambda j: ("xk", 2 * j + 1) if j < 2 else ("xv", 2 * (j - 2) + 1)),
    ("xq", 2, lambda j: ("xq", 4 * j + 3)),
    ("wo", 2, lambda j: ("wo", 4 * j + 3)),
    ("peer_wq", 4, lambda j: (f"pq{j}", 3)),
]


def build(nc, I, consts, out):
    ctx = ExitStack()
    with ctx:
        def sb(name, shape, dt=F32):
            return ctx.enter_context(nc.sbuf_tensor(name, shape, dt))

        sems = {}

        def S(name):
            if name not in sems:
                sems[name] = ctx.enter_context(nc.semaphore(name))
            return sems[name]

        def cst(name, rows=slice(0, P)):
            a, w = CONST_COLS[name]
            return consts[rows, a:a + w]

        def bcast(ap, n):
            return ap.unsqueeze(len(ap.shape)).to_broadcast(list(ap.shape) + [n])

        ps = [ctx.enter_context(nc.psum_tensor(f"bank{b}", [P, 512], F32)) for b in range(NBANK)]
        ticket0 = {}
        _n = 0
        for _name, _count in PLAN_TICKETS:
            ticket0[_name] = _n
            _n += _count

        def claim(pe, t, extra=0):
            if t >= NBANK:
                pe.wait_ge(S(f"bank{t % NBANK}_free"), t // NBANK + extra)
            return ps[t % NBANK]

        def fill(ins, t):
            ins.then_inc(S(f"bank{t % NBANK}_full"), 1)

        def filled(eng, t, extra=0):
            eng.wait_ge(S(f"bank{t % NBANK}_full"), t // NBANK + 1 + extra)
            return ps[t % NBANK]

        def drained(ins, t):
            ins.then_inc(S(f"bank{t % NBANK}_free"), 1)

        def emptied(eng, t, extra=0):
            eng.wait_ge(S(f"bank{t % NBANK}_free"), t // NBANK + 1 + extra)

        ring = sb("ring", [P, NSLOT, SLOT])
        block0, last_use = {}, []
        for _name, _count, _uses in PLAN_BLOCKS:
            block0[_name] = len(last_use)
            for _j in range(_count):
                _t, _o = _uses(_j)
                last_use.append(ticket0[_t] + _o)

        def load_block(eng, b, src, extra=0):
            if b >= NSLOT:
                filled(eng, last_use[b - NSLOT], extra)
            n = 1
            for s in src.shape[1:]:
                n *= s
            dst = ring[0:src.shape[0], b % NSLOT, 0:n]
            if len(src.shape) == 3:
                dst = dst.rearrange("p (a b) -> p a b", a=src.shape[1])
            if len(src.shape) == 4:
                dst = dst.rearrange("p (a b c) -> p a b c", a=src.shape[1], b=src.shape[2])
            eng.dma_start(dst, src).then_inc(S(f"weights{b % NSLOT}"), 16)

        def block(pe, b, k, extra=0, n=None):
            pe.wait_ge(S(f"weights{b % NSLOT}"), 16 * (b // NSLOT + 1) + 16 * extra)
            n = n or SLOT // k
            return ring[:, b % NSLOT, 0:k * n].rearrange("p (k n) -> p k n", k=k)

        class Steps:

            def __init__(self, name):
                self.name, self.n, self.off = name, 0, 0

            def __call__(self, eng, ins):
                self.n += 1
                ins.then_inc(S(self.name), 1)
                eng.wait_ge(S(self.name), self.n + self.off)

            def loop(self, i, per):
                self.start, self.per, self.off = self.n, per, i * per

            def end_loop(self, times):
                assert self.n - self.start == self.per, (self.name, self.n - self.start, self.per)
                self.n, self.off = self.start + self.per * times, 0

        arena = sb("arena", [P, ARENA])

        def at(off, n, parts=slice(0, P)):
            assert off + n <= ARENA, (off, n)
            return arena[parts, off:off + n]

        xT = sb("xT", [P, KD, NT])
        hT = sb("hT", [P, KD, NT])
        ident = sb("ident", [P, P])
        ones = sb("ones", [P, P])
        blk64 = sb("blk64", [P, P])
        small = sb("small", [P, 16])
        eps_col, nhalf_pi = small[:, 0:1], small[:, 1:2]
        x_in = at(0, 6 * D).rearrange("p (t d) -> p t d", t=6)
        VEC_A = [("ada_b", I["ada_b"].rearrange("l (r c) -> (l r) c", c=P)),
                 ("norm1_g", I["norm1_g"].rearrange("l (r c) -> (l r) c", c=P)),
                 ("norm2_g", I["norm2_g"].rearrange("l (r c) -> (l r) c", c=P))]
        VEC_B = [("c", I["c"].rearrange("o (r c) -> (o r) c", c=P)),
                 ("c_ctx", I["c_ctx"].rearrange("(r c) -> r c", c=P))]
        VEC_B += [(n, I[n].rearrange("o (r c) -> (o r) c", c=P)) for n in (
            "mla_q_norm_g", "mla_kv_norm_g", "s5_d", "norm_mix_w_2", "norm_xattn_w_2", "norm_mem_w_2",
            "norm_ffn_w_2", "lru_conv_b_2", "lru_ba_2", "lru_bx_2", "lru_lambda_2", "gdn_norm_w_2")]
        VEC_B += [("lru_conv_w_2", I["lru_conv_w_2"].rearrange("o j (r c) -> (o j r) c", c=P))]
        VEC_C = [("conv_qkv_w_2", I["conv_qkv_w_2"].rearrange("o j (r c) -> (o j r) c", c=P))]
        col_of = {}
        vec_rows, vec_cols = [], []
        for _i, _vec in enumerate((VEC_A, VEC_B, VEC_C)):
            _n = sum(v.shape[0] for _, v in _vec)
            vec_rows.append((at(6 * D + _i * P, P), _vec, _n))
            vec_cols.append(sb(f"vec_cols{_i}", [P, _n]))
            _r = 0
            for _name, _v in _vec:
                col_of[_name] = (_i, _r)
                _r += _v.shape[0]

        def col(name, j=0, n=1):
            i, r = col_of[name]
            return vec_cols[i][:, r + j:r + j + n]

        SMALL_LOADS = sum(len(v) for _, v, _ in vec_rows) + 3
        dve_step, act_step, pool_step = Steps("dve_done"), Steps("act_done"), Steps("pool_done")
        silu_c = sb("silu_c", [P, KD, 2])
        modT = [sb(f"modT{l}", [P, 6 * KD, 2]) for l in range(2)]
        gain1 = [sb(f"gain1_{l}", [P, KD, 2]) for l in range(2)]
        gain2 = [sb(f"gain2_{l}", [P, KD, 2]) for l in range(2)]
        rstd = sb("rstd", [P, NT])

        def norm_squares(act, tag, x, tbs, h, ready=None):
            n = tbs[-1][1]
            for k in range(KD):
                if ready:
                    ready(k)
                act.activation(h[:, k, 0:n], x[:, k, 0:n], ACT.Square).then_inc(S(f"{tag}_sq"), 1)

        def norm_sums(pe, tag, tbs, h, kd=KD, per=1):
            t0 = ticket0[f"norm_{tag}"]
            for b, (lo, hi) in enumerate(tbs):
                bank = claim(pe, t0 + b)
                for k in range(kd):
                    pe.wait_ge(S(f"{tag}_sq"), per * k + 1 + (b if per > 1 else 0))
                    last = pe.matmul(bank[:, 0:hi - lo], ones[:, :], h[:, k, lo:hi], start=(k == 0), stop=(k == kd - 1))
                fill(last, t0 + b)

        def norm_roots(act, tag, tbs, width=D, rs=rstd):
            t0 = ticket0[f"norm_{tag}"]
            for b, (lo, hi) in enumerate(tbs):
                bank = filled(act, t0 + b)
                ins = act.activation(rs[:, lo:hi], bank[:, 0:hi - lo], ACT.Sqrt, bias=eps_col, scale=1.0 / width)
                drained(ins, t0 + b)

        def norm_scale(dve, tag, x, tbs, h, gain, kd=KD, rs=rstd):
            t0 = ticket0[f"norm_{tag}"]
            n = tbs[-1][1]
            for b in range(len(tbs)):
                emptied(dve, t0 + b)
            dve_step(dve, dve.reciprocal(rs[:, 0:n], rs[:, 0:n]))
            for k in range(kd):
                for s, (lo, hi) in enumerate(tbs):
                    last = dve.scalar_tensor_tensor(h[:, k, lo:hi], x[:, k, lo:hi], gain(k, s), rs[:, lo:hi],
                                                    ALU.mult, ALU.mult)
                    last.then_inc(S(f"{tag}_mul"), 1)

        def norm_shift(act, tag, tbs, h, shift):
            for k in range(KD):
                for s, (lo, hi) in enumerate(tbs):
                    act.wait_ge(S(f"{tag}_mul"), k * len(tbs) + s + 1)
                    act.activation(h[:, k, lo:hi], h[:, k, lo:hi], ACT.Identity, bias=shift(k, s))\
                       .then_inc(S(f"{tag}_ready"), 1)

        def shift_of(l, which):
            return lambda k, s: modT[l][:, which * KD + k, s:s + 1]
        mixT = at(0, 8 * NT).rearrange("p (k n) -> p k n", k=8)
        cqT = at(6144, 2 * NT).rearrange("p (k n) -> p k n", k=2)
        ckvT = at(7680, NT)
        sqs = at(8448, 2 * NT).rearrange("p (k n) -> p k n", k=2)
        krT = at(9984, NT)
        v_tok = at(10752, 6 * 512).rearrange("p (t c) -> p t c", t=6)
        qh = at(13824, 2 * NT).rearrange("p (b n) -> p b n", b=2)
        kh = at(15360, 2 * NT).rearrange("p (b n) -> p b n", b=2)
        prob = at(16896, 2 * NT).rearrange("p (b n) -> p b n", b=2)
        probT = at(18432, 2 * NT).rearrange("p (b t n) -> p b t n", b=2, t=6)
        cos_mla, sin_mla = at(19968, NL), at(20480, NL)
        rot_mla = at(20992, P)
        rope_tmp = at(21120, NL)
        rstd_qk = at(4 * NT, 2 * NT).rearrange("p (b n) -> p b n", b=2)
        stat = sb("stat", [P, 2, 8])
        MLA_LOADS = 5
        KEYS = (slice(0, NL), slice(NL, NT))
        att_scale = QK ** -0.5
        HEADROWS = [slice(64 * (h % 2), 64 * (h % 2) + 64) for h in range(H_A)]
        rqT = at(6144, 4 * NT).rearrange("p (k n) -> p k n", k=4)
        rkT = at(9216, 4 * NT).rearrange("p (k n) -> p k n", k=4)
        rv = at(12288, 6 * 512).rearrange("p (t c) -> p t c", t=6)
        rgT = at(15360, 4 * NT).rearrange("p (k n) -> p k n", k=4)
        cos_ret, sin_ret = at(18432, NL), at(18944, NL)
        rot_ret = at(19456, P)
        decayed = at(19584, 4 * NL).rearrange("p (b n) -> p b n", b=4)
        h_flat = hT[:, :, :].rearrange("p k n -> p (k n)")
        ret_dist = h_flat[:, 0:896]
        decay_lat = [h_flat[:, 896 + 1536 * b:1792 + 1536 * b] for b in range(2)]
        decay_ctx = [h_flat[:, 1792 + 1536 * b:2432 + 1536 * b] for b in range(2)]
        decay_tmp = h_flat[:, 3968:4864]
        decay_ctx2 = h_flat[:, 4864:5504]
        lg = sb("lg", [P, 10, 2 * H_R])
        LG_RAW, LG_E, LG_U, LG_D, LG, LG_512, LG_256, LG_NEG = range(8)

        def ret_decay_slice(m):
            b, j = (m // 8) % 2, m % 8
            if j < 4:
                return decay_lat[b][:, 384 - P * j:384 - P * j + NL]
            if j < 6:
                return decay_ctx[b][:, P - P * (j - 4):P - P * (j - 4) + NL]
            return decay_lat[b][:, 384 - P * (j - 6):384 - P * (j - 6) + NC]
        MLP_Q = 4
        hid = at(0, 8 * NT).rearrange("p (m n) -> p m n", m=8)

        def mlp_loads(sp, l):
            w1 = I["mlp_w1"][l].rearrange("(k p) n -> p k n", p=P)
            w2 = I["mlp_w2"][l].rearrange("(k p) n -> p k n", p=P)

            def quarter(b0, q, extra):
                for j in range(2):
                    load_block(sp, b0 + j, w1[:, :, bass.ds(q * 1024 + j * 512, 512)], extra)
                for j in range(2):
                    load_block(sp, b0 + 2 + j, w2[:, bass.ds(q * 8, 8), j * 512:(j + 1) * 512], extra)

            quarter(block0[f"mlp{l}"], 0, 0)
            tickets = 16 * (2 if l == 0 else 1)
            with sp.Fori(0, MLP_Q - 1) as i:
                quarter(block0[f"mlp{l}"] + NSLOT, i + 1, i * (tickets // NBANK))

        def mlp_products(pe, l, tbs):
            nb = len(tbs)
            t0, uses, b0 = ticket0[f"mlp{l}"], 16 * nb // NBANK, block0[f"mlp{l}"]
            with pe.Fori(0, MLP_Q) as i:
                for part, x in enumerate((hT, hid)):
                    for j in range(2):
                        bi = b0 + 2 * part + j
                        pe.wait_ge(S(f"weights{bi % NSLOT}"), i * 16 + 16 * (bi // NSLOT + 1))
                        w = ring[:, bi % NSLOT, :].rearrange("p (k n) -> p k n", k=8)
                        for m in range(4):
                            for b, (lo, hi) in enumerate(tbs):
                                t = t0 + part * 8 * nb + (4 * j + m) * nb + b
                                bank = claim(pe, t, i * uses)
                                for k in range(8):
                                    if part == 1 and j == 0 and m == 0:
                                        pe.wait_ge(S(f"mlp{l}_hid"), i * (8 * nb) + k * nb + b + 1)
                                    last = pe.matmul(bank[:, 0:hi - lo], w[:, k, m * P:(m + 1) * P], x[:, k, lo:hi],
                                                     start=(k == 0), stop=(k == 7))
                                fill(last, t)

        def mlp_relu(act, l, tbs):
            nb = len(tbs)
            t0, uses = ticket0[f"mlp{l}"], 16 * nb // NBANK
            with act.Fori(0, MLP_Q) as i:
                for m in range(8):
                    for b, (lo, hi) in enumerate(tbs):
                        t = t0 + m * nb + b
                        bank = filled(act, t, i * uses)
                        drained(act.activation(hid[:, m, lo:hi], bank[:, 0:hi - lo], ACT.Relu), t)

        def mlp_square_and_add(dve, l, tbs):
            nb = len(tbs)
            t0, uses = ticket0[f"mlp{l}"], 16 * nb // NBANK
            with dve.Fori(0, MLP_Q) as i:
                for m in range(8):
                    for b, (lo, hi) in enumerate(tbs):
                        emptied(dve, t0 + m * nb + b, i * uses)
                        dve.tensor_tensor(hid[:, m, lo:hi], hid[:, m, lo:hi], hid[:, m, lo:hi], ALU.mult)\
                           .then_inc(S(f"mlp{l}_hid"), 1)
                for m in range(8):
                    for b, (lo, hi) in enumerate(tbs):
                        t = t0 + 8 * nb + m * nb + b
                        bank = filled(dve, t, i * uses)
                        drained(dve.scalar_tensor_tensor(xT[:, m, lo:hi], bank[:, 0:hi - lo], modT[l][:, 5 * KD + m, b:b + 1],
                                                         xT[:, m, lo:hi], ALU.mult, ALU.add), t)

        def tickets_emptied(eng, name, k, nb, first=0):
            for b in range(nb):
                emptied(eng, ticket0[name] + first + k * nb + b)
        NPR = 32
        NCH, LCH, CCH = NT // S5_CH, NL // S5_CH, NC // S5_CH
        DIRS = ("f", "b")
        s5_b = at(0, 2048).rearrange("p (d c r h) -> p d c r h", d=2, c=2, r=NPR)
        s5_c = at(2048, 2048).rearrange("p (d c r h) -> p d c r h", d=2, c=2, r=NPR)
        s5_pw = at(4096, 1152).rearrange("p (c d r k) -> p c d r k", c=2, d=2, r=NPR)
        s5_qp = at(5248, 896).rearrange("p (k c d r) -> p k c d r", k=7, c=2, d=2)
        s5_r8 = at(6144, 64).rearrange("p (d r) -> p d r", d=2)
        s5_qi = at(6208, 112).rearrange("p (k c d r) -> p k c d r", k=7, c=2, d=2)
        s5_prm = at(6208, 192).rearrange("p (d j r) -> p d j r", d=2, j=3)
        c_rows = at(6400, 4096).rearrange("p (a t x) -> p a t x", a=4, t=8)
        prep = at(10496, 24 * 64).rearrange("p (j d r) -> p j d r", j=24, d=2)
        prm_rows = at(12032, 256).rearrange("p (d x) -> p d x", d=2)
        prep_big = at(12288, 2048).rearrange("p (j r h) -> p j r h", j=4, r=NPR)
        dt_rows = at(12288, 4, slice(64, 96)).rearrange("p (d x) -> p d x", d=2)
        _o = 6400
        def s5_buf(n):
            global_off[0] += n
            return at(global_off[0] - n, n)
        global_off = [_o]
        s5_hs = s5_buf(1024)
        s5_ytok = s5_hs
        s5_utok = s5_buf(1024)
        s5_u = s5_buf(8 * NCH).rearrange("p (g c) -> p g c", g=8)
        s5_F = s5_buf(2048).rearrange("p (d c r x) -> p d c r x", d=2, c=2, r=4)
        s5_E = s5_buf(2048).rearrange("p (d c r x) -> p d c r x", d=2, c=2, r=4)
        s5_FT = s5_buf(1024).rearrange("p (c r x) -> p c r x", c=2, r=4)
        s5_M = s5_buf(1024).rearrange("p (g x) -> p g x", g=8)
        s5_g = s5_buf(768).rearrange("p (c r n) -> p c r n", c=2, r=4)
        s5_w = s5_buf(768).rearrange("p (c r n) -> p c r n", c=2, r=4)
        s5_tab = s5_buf(1536).rearrange("p (c d r n) -> p c d r n", c=2, d=2, r=4)
        s5_decay = s5_buf(768).rearrange("p (d r n) -> p d r n", d=2, r=4)
        s5_s = s5_buf(1024).rearrange("p (d c r n) -> p d c r n", d=2, c=2, r=4)
        s5_tmp = s5_buf(1024)
        s5_tmpP = s5_buf(1024)
        glu_sig = at(0, 4 * NL).rearrange("p (b n) -> p b n", b=4)
        s5_mask = s5_buf(2 * P).rearrange("p (d x) -> p d x", d=2)
        S5_LOADS = 2 * (2 + 4 + 2) + 2
        T_U, T_UT, T_FT, T_FI, T_MM, T_Y, T_YB = 0, 4, (6, 10), (8, 12), (14, 16), 18, 22

        def s5_t(i):
            return ticket0["s5"] + i

        def lead(ap, n):
            return ap.unsqueeze(2).to_broadcast([ap.shape[0], ap.shape[1], n, ap.shape[2]])
        TBL = TBS[:1]
        NTL = NL // P
        qkvT = at(0, 12 * NL).rearrange("p (m n) -> p m n", m=12)
        zT = at(6144, 4 * NL).rearrange("p (m n) -> p m n", m=4)
        k_tok = at(8192, 2048).rearrange("p (t h d) -> p t h d", t=4, h=4)
        u_tok = at(10240, 2048).rearrange("p (t h d) -> p t h d", t=4, h=4)
        mix2 = at(12288, 4096).rearrange("p (m n) -> p m n", m=8)
        xrT = at(16384, 2048).rearrange("p (m n) -> p m n", m=4)
        gateT = at(18432, 2048).rearrange("p (m n) -> p m n", m=4)
        lru_w = at(20480, 1024).rearrange("p (a m j) -> p a m j", a=2, m=4)
        lru_r, lru_i, lru_a, lru_th, lru_h = (h_flat[:, 512 * n:512 * n + 512] for n in range(5))
        inv_x = at(4096, 1024).rearrange("p (t h c) -> p t h c", t=2, h=4)
        inv_xt = at(5120, 1024).rearrange("p (t h c) -> p t h c", t=2, h=4)
        g_at = at(16384, 1024).rearrange("p (t h c) -> p t h c", t=2, h=4)
        inv_y = at(17408, 1024).rearrange("p (t h c) -> p t h c", t=2, h=4)
        attnT = at(18432, 2048).rearrange("p (t h c) -> p t h c", t=4, h=4)
        g_dec = at(20480, 1024).rearrange("p (t h c) -> p t h c", t=2, h=4)
        g_kbT = at(21504, 512).rearrange("p (h c) -> p h c", h=4)
        g_bc = at(22016, 512).rearrange("p (h c) -> p h c", h=4)
        g_masks = h_flat[:, 0:1026]
        tri_incl, g_suffix, g_ind = g_masks[:, 0:P], g_masks[:, P:2 * P], g_masks[:, 1024:1026]
        merge = [g_masks[:, 256 + P * lv:256 + P * (lv + 1)] for lv in range(6)]
        v_new = h_flat[:, 1028:1540]
        g_lvl = h_flat[:, 1540:2564].rearrange("p (t h c) -> p t h c", t=2, h=4)
        wT = h_flat[:, 2564:4612].rearrange("p (h n) -> p h n", h=4)
        g_kw = h_flat[:, 4612:5124].rearrange("p (h d) -> p h d", h=4)
        g_state = h_flat[:, 5124:5636].rearrange("p (h d) -> p h d", h=4)
        spare = h_flat[:, 7 * NT + NL:8 * NT]
        gt = spare[:, 0:160].rearrange("p (v t h) -> p v t h", v=10, t=4)
        G_A, G_B, G_E, G_U, G_LN, G_G, G_BETA, G_ABS, G_T, G_BE = range(10)
        qk_sq = at(8192, 4096).rearrange("p (m n) -> p m n", m=8)
        qk_rt = [at(12288, 2048).rearrange("p (m n) -> p m n", m=4)[:, m] if m < 4 else h_flat[:, 2564 + 512 * (m - 4):3076 + 512 * (m - 4)] for m in range(8)]
        o_rt = h_flat[:, 2564:4612].rearrange("p (m n) -> p m n", m=4)
        gs = spare[:, 160:224].rearrange("p (t c) -> p t c", t=4)
        gx = sb("gx", [P, 4, 16])
        gpar = sb("gpar", [P, 2, 4])
        lam = spare[:, 224:256].rearrange("p (v m) -> p v m", v=8)
        MIX2_LOADS = 6
        GHALF = (slice(0, GCH), slice(GCH, P))
        def bc4(ap):
            return ap.unsqueeze(1).to_broadcast([P, 4, ap.shape[1]])
        def bc24(ap):
            return ap.unsqueeze(1).to_broadcast([P, 8, ap.shape[1]])
        def pair8(ap):
            return ap.rearrange("p t h c -> p (t h) c")
        mem_in = at(0, 2 * D).rearrange("p (t d) -> p t d", t=2)
        memT = at(2048, KD * MEM).rearrange("p (k n) -> p k n", k=KD)
        mem_h = at(4096, KD * MEM).rearrange("p (k n) -> p k n", k=KD)
        xqT = at(6144, KD * NL).rearrange("p (k n) -> p k n", k=KD)
        xkT = at(10240, KD * MEM).rearrange("p (k n) -> p k n", k=KD)
        xoT = at(12288, KD * NL).rearrange("p (k n) -> p k n", k=KD)
        xv_tok = at(16384, 2 * D).rearrange("p (t d) -> p t d", t=2)
        xprob = at(18432, 2 * MEM).rearrange("p (b n) -> p b n", b=2)
        xprobT = at(18944, 2 * MEM).rearrange("p (b t n) -> p b t n", b=2, t=2)
        rstd_mem = at(19456, MEM)
        TBM = ((0, MEM),)
        XDH = D // XA_H
        xat_scale = XDH ** -0.5
        XAT_ORDER = [(s, n - o) for n in range(18) for o, s in enumerate(("xscore", "xturn", "xout")) if 0 <= n - o < 16]
        NVEC = 2 * PH
        h_tok = at(0, NTL * D).rearrange("p (t d) -> p t d", t=NTL)
        pqT = at(4096, 4096).rearrange("p (b v n) -> p b v n", b=2, v=4)
        subT = at(8192, NVEC * P).rearrange("p (v n) -> p v n", v=NVEC)
        sub_rows = at(10240, NVEC * P).rearrange("p (v d) -> p v d", v=NVEC)
        psc = at(12288, 1024).rearrange("p (b v n) -> p b v n", b=2, v=4)
        s_top = at(13312, 64).rearrange("p (h s k) -> p h s k", h=2, s=2)
        i_top = at(13376, 64).bitcast(U32).rearrange("p (h s k) -> p h s k", h=2, s=2)
        i_f = at(13440, 64).rearrange("p (h s k) -> p h s k", h=2, s=2)
        cand = at(13504, 512).rearrange("p (h c) -> p h c", h=2)
        pos_u = at(14016, 32).bitcast(U32).rearrange("p (h k) -> p h k", h=2)
        pos_f, pos_hi, pos_lo, pos_r = (at(14048 + 32 * n, 32).rearrange("p (h k) -> p h k", h=2) for n in range(4))
        onehot = at(14176, 1024).rearrange("p (s h k j) -> p s h k j", s=2, h=2, k=PTOPK)
        e_half = at(15200, 64).rearrange("p (s h k) -> p s h k", s=2, h=2)
        best = at(15264, 512).rearrange("p (t h k) -> p t h k", t=NTL, h=PH)
        idxs = at(15776, 512).bitcast(U32).rearrange("p (t e) -> p t e", t=NTL)
        gate = at(16288, 512).rearrange("p (t e) -> p t e", t=NTL)
        gate_sum = at(16800, 32)
        iota16 = at(16832, 16)
        dots, gelus, acts = (at(16848 + 8 * n, 8) for n in range(3))
        fin = at(16872, 8)
        wide_ident = at(4096, 7 * P)
        idx_now = [at(21760 + 8 * n, 8).bitcast(U32) for n in range(2)]
        diag = at(16880, 1024).rearrange("p (s n) -> p s n", s=8)
        sq_junk = at(17904, D)
        w_final, out_tile = at(19712, D), at(20736, D)
        ERING = 8
        u_row = [ring[:, s // 4, s % 4 * D:(s % 4 + 1) * D] for s in range(ERING)]
        v_row = [ring[:, 2 + s // 4, s % 4 * D:(s % 4 + 1) * D] for s in range(ERING)]
        EXPERTS = PH * PTOPK
        EGROUPS = EXPERTS // ERING
        UNITS = [(j, t) for j in range(4) for t in range(NTL)]

        block_ = ctx.enter_context(nc.Block())

        @block_.sync
        def _(sp):
            for t in range(6):
                src = I["x"][0, t * P:(t + 1) * P, :] if t < 4 else I["ctx"][0, (t - 4) * P:(t - 3) * P, :]
                sp.dma_start(x_in[:, t, :], src).then_inc(S("x_landed"), 16)
            for l in range(2):
                ada_w = I["ada_w"][l].rearrange("(k p) n -> p k n", p=P)
                for s in range(NSLOT):
                    load_block(sp, block0[f"ada{l}"] + s, ada_w[:, :, s * 512:(s + 1) * 512])
                with sp.Fori(0, 2) as i:
                    for s in range(NSLOT):
                        load_block(sp, block0[f"ada{l}"] + NSLOT + s, ada_w[:, :, bass.ds((i + 1) * (NSLOT * 512) + s * 512, 512)],
                                   extra=i)
            load_block(sp, block0["w_in0"], I["w_in"][0].rearrange("(k p) n -> p k n", p=P)[:, :, 0:MLA_IN])
            load_block(sp, block0["uq"], I["mla_w_uq"][0].rearrange("(k p) n -> p k n", p=P))
            load_block(sp, block0["ukv"], I["mla_w_ukv"][0])
            w_in_v = I["w_in"][0].rearrange("(k p) n -> p k n", p=P)
            for j in range(4):
                load_block(sp, block0["w_in_r"] + j, w_in_v[:, :, MLA_IN + j * RET_W:MLA_IN + (j + 1) * RET_W])
            for j in range(2):
                load_block(sp, block0["w_out"] + j, I["w_out"][0].rearrange("(k p) n -> p k n", p=P)[:, :, j * 512:(j + 1) * 512])
            mlp_loads(sp, 0)
            for j in range(4):
                load_block(sp, block0["glu"] + j, I["s5_w_glu"][0].rearrange("(k p) n -> p k n", p=P)[
                    :, :, D * (j % 2) + 512 * (j // 2):D * (j % 2) + 512 * (j // 2) + 512])
            mlp_loads(sp, 1)
            w_in2 = I["w_in_2"][0].rearrange("(k p) n -> p k n", p=P)
            for j in range(4):
                load_block(sp, block0["w_in2"] + j, w_in2[:, :, j * 512:(j + 1) * 512])
            load_block(sp, block0["w_ab"], w_in2[:, :, 2048:2056])
            for j in range(2):
                load_block(sp, block0["w_xg"] + j, w_in2[:, :, 2056 + j * 512:2568 + j * 512])
            for j in range(2):
                load_block(sp, block0["w_out2"] + j, I["w_out_2"][0].rearrange("(k p) n -> p k n", p=P)[:, :, j * 512:(j + 1) * 512])
            filled(sp, ticket0["norm_o"] + 3)
            for t in range(2):
                sp.dma_start(mem_in[:, t, :], I["mem_2"][0, t * P:(t + 1) * P, :]).then_inc(S("mem_landed"), 16)
            wkv = I["xattn_wkv_2"][0].rearrange("(k p) n -> p k n", p=P)
            for j in range(4):
                load_block(sp, block0["xkv"] + j, wkv[:, :, j * 512:(j + 1) * 512])
            for name, src in (("xq", "xattn_wq_2"), ("wo", "xattn_wo_2")):
                for j in range(2):
                    load_block(sp, block0[name] + j, I[src][0].rearrange("(k p) n -> p k n", p=P)[:, :, j * 512:(j + 1) * 512])
            filled(sp, ticket0["xscore15"])
            for dst, src in ((sub_rows, I["peer_subkeys_2"][0].rearrange("h s k d -> k (h s) d")), (iota16, cst("iota16")),
                             (w_final, I["norm_final_w_2"].partition_broadcast(P))):
                sp.dma_start(dst, src).then_inc(S("peer_landed"), 16)
            for j in range(4):
                load_block(sp, block0["peer_wq"] + j, I["peer_wq_2"][0].rearrange("(k p) n -> p k n", p=P)[:, :, j * 512:(j + 1) * 512])
            for T_ in range(NTL):
                sp.wait_ge(S("out_ready"), T_ + 1)
                sp.dma_start(out[0, T_ * P:(T_ + 1) * P, :], out_tile).then_inc(S("out_done"), 16)
            sp.wait_ge(S("out_done"), 16 * NTL)

        @block_.gpsimd
        def _(pool):
            for tile, name in ((ident, "ident"), (ones, "ones"), (blk64, "blk64")):
                pool.dma_start(tile[:, :], cst(name)).then_inc(S("small_landed"), 16)
            for tile, vec, _ in vec_rows:
                r = 0
                for name, v in vec:
                    pool.dma_start(tile[r:r + v.shape[0], :], v).then_inc(S("small_landed"), 16)
                    r += v.shape[0]
            for n in range(12):
                emptied(pool, ticket0["x_in"] + n)
            for i in range(3):
                emptied(pool, ticket0["vecs"] + i)
            for tile, name in ((cos_mla, "cos_mla"), (sin_mla, "sin_mla"), (rot_mla, "rot_mla")):
                pool.dma_start(tile, cst(name)).then_inc(S("mla_tables"), 16)
            for j, name in ((2, "mla_qn_g"), (3, "mla_kn_g")):
                pool.dma_start(small[0:QK, j:j + 1], I[name].rearrange("o q -> q o")).then_inc(S("mla_tables"), 16)
            for j, name in enumerate(("ret_lg_f", "ret_lg_b")):
                pool.dma_start(lg[:, LG_RAW, j * H_R:(j + 1) * H_R], I[name][0].partition_broadcast(P)).then_inc(S("lg_landed"), 16)
            emptied(pool, ticket0[f"out{6 * H_A - 1}"])
            emptied(pool, ticket0["z_rq"])
            for tile, name in ((cos_ret, "cos_ret"), (sin_ret, "sin_ret"), (rot_ret, "rot_ret")):
                pool.dma_start(tile, cst(name)).then_inc(S("ret_tables"), 16)
            for j in range(8):
                filled(pool, ticket0["z_rg"] + j)
            pool.dma_start(ret_dist, cst("ret_dist")).then_inc(S("dist_landed"), 16)
            for n in range(8):
                emptied(pool, ticket0["mlp0"] + 120 + n)
            for d, x in enumerate(DIRS):
                for c, part in enumerate(("re", "im")):
                    pool.dma_start(s5_b[:, d, c], I[f"s5_b_{part}_{x}"][0].rearrange("(r two) p h -> (two p) r h", two=2))\
                        .then_inc(S("s5_landed"), 16)
                    for half in range(2):
                        pool.dma_start(c_rows[:, 2 * d + c, :, 64 * half:64 * half + 64],
                                       I[f"s5_c_{part}_{x}"][0].rearrange("(t g) h p -> (g h) t p", t=8)).then_inc(S("s5_landed"), 16)
                for j, part in enumerate(("re", "im")):
                    pool.dma_start(prm_rows[32 * j:32 * j + 32, d, :], I[f"s5_a_{part}_{x}"][0].rearrange("(r two) p -> r (two p)", two=2))\
                        .then_inc(S("s5_landed"), 16)
                pool.dma_start(dt_rows[:, d, :], I[f"s5_log_dt_{x}"][0].rearrange("(r two) -> r two", two=2)).then_inc(S("s5_dt"), 16)
            for d, x in enumerate(("s5_fwd", "s5_bwd")):
                pool.dma_start(s5_mask[:, d, :], cst(x)[:, 0:P]).then_inc(S("s5_landed"), 16)
            pool.wait_ge(S("s5_dt"), 32)
            for d in range(2):
                pool.tensor_copy(prm_rows[64:96, d, :].rearrange("r (two p) -> r two p", two=2), bcast(dt_rows[:, d, :], 64)).then_inc(S("s5_dt_rows"), 1)
            pool.wait_ge(S("s5_prep"), 1)
            pool_step(pool, pool.memset(s5_tab[:, 0, :, :, 0:1], 1.0))
            pool_step(pool, pool.memset(s5_tab[:, 1, :, :, 0:1], 0.0))
            pool_step(pool, pool.memset(s5_decay[:, :, :, NCH - 1:NCH], 0.0))
            with pool.Fori(0, 8) as i:
                pool_step.loop(i, 1 + 7 * 6 + 2 * 6)
                pool.wait_ge(S("s5_turned"), 2 * i + 1)
                pool.nop(nofuse=True)
                pool_step(pool, pool.tensor_copy(s5_qi, s5_qp[:, :, :, :, bass.ds(i * 4, 4)]))
                pool.nop(nofuse=True)
                for d in range(2):
                    pool.tensor_copy(s5_decay[:, d, :, 0:NCH - 1], bcast(s5_r8[:, d, bass.ds(i * 4, 4)], NCH - 1)).then_inc(S("s5_decays"), 1)
                for k in range(7):
                    n = min(1 << k, NCH - (1 << k))
                    lo, hi = slice(0, n), slice(1 << k, (1 << k) + n)
                    re, im = s5_tab[:, 0], s5_tab[:, 1]
                    qr, qi = (bcast(s5_qi[:, k, c], n) for c in range(2))
                    t1 = s5_tmpP[:, 0:8 * n].rearrange("p (d r n) -> p d r n", d=2, r=4)
                    t2 = s5_tmpP[:, 512:512 + 8 * n].rearrange("p (d r n) -> p d r n", d=2, r=4)
                    pool_step(pool, pool.tensor_tensor(t1, re[:, :, :, lo], qr, ALU.mult))
                    pool_step(pool, pool.tensor_tensor(t2, im[:, :, :, lo], qi, ALU.mult))
                    pool_step(pool, pool.tensor_tensor(re[:, :, :, hi], t1, t2, ALU.subtract))
                    pool_step(pool, pool.tensor_tensor(t1, re[:, :, :, lo], qi, ALU.mult))
                    pool_step(pool, pool.tensor_tensor(t2, im[:, :, :, lo], qr, ALU.mult))
                    ins = pool.tensor_tensor(im[:, :, :, hi], t1, t2, ALU.add)
                    pool_step(pool, ins)
                filled(pool, s5_t(T_Y + 3), (i - 1) * 3)
                for d in range(2):
                    ks = slice(0, 8) if d == 0 else slice(1, 9)
                    pr, pi = (bcast(s5_pw[:, c, d, bass.ds(i * 4, 4), ks], 16) for c in range(2))
                    cr, ci = (lead(s5_c[:, d, c, bass.ds(i * 4, 4), :], 8) for c in range(2))
                    t1, t2, er, ei = (x.rearrange("p (r k h) -> p r k h", r=4, k=8) for x in (
                        s5_tmpP[:, 0:512], s5_tmpP[:, 512:1024], s5_E[:, d, 0].rearrange("p r x -> p (r x)"),
                        s5_E[:, d, 1].rearrange("p r x -> p (r x)")))
                    if d == 1:
                        er, ei = er[:, :, ::-1, :], ei[:, :, ::-1, :]
                    pool.nop(nofuse=True)
                    pool_step(pool, pool.tensor_tensor(t1, pr, cr, ALU.mult))
                    pool.nop(nofuse=True)
                    pool_step(pool, pool.tensor_tensor(t2, pi, ci, ALU.mult))
                    pool_step(pool, pool.tensor_tensor(er, t1, t2, ALU.add))
                    pool.nop(nofuse=True)
                    pool_step(pool, pool.tensor_tensor(t1, pr, ci, ALU.mult))
                    pool.nop(nofuse=True)
                    pool_step(pool, pool.tensor_tensor(t2, pi, cr, ALU.mult))
                    pool_step(pool, pool.tensor_tensor(ei, t1, t2, ALU.subtract))
                pool_step.end_loop(8)
            pool.dma_start(gpar[:, 0, :], I["gdn_a_log_2"][0].partition_broadcast(P)).then_inc(S("mix2_landed"), 16)
            pool.dma_start(gpar[:, 1, :], I["gdn_dt_bias_2"][0].partition_broadcast(P)).then_inc(S("mix2_landed"), 16)
            for n in range(8):
                emptied(pool, ticket0["mlp1"] + 56 + n)
            pool_step(pool, pool.memset(lru_w[:, :, :, :], 0.0))
            for a, name in enumerate(("lru_wa_2", "lru_wx_2")):
                for b in range(2):
                    pool.dma_start(lru_w[64 * b:64 * b + 64, a, :, 64 * b:64 * b + 64],
                                   I[name][0].rearrange("(c two) i j -> two i c j", two=2)[b]).then_inc(S("mix2_landed"), 16)
            pool.wait_ge(S("lru_done"), 4)
            for j, name in enumerate(["tri_incl", "suffix"] + [f"merge{lv}" for lv in range(6)] + ["chunk_ind"]):
                pool.dma_start(g_masks[:, P * j:P * j + CONST_COLS[name][1]], cst(name)).then_inc(S("g_masks"), 16)
            pool.wait_ge(S("peer_idx"), len(UNITS))
            filled(pool, ticket0["pq3"] + 3)
            for T_ in range(NTL):
                with pool.Fori(0, EGROUPS // 2) as i:
                    pool_step.loop(i, 2)
                    for half in range(2):
                        pool_step(pool, pool.tensor_copy(idx_now[half], idxs[:, T_, bass.ds(i * (2 * ERING) + half * ERING, ERING)]))
                        for rows, table, used, landed in ((u_row, "peer_u_2", "u_used", "u_landed"), (v_row, "peer_v_2", "v_used", "v_landed")):
                            for s in range(ERING):
                                pool.wait_ge(S(used), i * (2 * ERING) + T_ * EXPERTS + half * ERING + s + 1)
                                pool.nop(nofuse=True)
                                pool.indirect_dma_start(rows[s], None, I[table][0], bass.IndirectOffsetOnAxis(idx_now[half][:, s:s + 1], 0))\
                                    .then_inc(S(f"{landed}{s}"), 16)
                    pool_step.end_loop(EGROUPS // 2)

        @block_.scalar
        def _(act):
            for n in range(1, 12, 2):
                t, g = n // 2, n % 2
                bank = filled(act, ticket0["x_in"] + n)
                drained(act.activation(xT[:, 4 * g:4 * g + 4, t * P:(t + 1) * P],
                                       bank[:, :].rearrange("p (k n) -> p k n", k=4), ACT.Copy), ticket0["x_in"] + n)
            for i in range(3):
                emptied(act, ticket0["vecs"] + i)
            for s, name in enumerate(("c", "c_ctx")):
                act_step(act, act.activation(silu_c[:, :, s], col(name, 0, KD), ACT.Silu))
            for n in range(12):
                emptied(act, ticket0["x_in"] + n)
            norm_squares(act, "l0a", xT, TBS, hT)
            norm_roots(act, "l0a", TBS)
            norm_shift(act, "l0a", TBS, hT, shift_of(0, 0))
            for m in range(4):
                for b, (lo, hi) in enumerate(TBS):
                    t = ticket0["z_q"] + 2 * m + b
                    bank = filled(act, t)
                    if m < 3:
                        sq, raw = (sqs[:, m, lo:hi], cqT[:, m, lo:hi]) if m < 2 else (prob[:, 0, lo:hi], ckvT[:, lo:hi])
                        act.activation(sq, bank[:, 0:hi - lo], ACT.Square).then_inc(S("cq_sq" if m < 2 else "ckv_sq"), 1)
                        drained(act.activation(raw, bank[:, 0:hi - lo], ACT.Copy), t)
                    else:
                        drained(act.activation(krT[NOPE:QK, lo:hi], bank[NOPE:QK, 0:hi - lo], ACT.Copy), t)
            norm_roots(act, "cq", TBS, Q_LORA)
            norm_roots(act, "ckv", TBS, KV_LORA, rs=rstd_qk[:, 0, :])
            for t in range(1, 6, 2):
                bank = filled(act, ticket0["v_tok"] + t)
                drained(act.activation(v_tok[:, t, :], bank[:, :], ACT.Copy), ticket0["v_tok"] + t)
            for step, n in mla_order():
                t0 = ticket0[f"{step}{n}"]
                if step == "proj":
                    for b, (lo, hi) in enumerate(TBS):
                        bank = filled(act, t0 + b)
                        act.activation(qh[0:QK, n % 2, lo:hi], bank[0:QK, 0:hi - lo], ACT.Copy).then_inc(S("q_raw"), 1)
                        drained(act.activation(sqs[0:QK, 0, lo:hi], bank[0:QK, 0:hi - lo], ACT.Square), t0 + b)
                    for b, (lo, hi) in enumerate(TBS):
                        bank = filled(act, t0 + 2 + b)
                        act.activation(sqs[0:NOPE, 1, lo:hi], bank[0:NOPE, 0:hi - lo], ACT.Square)
                        drained(act.activation(kh[0:NOPE, n % 2, lo:hi], bank[0:NOPE, 0:hi - lo], ACT.Copy), t0 + 2 + b)
                    act_step(act, act.activation(kh[NOPE:QK, n % 2, :], krT[NOPE:QK, :], ACT.Copy))
                    act.activation(sqs[NOPE:QK, 1, :], krT[NOPE:QK, :], ACT.Square).then_inc(S("qk_sq"), 1)
                elif step == "norm":
                    for j in range(2):
                        for b, (lo, hi) in enumerate(TBS):
                            t = t0 + 2 * j + b
                            bank = filled(act, t)
                            drained(act.activation(rstd_qk[0:QK, j, lo:hi], bank[0:QK, 0:hi - lo], ACT.Sqrt,
                                                   bias=eps_col[0:QK], scale=1.0 / QK), t)
                elif step == "scores":
                    act.wait_ge(S("score_max"), n + 1)
                    for b, keys in enumerate(KEYS if n % 6 < 4 else KEYS[1:]):
                        bank = filled(act, t0 + b)
                        drained(act.activation(prob[:, n % 2, keys], bank[:, 0:keys.stop - keys.start], ACT.Exp,
                                               bias=stat[:, n % 2, 3:4], scale=att_scale,
                                               accum_out=stat[:, n % 2, 4 + b:5 + b]), t0 + b)
                elif step == "turn":
                    b = mla_tickets("turn", n) - 1
                    bank = filled(act, t0 + b)
                    drained(act.activation(probT[:, n % 2, 4:6, :], bank[:, 0:2 * P].rearrange("p (t n) -> p t n", t=2), ACT.Copy),
                            t0 + b)
            for name, x, scale in (("z_rq", rqT, 1.0), ("z_rk", rkT, DK_R ** -0.5)):
                for m in range(4):
                    for b, (lo, hi) in enumerate(TBS):
                        t = ticket0[name] + 2 * m + b
                        bank = filled(act, t)
                        drained(act.activation(x[:, m, lo:hi], bank[:, 0:hi - lo], ACT.Copy, scale=scale), t)
            for m in range(4):
                for b, (lo, hi) in enumerate(TBS):
                    t = ticket0["z_rg"] + 2 * m + b
                    bank = filled(act, t)
                    drained(act.activation(rgT[:, m, lo:hi], bank[:, 0:hi - lo], ACT.Silu), t)
            act.wait_ge(S("lg_landed"), 32)
            act.activation(lg[:, LG_E, :], lg[:, LG_RAW, :], ACT.Exp, scale=float(np.log(2.0))).then_inc(S("lg_exp"), 1)
            act.wait_ge(S("lg_u"), 1)
            act.activation(lg[:, LG, :], lg[:, LG_U, :], ACT.Ln).then_inc(S("lg_ln"), 1)
            act.wait_ge(S("dist_landed"), 16)
            act.wait_ge(S("lg_ready"), 1)
            for step, m in ret_order():
                h, j = m // 8, m % 8
                if step == "rscore" and j == 0:
                    for sc, of, dst in ((LG, LG_512, decay_ctx[h % 2]), (LG_NEG, LG_256, None)):
                        d = h if sc == LG else H_R + h
                        if h >= 2:
                            emptied(act, ticket0[f"rscore{8 * (h - 1) - 1}"])
                        if dst is None:
                            dst = decay_ctx2
                            if h >= 1:
                                act.wait_ge(S("decay_ready"), h)
                        act.activation(dst, ret_dist[:, 0:640], ACT.Exp, bias=lg[:, of, d:d + 1],
                                       scale=lg[:, sc, d:d + 1]).then_inc(S("decay_exp"), 1)
                    act.wait_ge(S("decay_arg"), h + 1)
                    act.activation(decay_lat[h % 2], decay_tmp, ACT.Exp).then_inc(S("decay_exp"), 1)
                elif step == "rval" and j in (5, 7):
                    t = ticket0[f"rout{h}_{j // 6}"]
                    bank = filled(act, t)
                    q = slice(0, NL) if j == 5 else KEYS[1]
                    drained(act.activation(mixT[HEADROWS[h], 4 + h // 2, q], bank[HEADROWS[h], 0:q.stop - q.start], ACT.Copy), t)
            for c in range(4):
                for b, (lo, hi) in enumerate(TBS):
                    emptied(act, ticket0["rmean"] + 2 * c + b)
                    act.activation(rqT[:, c, lo:hi], mixT[:, 4 + c, lo:hi], ACT.Square).then_inc(S("ret_sq"), 1)
            for c in range(4):
                for b, (lo, hi) in enumerate(TBS):
                    t = ticket0["rvar"] + 2 * c + b
                    bank = filled(act, t)
                    drained(act.activation(rkT[:, c, lo:hi], bank[:, 0:hi - lo], ACT.Sqrt, bias=eps_col), t)
            norm_squares(act, "l0b", xT, TBS, hT, lambda k: tickets_emptied(act, "w_out", k, 2))
            norm_roots(act, "l0b", TBS)
            norm_shift(act, "l0b", TBS, hT, shift_of(0, 3))
            mlp_relu(act, 0, TBS)
            norm_squares(act, "l1a", xT, TBS, hT, lambda k: tickets_emptied(act, "mlp0", k, 2, 112))
            norm_roots(act, "l1a", TBS)
            norm_shift(act, "l1a", TBS, hT, shift_of(1, 0))
            for n in range(8):
                a, half = n // 2, n % 2
                t = ticket0["s5_c"] + n
                bank = filled(act, t)
                for par in range(2):
                    rows = slice(64 * par, 64 * par + 64)
                    ins = act.activation(s5_c[rows, a // 2, a % 2, 16 * half:16 * half + 16, :],
                                         bank[rows, :].rearrange("p (r two h) -> p r two h", r=16, two=2)[:, :, par, :],
                                         ACT.Copy, scale=1.0 - 2.0 * (a % 2))
                drained(ins, t)
            act.wait_ge(S("s5_prm_ready"), 1)
            act.activation(prep[:, 0], s5_prm[:, :, 2, :], ACT.Exp).then_inc(S("s5_act"), 1)
            act.wait_ge(S("s5_args"), 1)
            act.activation(prep[:, 4], prep[:, 1], ACT.Exp).then_inc(S("s5_act"), 1)
            act.activation(prep[:, 5], prep[:, 1], ACT.Exp, scale=-1.0).then_inc(S("s5_act"), 1)
            act.activation(s5_r8, prep[:, 1], ACT.Exp, scale=float(S5_CH)).then_inc(S("s5_act"), 1)
            act.activation(prep[:, 6], prep[:, 2], ACT.Sin).then_inc(S("s5_act"), 1)
            act.activation(prep[:, 7], prep[:, 3], ACT.Sin).then_inc(S("s5_act"), 1)
            with act.Fori(0, 8) as i:
                filled(act, s5_t(T_YB + 1), (i - 1) * 3)
                act.activation(s5_hs[:, 0:NT], hT[:, bass.ds(i, 1), :].squeeze(1), ACT.Copy).then_inc(S("s5_hs"), 1)
                ut = s5_utok.rearrange("p (g t h) -> p t g h", g=8, t=8)
                for n in range(4):
                    t = s5_t(T_U + n)
                    bank = filled(act, t, 3 * i)
                    for j in range(2):
                        ins = act.activation(ut[0:NCH, 2 * n + j], bank[0:NCH, j * P:(j + 1) * P].rearrange("p (g h) -> p g h", g=8), ACT.Copy)
                    drained(ins, t)
                for n in range(2):
                    t = s5_t(T_UT + n)
                    bank = filled(act, t, 3 * i)[:, 0:4 * NCH].rearrange("p (g c) -> p g c", g=4)
                    act.activation(s5_u[:, 4 * n:4 * n + 4, CCH:NCH], bank[:, :, 0:LCH], ACT.Copy)
                    drained(act.activation(s5_u[:, 4 * n:4 * n + 4, 0:CCH], bank[:, :, LCH:NCH], ACT.Copy), t)
                for d in range(2):
                    for c in range(2):
                        t = s5_t(T_FT[d] + c)
                        bank = filled(act, t, 3 * i)
                        drained(act.activation(s5_FT[:, c], bank[:, :].rearrange("p (r x) -> p r x", r=4), ACT.Copy), t)
                yt = s5_ytok.rearrange("p (t g h) -> p g t h", t=8, g=8)
                for n in range(4):
                    t = s5_t(T_Y + n)
                    bank = filled(act, t, 3 * i)
                    for j in range(2):
                        ins = act.activation(yt[0:LCH, 2 * (2 * (n // 2) + j) + n % 2], bank[0:LCH, j * P:(j + 1) * P].rearrange("p (t h) -> p t h", t=8), ACT.Copy)
                    drained(ins, t)
            for n in range(2):
                emptied(act, s5_t(T_YB + n), 3 * 7)
            for k in range(KD):
                act.activation(hT[:, k, 0:NL], hT[:, k, 0:NL], ACT.Gelu_apprx_tanh).then_inc(S("gelu"), 1)
            for m in range(8):
                t = ticket0["glu"] + 2 * m + 1
                bank = filled(act, t)
                if m >= 4:
                    act.wait_ge(S("glu_gated"), m - 3)
                drained(act.activation(glu_sig[:, m % 4, :], bank[:, :], ACT.Sigmoid), t)
            norm_squares(act, "l1b", xT, TBL, hT, lambda k: act.wait_ge(S("glu_gated"), k + 1))
            norm_roots(act, "l1b", TBL)
            norm_shift(act, "l1b", TBL, hT, shift_of(1, 3))
            mlp_relu(act, 1, TBL)
            norm_squares(act, "mix", xT, TBL, hT, lambda k: tickets_emptied(act, "mlp1", k, 1, 56))
            norm_roots(act, "mix", TBL)
            for m in range(12):
                emptied(act, ticket0["qkv"] + m)
                act.activation(qkvT[:, m, :], qkvT[:, m, :], ACT.Silu).then_inc(S("qkv_silu"), 1)
            for name, o, func in (("zg", zT, ACT.Silu), ("gate", gateT, ACT.Gelu_apprx_tanh)):
                for m in range(4):
                    t = ticket0[name] + m
                    bank = filled(act, t)
                    drained(act.activation(o[:, m, :], bank[:, :], func), t)
            for m in range(8):
                act.wait_ge(S("qkv_silu"), m + 1)
                act.activation(qk_sq[:, m, :], qkvT[:, m, :], ACT.Square).then_inc(S("gq_sq"), 1)
            act.wait_ge(S("sp_abs"), 1)
            act.activation(lam[:, 2, :], lam[:, 1, :], ACT.Exp, scale=-1.0).then_inc(S("sp_act"), 1)
            act.activation(gt[:, G_E], gt[:, G_ABS], ACT.Exp, scale=-1.0).then_inc(S("sp_act"), 1)
            act.activation(gpar[:, 0, :], gpar[:, 0, :], ACT.Exp).then_inc(S("sp_act"), 1)
            act.wait_ge(S("sp_u"), 1)
            act.activation(lam[:, 4, :], lam[:, 3, :], ACT.Ln).then_inc(S("sp_act"), 1)
            act.activation(gt[:, G_LN], gt[:, G_U], ACT.Ln).then_inc(S("sp_act"), 1)
            act.activation(gt[:, G_BETA], gt[:, G_B], ACT.Sigmoid).then_inc(S("sp_act"), 1)
            act.wait_ge(S("g_ready"), 1)
            for m in range(4):
                if m >= 1:
                    act.wait_ge(S("lru_done"), m)
                tr, ti = ticket0["lru_r"] + m, ticket0["lru_i"] + m
                bank = filled(act, tr)
                drained(act.activation(lru_r, bank[:, :], ACT.Sigmoid, bias=col("lru_ba_2", m)), tr)
                bank = filled(act, ti)
                drained(act.activation(lru_i, bank[:, :], ACT.Sigmoid, bias=col("lru_bx_2", m)), ti)
                emptied(act, tr)
                act.activation(lru_a, lru_r, ACT.Exp, scale=lam[:, 7, m:m + 1]).then_inc(S("lru_exp"), 1)
                act.activation(lru_th, lru_r, ACT.Tanh, scale=lam[:, 7, m:m + 1]).then_inc(S("lru_exp"), 1)
                act.wait_ge(S("lru_gap"), m + 1)
                act.activation(lru_th, lru_th, ACT.Sqrt, scale=-1.0).then_inc(S("lru_root"), 1)
            for m in range(8):
                t = ticket0["gnorm"] + m
                bank = filled(act, t)
                drained(act.activation(qk_rt[m], bank[:, :], ACT.Sqrt, bias=eps_col), t)
            for t in range(NTL):
                tk = ticket0["ktok"] + t
                bank = filled(act, tk)
                drained(act.activation(k_tok[:, t], bank[:, :].rearrange("p (h d) -> p h d", h=4), ACT.Copy), tk)
            for pair in range(2):
                for tt in (2 * pair, 2 * pair + 1):
                    t0 = ticket0[f"gpre{tt}"]
                    bank = filled(act, t0)
                    act.activation(gs[:, tt, :], bank[:, 0:16], ACT.Copy)
                    drained(act.activation(gx[:, tt, :], bank[:, 0:16], ACT.Exp), t0)
                    bank = filled(act, t0 + 1)
                    act.wait_ge(S("g_diff"), tt + 1)
                    act.activation(g_dec[:, tt % 2], g_dec[:, tt % 2], ACT.Exp).then_inc(S("g_dexp"), 1)
                    drained(act.activation(g_bc, bank[:, :].rearrange("p (h c) -> p h c", h=4), ACT.Exp), t0 + 1)
                    bank = filled(act, t0 + 2)
                    drained(act.activation(g_kbT, bank[:, :].rearrange("p (h c) -> p h c", h=4), ACT.Copy), t0 + 2)
                for lv in range(6):
                    for x in range(2):
                        t = ticket0[f"inv{pair}_{lv}"] + x
                        bank = filled(act, t)
                        drained(act.activation(inv_y[:, x], bank[:, :].rearrange("p (h c) -> p h c", h=4), ACT.Copy), t)
                for tt in (2 * pair, 2 * pair + 1):
                    t0 = ticket0[f"uw{tt}"]
                    bank = filled(act, t0)
                    drained(act.activation(u_tok[:, tt], bank[:, :].rearrange("p (h d) -> p h d", h=4), ACT.Copy), t0)
                    bank = filled(act, t0 + 1)
                    drained(act.activation(wT[:, :, tt * P:(tt + 1) * P], bank[:, :].rearrange("p (h c) -> p h c", h=4), ACT.Copy), t0 + 1)
            for n in range(8):
                t = ticket0["gscan"] + 3 * n + 1
                bank = filled(act, t)
                drained(act.activation(mix2[:, 0:4, n * GCH:(n + 1) * GCH], bank[:, 0:4 * GCH].rearrange("p (h c) -> p h c", h=4), ACT.Copy), t)
            emptied(act, ticket0["gscan"] + 22)
            for m in range(4):
                act.activation(qkvT[:, m, :], mix2[:, m, :], ACT.Square).then_inc(S("o_sq"), 1)
            for m in range(4):
                t = ticket0["norm_o"] + m
                bank = filled(act, t)
                drained(act.activation(o_rt[:, m, :], bank[:, :], ACT.Sqrt, bias=eps_col, scale=1.0 / P), t)
            for n in range(4):
                t, g = n // 2, n % 2
                bank = filled(act, ticket0["mem_in"] + n)
                drained(act.activation(memT[:, 4 * g:4 * g + 4, t * P:(t + 1) * P], bank[:, :].rearrange("p (k n) -> p k n", k=4), ACT.Copy),
                        ticket0["mem_in"] + n)
            for n in range(4):
                emptied(act, ticket0["mem_in"] + n)
            norm_squares(act, "mem", memT, TBM, mem_h)
            norm_roots(act, "mem", TBM, rs=rstd_mem)
            for n in range(4):
                t = ticket0["xk"] + n
                bank = filled(act, t)
                drained(act.activation(xkT[:, 2 * n:2 * n + 2, :], bank[:, :].rearrange("p (m n) -> p m n", m=2), ACT.Copy), t)
            for n in range(4):
                t = ticket0["xv"] + n
                bank = filled(act, t)
                drained(act.activation(xv_tok[:, n % 2, (n // 2) * 512:(n // 2 + 1) * 512], bank[:, :], ACT.Copy), t)
            norm_squares(act, "xat", xT, TBL, hT, lambda k: emptied(act, ticket0["w_out2"] + k))
            norm_roots(act, "xat", TBL)
            for m in range(KD):
                t = ticket0["xq"] + m
                bank = filled(act, t)
                drained(act.activation(xqT[:, m, :], bank[:, :], ACT.Copy), t)
            for step, n in XAT_ORDER:
                t = ticket0[f"{step}{n}"]
                if step == "xscore":
                    act.wait_ge(S("xat_max"), n + 1)
                    bank = filled(act, t)
                    drained(act.activation(xprob[:, n % 2, :], bank[:, 0:MEM], ACT.Exp, bias=stat[:, n % 2, 3:4], scale=xat_scale,
                                           accum_out=stat[:, n % 2, 4:5]), t)
                else:
                    bank = filled(act, t)
                    o = xprobT[:, n % 2] if step == "xturn" else xoT[:, 2 * (n // 4):2 * (n // 4) + 2, n % 4 * P:(n % 4 + 1) * P]
                    drained(act.activation(o, bank[:, 0:2 * P].rearrange("p (t n) -> p t n", t=2), ACT.Copy), t)
            for n in range(4):
                t = ticket0["subk"] + n
                bank = filled(act, t)
                drained(act.activation(subT[:, 4 * n:4 * n + 4, :], bank[:, :].rearrange("p (v n) -> p v n", v=4), ACT.Copy), t)
            norm_squares(act, "ffn", xT, TBL, hT, lambda k: emptied(act, ticket0["wo"] + k))
            norm_roots(act, "ffn", TBL)
            for j in range(4):
                for v in range(4):
                    t = ticket0[f"pq{j}"] + v
                    bank = filled(act, t)
                    drained(act.activation(pqT[:, j % 2, v, :], bank[:, :], ACT.Copy), t)
                for t in range(NTL):
                    u = NTL * j + t
                    if u >= 2:
                        act.wait_ge(S("psc_used"), u - 1)
                    bank = filled(act, ticket0[f"psc{j}"] + t)
                    drained(act.activation(psc[:, u % 2], bank[:, :].rearrange("p (v n) -> p v n", v=4), ACT.Copy), ticket0[f"psc{j}"] + t)
            for n in range(8):
                tk = ticket0["htok"] + n
                bank = filled(act, tk)
                drained(act.activation(h_tok[:, n // 2, n % 2 * 512:(n % 2 + 1) * 512], bank[:, :], ACT.Copy), tk)
            act.wait_ge(S("best_ready"), 1)
            act.activation(gate, best.rearrange("p t h k -> p t (h k)"), ACT.Exp).then_inc(S("gate_exp"), 1)
            for T_ in range(NTL):
                with act.Fori(0, EGROUPS) as i:
                    act.wait_ge(S("u_used"), i * ERING + T_ * EXPERTS + 2 * ERING)
                    act.activation(gelus, dots, ACT.Gelu_apprx_tanh).then_inc(S("gelus_ready"), 1)
                    act.wait_ge(S("acts_ready"), i + EGROUPS * T_ + 1)
                    for s in range(ERING):
                        act.wait_ge(S("v_used"), i * ERING + T_ * EXPERTS + s + 1)
                        act.activation(diag[:, s, :], ident[:, :], ACT.Copy, scale=acts[:, s:s + 1]).then_inc(S("diag_ready"), 1)
                if T_ >= 1:
                    act.wait_ge(S("out_ready"), T_)
                for g in range(2):
                    last = act.activation(sq_junk[:, 512 * g:512 * g + 512], filled(act, ticket0["ffn"] + 2 * T_ + g)[:, :], ACT.Square, accum_out=fin[:, g:g + 1])
                last.then_inc(S("fin_sq"), 1)
                act.wait_ge(S("fin_sum"), T_ + 1)
                act.activation(fin[:, 3:4], fin[:, 2:3], ACT.Sqrt, bias=eps_col, scale=1.0 / D).then_inc(S("fin_root"), 1)

        @block_.vector
        def _(dve):
            dve_step(dve, dve.memset(eps_col, EPS))
            for n in range(0, 12, 2):
                t, g = n // 2, n % 2
                bank = filled(dve, ticket0["x_in"] + n)
                drained(dve.tensor_copy(xT[:, 4 * g:4 * g + 4, t * P:(t + 1) * P],
                                        bank[:, :].rearrange("p (k n) -> p k n", k=4)), ticket0["x_in"] + n)
            for i, (_, _, n) in enumerate(vec_rows):
                t = ticket0["vecs"] + i
                bank = filled(dve, t)
                drained(dve.tensor_copy(vec_cols[i][:, :], bank[:, 0:n]), t)
                emptied(dve, t)

            for l in range(2):
                with dve.Fori(0, 3) as i:
                    for n in range(8):
                        t = ticket0[f"ada{l}"] + n
                        bank = filled(dve, t, i)
                        ci, r = col_of["ada_b"]
                        bias = vec_cols[ci][:, bass.ds(i * 16 + (r + 48 * l + 2 * n), 2)]
                        drained(dve.tensor_tensor(modT[l][:, bass.ds(i * 16 + 2 * n, 2), :],
                                                  bank[:, 0:4].rearrange("p (m s) -> p m s", s=2), bcast(bias, 2), ALU.add), t)
                for n in range(16, 24):
                    emptied(dve, ticket0[f"ada{l}"] + n)
                for gain, norm, at_ in ((gain1[l], "norm1_g", 1), (gain2[l], "norm2_g", 4)):
                    dve_step(dve, dve.tensor_scalar(gain[:, :, :], modT[l][:, at_ * KD:(at_ + 1) * KD, :], 1.0, None, ALU.add))
                    dve_step(dve, dve.tensor_tensor(gain[:, :, :], gain[:, :, :], bcast(col(norm, KD * l, KD), 2), ALU.mult))

            norm_scale(dve, "l0a", xT, TBS, hT, lambda k, s: gain1[0][:, k, s:s + 1])

            norm_scale(dve, "cq", cqT, TBS, cqT, lambda k, s: col("mla_q_norm_g", k), kd=2)
            norm_scale(dve, "ckv", ckvT.unsqueeze(1), TBS, ckvT.unsqueeze(1), lambda k, s: col("mla_kv_norm_g"), kd=1,
                       rs=rstd_qk[:, 0, :])
            for t in range(0, 6, 2):
                bank = filled(dve, ticket0["v_tok"] + t)
                drained(dve.tensor_copy(v_tok[:, t, :], bank[:, :]), ticket0["v_tok"] + t)
            dve.wait_ge(S("mla_tables"), 16 * MLA_LOADS)
            for step, n in mla_order():
                t0 = ticket0[f"{step}{n}"]
                if step == "norm":
                    for j, x in enumerate((qh, kh)):
                        for b in range(2):
                            emptied(dve, t0 + 2 * j + b)
                        dve_step(dve, dve.reciprocal(rstd_qk[0:QK, j, :], rstd_qk[0:QK, j, :]))
                        for lo, hi in TBS:
                            dve.scalar_tensor_tensor(x[0:QK, n % 2, lo:hi], x[0:QK, n % 2, lo:hi], small[0:QK, 2 + j:3 + j],
                                                     rstd_qk[0:QK, j, lo:hi], ALU.mult, ALU.mult).then_inc(S("qk_normed"), 1)
                        dve.wait_ge(S("qk_normed"), 4 * n + 2 * j + 2)
                elif step == "rot":
                    r = slice(NOPE, QK)
                    for j, x in enumerate((qh, kh)):
                        bank = filled(dve, t0 + j)
                        ins = dve.tensor_tensor(rope_tmp[r], bank[r, :], sin_mla[r], ALU.mult)
                        drained(ins, t0 + j)
                        emptied(dve, t0 + j)
                        dve_step(dve, dve.tensor_tensor(x[r, n % 2, 0:NL], x[r, n % 2, 0:NL], cos_mla[r], ALU.mult))
                        dve.tensor_tensor(x[r, n % 2, 0:NL], x[r, n % 2, 0:NL], rope_tmp[r], ALU.add).then_inc(S("qk_ready"), 1)
                        dve.wait_ge(S("qk_ready"), 2 * n + j + 1)
                elif step == "scores":
                    st = stat[:, n % 2, :]
                    two = n % 6 < 4
                    for b in range(2 if two else 1):
                        bank = filled(dve, t0 + b)
                        w = NL if two and b == 0 else NC
                        dve_step(dve, dve.reduce_max(st[:, b:b + 1], bank[:, 0:w], AX_X))
                    if two:
                        dve_step(dve, dve.tensor_tensor(st[:, 0:1], st[:, 0:1], st[:, 1:2], ALU.max))
                    dve.tensor_scalar(st[:, 3:4], st[:, 0:1], -att_scale, None, ALU.mult).then_inc(S("score_max"), 1)
                    for b in range(2 if two else 1):
                        emptied(dve, t0 + b)
                    if two:
                        dve_step(dve, dve.tensor_tensor(st[:, 4:5], st[:, 4:5], st[:, 5:6], ALU.add))
                    dve_step(dve, dve.reciprocal(st[:, 6:7], st[:, 4:5]))
                    keys = slice(0, NT) if two else KEYS[1]
                    dve.tensor_scalar(prob[:, n % 2, keys], prob[:, n % 2, keys], st[:, 6:7], None, ALU.mult)\
                       .then_inc(S("prob_ready"), 1)
                elif step == "turn" and n % 6 < 4:
                    bank = filled(dve, t0)
                    drained(dve.tensor_copy(probT[:, n % 2, 0:4, :], bank[:, :].rearrange("p (t n) -> p t n", t=4)), t0)
                elif step == "out":
                    h, rows = n // 6, HEADROWS[n // 6]
                    bank = filled(dve, t0)
                    drained(dve.tensor_copy(mixT[rows, h // 2, (n % 6) * P:(n % 6 + 1) * P], bank[rows, 0:P]), t0)

            for t in range(6):
                bank = filled(dve, ticket0["z_rv"] + t)
                drained(dve.tensor_copy(rv[:, t, :], bank[:, :]), ticket0["z_rv"] + t)
            dve.wait_ge(S("ret_tables"), 48)
            for j, x in enumerate((rqT, rkT)):
                for m in range(4):
                    t = ticket0["rrot"] + 4 * j + m
                    bank = filled(dve, t)
                    drained(dve.tensor_tensor(decayed[:, m, :], bank[:, :], sin_ret, ALU.mult), t)
                    emptied(dve, t)
                    dve_step(dve, dve.tensor_tensor(x[:, m, 0:NL], x[:, m, 0:NL], cos_ret, ALU.mult))
                    dve.tensor_tensor(x[:, m, 0:NL], x[:, m, 0:NL], decayed[:, m, :], ALU.add).then_inc(S("rot_done"), 1)
            dve.wait_ge(S("rot_done"), 8)
            dve.wait_ge(S("lg_exp"), 1)
            dve.tensor_scalar(lg[:, LG_U, :], lg[:, LG_E, :], -1.0, 1.0, ALU.mult, ALU.add).then_inc(S("lg_u"), 1)
            dve.wait_ge(S("lg_u"), 1)
            dve_step(dve, dve.tensor_scalar(lg[:, LG_D, :], lg[:, LG_U, :], -1.0, -1e-30, ALU.add, ALU.add))
            dve_step(dve, dve.reciprocal(lg[:, LG_D, :], lg[:, LG_D, :]))
            dve_step(dve, dve.tensor_tensor(lg[:, LG_D, :], lg[:, LG_D, :], lg[:, LG_E, :], ALU.mult))
            dve.wait_ge(S("lg_ln"), 1)
            dve_step(dve, dve.tensor_scalar(lg[:, LG, :], lg[:, LG, :], -1e-30, -1.0, ALU.add, ALU.mult))
            dve_step(dve, dve.tensor_tensor(lg[:, LG, :], lg[:, LG, :], lg[:, LG_D, :], ALU.mult))
            dve_step(dve, dve.tensor_scalar(lg[:, LG_512, :], lg[:, LG, :], 512.0, None, ALU.mult))
            dve_step(dve, dve.tensor_scalar(lg[:, LG_256, :], lg[:, LG, :], 256.0, None, ALU.mult))
            dve.tensor_scalar(lg[:, LG_NEG, :], lg[:, LG, :], -1.0, None, ALU.mult).then_inc(S("lg_ready"), 1)
            dve.wait_ge(S("lg_ready"), 1)
            dve.wait_ge(S("dist_landed"), 16)
            for step, m in ret_order():
                h, j = m // 8, m % 8
                if step == "rscore":
                    if j == 0:
                        if h >= 1:
                            dve.wait_ge(S("decay_exp"), 3 * h)
                        dve_step(dve, dve.tensor_scalar(decay_tmp, ret_dist, lg[:, LG, h:h + 1], None, ALU.mult))
                        dve.scalar_tensor_tensor(decay_tmp, ret_dist, lg[:, LG_NEG, H_R + h:H_R + h + 1], decay_tmp,
                                                 ALU.mult, ALU.min).then_inc(S("decay_arg"), 1)
                        dve.wait_ge(S("decay_exp"), 3 * h + 2)
                        dve.tensor_tensor(decay_ctx[h % 2], decay_ctx[h % 2], decay_ctx2, ALU.add).then_inc(S("decay_ready"), 1)
                        dve.wait_ge(S("decay_ready"), h + 1)
                        dve.wait_ge(S("decay_exp"), 3 * h + 3)
                    t = ticket0[f"rscore{m}"]
                    bank = filled(dve, t)
                    w = NL if j < 6 else NC
                    drained(dve.tensor_tensor(decayed[:, m % 4, 0:w], bank[:, 0:w], ret_decay_slice(m), ALU.mult), t)
            for c in range(4):
                for b, (lo, hi) in enumerate(TBS):
                    t = ticket0["rmean"] + 2 * c + b
                    bank = filled(dve, t)
                    drained(dve.tensor_tensor(mixT[:, 4 + c, lo:hi], mixT[:, 4 + c, lo:hi], bank[:, 0:hi - lo], ALU.subtract), t)
            for c in range(4):
                for b, (lo, hi) in enumerate(TBS):
                    emptied(dve, ticket0["rvar"] + 2 * c + b)
                    dve_step(dve, dve.reciprocal(rkT[:, c, lo:hi], rkT[:, c, lo:hi]))
                    dve_step(dve, dve.tensor_tensor(rkT[:, c, lo:hi], rkT[:, c, lo:hi], rgT[:, c, lo:hi], ALU.mult))
                    dve.tensor_tensor(mixT[:, 4 + c, lo:hi], mixT[:, 4 + c, lo:hi], rkT[:, c, lo:hi], ALU.mult)\
                       .then_inc(S("ret_gated"), 1)
            for m in range(8):
                for b, (lo, hi) in enumerate(TBS):
                    t = ticket0["w_out"] + 2 * m + b
                    bank = filled(dve, t)
                    drained(dve.scalar_tensor_tensor(xT[:, m, lo:hi], bank[:, 0:hi - lo], modT[0][:, 2 * KD + m, b:b + 1],
                                                     xT[:, m, lo:hi], ALU.mult, ALU.add), t)

            norm_scale(dve, "l0b", xT, TBS, hT, lambda k, s: gain2[0][:, k, s:s + 1])
            mlp_square_and_add(dve, 0, TBS)

            norm_scale(dve, "l1a", xT, TBS, hT, lambda k, s: gain1[1][:, k, s:s + 1])
            for d in range(2):
                t = ticket0["s5_prm"] + d
                bank = filled(dve, t)
                drained(dve.tensor_copy(s5_prm[:, d], bank[:, 0:96].rearrange("p (j r) -> p j r", j=3)), t)
            for d in range(2):
                emptied(dve, ticket0["s5_prm"] + d)
            dve_step(dve, dve.memset(prep[:, 23], 0.0))
            dve.memset(small[:, 14:15], 0.0).then_inc(S("s5_prm_ready"), 1)
            are, aim = s5_prm[:, :, 0, :], s5_prm[:, :, 1, :]
            DT, LR, SIN_IN, COS_IN, RAD, RADI, SIN, COS = (prep[:, j] for j in range(8))
            T = [prep[:, j] for j in range(8, 23)]

            def mul(o, a, b):
                dve_step(dve, dve.tensor_tensor(o, a, b, ALU.mult))

            def add(o, a, b):
                dve_step(dve, dve.tensor_tensor(o, a, b, ALU.add))

            def sub(o, a, b):
                dve_step(dve, dve.tensor_tensor(o, a, b, ALU.subtract))

            def cmul(o_re, o_im, a, b, t1, t2):
                mul(t1, a[0], b[0])
                mul(t2, a[1], b[1])
                sub(o_re, t1, t2)
                mul(t1, a[0], b[1])
                mul(t2, a[1], b[0])
                add(o_im, t1, t2)

            def wrap(o, x):
                magic, two_pi = 12582912.0, 2.0 * np.pi
                dve_step(dve, dve.tensor_scalar(T[0], x, 1.0 / two_pi, None, ALU.mult))
                dve_step(dve, dve.tensor_scalar(T[0], T[0], magic, None, ALU.add))
                dve_step(dve, dve.tensor_scalar(T[0], T[0], -magic, None, ALU.add))
                dve_step(dve, dve.scalar_tensor_tensor(T[1], T[0], -6.28125, x, ALU.mult, ALU.add))
                dve_step(dve, dve.scalar_tensor_tensor(o, T[0], -(two_pi - 6.28125), T[1], ALU.mult, ALU.add))
                dve_step(dve, dve.tensor_scalar(o, o, 3.1415925, -3.1415925, ALU.min, ALU.max))

            dve.wait_ge(S("s5_act"), 1)
            mul(T[2], are, DT)
            dve_step(dve, dve.tensor_scalar(LR, T[2], -21.0, None, ALU.max))
            mul(T[2], aim, DT)
            wrap(SIN_IN, T[2])
            dve_step(dve, dve.tensor_scalar(T[3], SIN_IN, float(np.pi / 2), None, ALU.add))
            wrap(COS_IN, T[3])
            dve.memset(small[:, 14:15], 0.0).then_inc(S("s5_args"), 1)
            dve.wait_ge(S("s5_act"), 6)
            A1, AI = (T[2], T[3]), (T[4], T[5])
            mul(A1[0], RAD, COS)
            mul(A1[1], RAD, SIN)
            mul(AI[0], RADI, COS)
            mul(AI[1], RADI, SIN)
            dve_step(dve, dve.tensor_scalar(AI[1], AI[1], -1.0, None, ALU.mult))
            mul(T[0], are, are)
            mul(T[1], aim, aim)
            add(T[0], T[0], T[1])
            dve_step(dve, dve.reciprocal(T[0], T[0]))
            dve_step(dve, dve.tensor_scalar(T[6], A1[0], -1.0, None, ALU.add))
            mul(T[1], T[6], are)
            mul(T[7], A1[1], aim)
            add(T[1], T[1], T[7])
            mul(T[8], T[1], T[0])
            mul(T[1], A1[1], are)
            mul(T[7], T[6], aim)
            sub(T[1], T[1], T[7])
            mul(T[9], T[1], T[0])
            for d in range(2):
                q = [bcast(T[8 + c][:, d, :], 16) for c in range(2)]
                cmul(prep_big[:, 2], prep_big[:, 3], q, (s5_b[:, d, 0], s5_b[:, d, 1]), prep_big[:, 0], prep_big[:, 1])
                for c in range(2):
                    dve_step(dve, dve.tensor_copy(s5_b[:, d, c], prep_big[:, 2 + c]))
            pw = [[s5_pw[:, c, :, :, k] for c in range(2)] for k in range(9)]
            dve_step(dve, dve.memset(s5_pw[:, 0, :, :, 4], 1.0))
            dve_step(dve, dve.memset(s5_pw[:, 1, :, :, 4], 0.0))
            for base, sgn in ((A1, 1), (AI, -1)):
                for c in range(2):
                    dve_step(dve, dve.tensor_copy(pw[4 + sgn][c], base[c]))
                cmul(*pw[4 + 2 * sgn], base, base, T[0], T[1])
                cmul(*pw[4 + 3 * sgn], pw[4 + 2 * sgn], base, T[0], T[1])
                cmul(*pw[4 + 4 * sgn], pw[4 + 2 * sgn], pw[4 + 2 * sgn], T[0], T[1])
            u = (COS, SIN)
            for n in range(9):
                o = (s5_qp[:, n - 2, 0], s5_qp[:, n - 2, 1]) if n >= 2 else (T[6 + 2 * n], T[7 + 2 * n])
                cmul(*o, u, u, T[0], T[1])
                u = o
            dve.memset(small[:, 14:15], 0.0).then_inc(S("s5_prep"), 1)
            dve.wait_ge(S("s5_prep"), 1)
            dve.memset(small[:, 14:15], 0.0).then_inc(S("s5_turned"), 1)
            for n in range(8):
                emptied(dve, ticket0["s5_c"] + n)
            rev = lambda ap, lo, hi: ap[:, :, hi - 1:(lo - 1 if lo else None):-1]
            with dve.Fori(0, 8) as i:
                dve_step.loop(i, S5_DVE_STEPS)
                ta, tb = s5_tmp[:, 0:512], s5_tmp[:, 512:1024]
                for d in range(2):
                    ks = slice(1, 9) if d == 0 else slice(0, 8)
                    p = [bcast(s5_pw[:, c, d, bass.ds(i * 4, 4), ks], 16) for c in range(2)]
                    b = [lead(s5_b[:, d, c, bass.ds(i * 4, 4), :], 8) for c in range(2)]
                    t1, t2, fr, fi = (x.rearrange("p (r k h) -> p r k h", r=4, k=8) for x in (
                        ta, tb, s5_F[:, d, 0].rearrange("p r x -> p (r x)"), s5_F[:, d, 1].rearrange("p r x -> p (r x)")))
                    if d == 0:
                        fr, fi = fr[:, :, ::-1, :], fi[:, :, ::-1, :]
                    mul(t1, p[0], b[0])
                    mul(t2, p[1], b[1])
                    sub(fr, t1, t2)
                    mul(t1, p[0], b[1])
                    mul(t2, p[1], b[0])
                    dve.tensor_tensor(fi, t1, t2, ALU.add).then_inc(S("s5_F"), 1)
                    dve.wait_ge(S("s5_F"), 2 * i + d + 1)
                for d in range(2):
                    if d == 0:
                        pool_done = i * (1 + 7 * 6 + 2 * 6) + 4 + 7 * 6
                        dve.wait_ge(S("pool_done"), pool_done)
                        dve.wait_ge(S("s5_decays"), 2 * i + 2)
                    banks = [filled(dve, s5_t(T_FI[d] + c), 3 * i)[:, 0:4 * NCH].rearrange("p (r n) -> p r n", r=4) for c in range(2)]
                    tab = [s5_tab[:, c, d] for c in range(2)]
                    parts = ((0, NCH),) if d == 0 else ((0, CCH), (CCH, NCH))
                    t1, t2 = (x[:, 0:4 * NCH].rearrange("p (r n) -> p r n", r=4) for x in (ta, tb))
                    order = (lambda ap, lo, hi: ap[:, :, lo:hi]) if d == 0 else rev
                    for lo, hi in parts:
                        x = [b_[:, :, lo:hi] for b_ in banks]
                        c_, s_ = (order(t_, lo, hi) for t_ in tab)
                        o1, o2 = t1[:, :, lo:hi], t2[:, :, lo:hi]
                        mul(o1, x[0], c_)
                        mul(o2, x[1], s_)
                        add(order(s5_g[:, 0], lo, hi), o1, o2)
                        if hi < NCH:
                            mul(o1, x[1], c_)
                            mul(o2, x[0], s_)
                        else:
                            drained(dve.tensor_tensor(o1, x[1], c_, ALU.mult), s5_t(T_FI[d] + 1))
                            drained(dve.tensor_tensor(o2, x[0], s_, ALU.mult), s5_t(T_FI[d]))
                            for c in range(2):
                                emptied(dve, s5_t(T_FI[d] + c), 3 * i)
                        sub(order(s5_g[:, 1], lo, hi), o1, o2)
                    for c in range(2):
                        dve_step(dve, dve.tensor_tensor_scan(s5_w[:, c].rearrange("p r n -> p (r n)"), s5_g[:, c].rearrange("p r n -> p (r n)"),
                                                             s5_decay[:, d].rearrange("p r n -> p (r n)"), 0.0, ALU.add, ALU.mult))
                    w = [s5_w[:, c, :, CCH - 1:NCH - 1] if d == 0 else s5_w[:, c, :, NCH - 2:CCH - 2:-1] for c in range(2)]
                    t_ = [x[:, :, CCH:NCH] if d == 0 else x[:, :, NCH - 1:CCH - 1:-1] for x in tab]
                    o1, o2 = t1[:, :, 0:LCH], t2[:, :, 0:LCH]
                    mul(o1, w[0], t_[0])
                    mul(o2, w[1], t_[1])
                    sub(s5_s[:, d, 0], o1, o2)
                    mul(o1, w[0], t_[1])
                    mul(o2, w[1], t_[0])
                    dve.tensor_tensor(s5_s[:, d, 1], o1, o2, ALU.add).then_inc(S("s5_turned"), 1)
                    dve.wait_ge(S("s5_turned"), 2 * i + d + 2)
                for d in range(2):
                    for n in range(2):
                        t = s5_t(T_MM[d] + n)
                        bank = filled(dve, t, 3 * i)[:, :].rearrange("p (g x) -> p g x", g=4)
                        mask = s5_mask[:, d, :].unsqueeze(1).to_broadcast([P, 4, P])
                        o = s5_M.rearrange("p (r two) x -> p two r x", two=2)[:, n]
                        o_ = o if d == 0 else s5_tmp[:, 512 * n:512 * n + 512].rearrange("p (g x) -> p g x", g=4)
                        drained(dve.tensor_tensor(o_, bank, mask, ALU.mult), t)
                        emptied(dve, t, 3 * i)
                        if d == 1:
                            dve.tensor_tensor(o, o, o_, ALU.add).then_inc(S("s5_M"), 1)
                ci, r = col_of["s5_d"]
                for n in range(2):
                    t = s5_t(T_YB + n)
                    bank = filled(dve, t, 3 * i)[:, 0:4 * LCH].rearrange("p (t c) -> p t c", t=4)
                    hv = hT[:, bass.ds(i, 1), 0:NL].squeeze(1).rearrange("p (c t) -> p t c", t=8)[:, 4 * n:4 * n + 4, :]
                    drained(dve.scalar_tensor_tensor(hv, hv, vec_cols[ci][:, bass.ds(i + r, 1)], bank, ALU.mult, ALU.add), t)
                dve_step.end_loop(8)
            for m in range(8):
                t = ticket0["glu"] + 2 * m
                bank = filled(dve, t)
                emptied(dve, t + 1)
                drained(dve.tensor_tensor(glu_sig[:, m % 4, :], bank[:, :], glu_sig[:, m % 4, :], ALU.mult), t)
                emptied(dve, t)
                dve.scalar_tensor_tensor(xT[:, m, 0:NL], glu_sig[:, m % 4, :], modT[1][:, 2 * KD + m, 0:1], xT[:, m, 0:NL],
                                         ALU.mult, ALU.add).then_inc(S("glu_gated"), 1)
            norm_scale(dve, "l1b", xT, TBL, hT, lambda k, s: gain2[1][:, k, 0:1])
            mlp_square_and_add(dve, 1, TBL)

            norm_scale(dve, "mix", xT, TBL, hT, lambda k, s: col("norm_mix_w_2", k))

            def conv(bank, t, o, w, bias=None):
                if bias is None:
                    dve_step(dve, dve.tensor_scalar(o, bank[:, :], w(3), None, ALU.mult))
                else:
                    dve_step(dve, dve.tensor_scalar(o, bank[:, :], w(3), bias, ALU.mult, ALU.add))
                for j in (2, 1):
                    s = 3 - j
                    dve_step(dve, dve.scalar_tensor_tensor(o[:, s:NL], bank[:, 0:NL - s], w(j), o[:, s:NL], ALU.mult, ALU.add))
                drained(dve.scalar_tensor_tensor(o[:, 3:NL], bank[:, 0:NL - 3], w(0), o[:, 3:NL], ALU.mult, ALU.add), t)

            for m in range(12):
                t = ticket0["qkv"] + m
                conv(filled(dve, t), t, qkvT[:, m, :], lambda j: col("conv_qkv_w_2", 12 * j + m))
            dve.wait_ge(S("mix2_landed"), 16 * MIX2_LOADS)
            t = ticket0["ab"]
            ab = filled(dve, t)[:, 0:8 * NTL].rearrange("p (t c) -> p t c", t=NTL)
            dve_step(dve, dve.tensor_tensor(gt[:, G_A], ab[:, :, 0:4], gpar[:, 1, :].unsqueeze(1).to_broadcast([P, NTL, 4]), ALU.add))
            drained(dve.tensor_copy(gt[:, G_B], ab[:, :, 4:8]), t)
            dve_step(dve, dve.tensor_scalar(lam[:, 0, :], col("lru_lambda_2", 0, 4), -1.0, None, ALU.mult))
            SOFTPLUS = ((lam[:, 0, :], lam[:, 1, :], lam[:, 2, :], lam[:, 3, :], lam[:, 4, :], lam[:, 5, :]),
                        (gt[:, G_A], gt[:, G_ABS], gt[:, G_E], gt[:, G_U], gt[:, G_LN], gt[:, G_T]))
            for x, mag, *_ in SOFTPLUS:
                dve_step(dve, dve.scalar_tensor_tensor(mag, x, -1.0, x, ALU.mult, ALU.max))
            dve.memset(small[:, 14:15], 0.0).then_inc(S("sp_abs"), 1)
            dve.wait_ge(S("sp_act"), 3)
            for _, _, e, u, *_ in SOFTPLUS:
                dve_step(dve, dve.tensor_scalar(u, e, 1.0, None, ALU.add))
            dve.memset(small[:, 14:15], 0.0).then_inc(S("sp_u"), 1)
            for m in range(4):
                t = ticket0["xr"] + m
                conv(filled(dve, t), t, xrT[:, m, :], lambda j: col("lru_conv_w_2", 4 * j + m), col("lru_conv_b_2", m))
            dve.wait_ge(S("sp_act"), 6)
            for x, _, e, u, ln, tmp in SOFTPLUS:
                dve_step(dve, dve.tensor_scalar(tmp, u, -1.0, 1e-30, ALU.add, ALU.add))
                dve_step(dve, dve.reciprocal(tmp, tmp))
                mul(tmp, tmp, e)
                dve_step(dve, dve.scalar_tensor_tensor(tmp, ln, 1e-30, tmp, ALU.add, ALU.mult))
                dve_step(dve, dve.scalar_tensor_tensor(tmp, x, 0.0, tmp, ALU.max, ALU.add))
            dve_step(dve, dve.tensor_scalar(lam[:, 7, :], lam[:, 5, :], -8.0, None, ALU.mult))
            dve_step(dve, dve.tensor_tensor(gt[:, G_T], gt[:, G_T], gpar[:, 0, :].unsqueeze(1).to_broadcast([P, NTL, 4]), ALU.mult))
            dve.tensor_scalar(gt[:, G_G], gt[:, G_T], -1.0, None, ALU.mult).then_inc(S("g_ready"), 1)
            dve.wait_ge(S("g_ready"), 1)
            for m in range(4):
                dve.wait_ge(S("lru_exp"), 2 * m + 2)
                mul(lru_h, lru_a, lru_a)
                dve.scalar_tensor_tensor(lru_th, lru_h, 1.0, lru_th, ALU.add, ALU.mult).then_inc(S("lru_gap"), 1)
                emptied(dve, ticket0["lru_i"] + m)
                emptied(dve, ticket0["xr"] + m)
                mul(lru_i, lru_i, xrT[:, m, :])
                dve.wait_ge(S("lru_root"), m + 1)
                mul(lru_i, lru_i, lru_th)
                dve_step(dve, dve.tensor_tensor_scan(lru_h, lru_a, lru_i, 0.0, ALU.mult, ALU.add))
                emptied(dve, ticket0["gate"] + m)
                dve.tensor_tensor(mix2[:, 4 + m, :], lru_h, gateT[:, m, :], ALU.mult).then_inc(S("lru_done"), 1)
            for m in range(8):
                emptied(dve, ticket0["gnorm"] + m)
                dve_step(dve, dve.reciprocal(qk_rt[m], qk_rt[m]))
                dve.scalar_tensor_tensor(qkvT[:, m, :], qkvT[:, m, :], float(P ** -0.5) if m < 4 else 1.0, qk_rt[m],
                                         ALU.mult, ALU.mult).then_inc(S("g_normed"), 1)
            for t in range(NTL):
                tk = ticket0["vtok"] + t
                bank = filled(dve, tk)
                drained(dve.tensor_tensor(u_tok[:, t], bank[:, :].rearrange("p (h d) -> p h d", h=4), bcast(gt[:, G_BETA, t, :], P), ALU.mult), tk)
            dve.memset(g_state, 0.0).then_inc(S("g_state"), 1)
            dve.wait_ge(S("lru_done"), 4)
            dve.wait_ge(S("g_masks"), 16 * 9)
            for pair in range(2):
                for tt in (2 * pair, 2 * pair + 1):
                    t0, x = ticket0[f"gpre{tt}"], tt % 2
                    tok = slice(tt * P, (tt + 1) * P)
                    if tt > 0:
                        dve.wait_ge(S("g_qdec"), tt)
                        filled(dve, ticket0[f"gpre{tt - 1}"] + 2)
                    if tt == 2:
                        filled(dve, ticket0["uw1"] + 1)
                    dve.tensor_copy(g_bc, bcast(gt[:, G_G, tt, :], P)).then_inc(S("g_bcast"), 1)
                    emptied(dve, ticket0["ktok"] + tt)
                    dve.tensor_tensor(g_kw, k_tok[:, tt], bcast(gt[:, G_BETA, tt, :], P), ALU.mult).then_inc(S("g_kb"), 1)
                    emptied(dve, t0)
                    bank = filled(dve, t0 + 1)
                    for h in range(4):
                        last = dve.tensor_scalar(g_dec[:, x, h, :], bank[:, h * P:(h + 1) * P], gs[:, tt, h:h + 1], 0.0, ALU.subtract, ALU.min)
                    last.then_inc(S("g_diff"), 1)
                    dve.wait_ge(S("g_dexp"), tt + 1)
                    dve_step(dve, dve.tensor_tensor(g_dec[:, x], g_dec[:, x], bc4(tri_incl), ALU.mult))
                    for o, t in ((g_at[:, x], t0 + 3), (attnT[:, tt], t0 + 4)):
                        bank = filled(dve, t)
                        drained(dve.tensor_tensor(o, bank[:, :].rearrange("p (h c) -> p h c", h=4), g_dec[:, x], ALU.mult), t)
                    emptied(dve, t0 + 1)
                    dve.tensor_tensor(qkvT[:, 0:4, tok], qkvT[:, 0:4, tok], g_bc, ALU.mult).then_inc(S("g_qdec"), 1)
                if pair:
                    filled(dve, ticket0["uw1"] + 1)
                for x in range(2):
                    dve.tensor_copy(inv_x[:, x], bc4(ident[:, :]))
                    last = dve.tensor_copy(inv_xt[:, x], bc4(ident[:, :]))
                last.then_inc(S("g_eye"), 1)
                dve.wait_ge(S("g_eye"), pair + 1)
                for x in range(2):
                    emptied(dve, ticket0[f"gpre{2 * pair + x}"] + 3)
                for lv in range(6):
                    for x in range(2):
                        if lv > 0:
                            filled(dve, ticket0[f"inv{pair}_{lv - 1}"] + x)
                        dve.tensor_tensor(g_lvl[:, x], g_at[:, x], bc4(merge[lv]), ALU.mult).then_inc(S("g_level"), 1)
                    for x in range(2):
                        for o, t in ((inv_x[:, x], ticket0[f"inv{pair}_{lv}"] + 2 + 2 * x), (inv_xt[:, x], ticket0[f"inv{pair}_{lv}"] + 3 + 2 * x)):
                            if lv > 0:
                                emptied(dve, t - 6)
                            bank = filled(dve, t)
                            if o is inv_x[:, x]:
                                filled(dve, t + 1)
                            drained(dve.tensor_tensor(o, o, bank[:, :].rearrange("p (h c) -> p h c", h=4), ALU.subtract), t)
                for tt in (2 * pair, 2 * pair + 1):
                    mul(gt[:, G_BE, tt, :], gt[:, G_BETA, tt, :], gx[:, tt, 0:4])
                    if tt % 2:
                        filled(dve, ticket0[f"uw{tt - 1}"] + 1)
                    dve.tensor_tensor(g_kw, k_tok[:, tt], bcast(gt[:, G_BE, tt, :], P), ALU.mult).then_inc(S("g_kw"), 1)
                    dve.wait_ge(S("g_kw"), tt + 1)
                    dve.tensor_tensor(k_tok[:, tt], k_tok[:, tt], bcast(gx[:, tt, 4:8], P), ALU.mult).then_inc(S("g_kdec"), 1)
            for n in range(8):
                tt, r = n // 2, GHALF[n % 2]
                t0 = ticket0["gscan"] + 3 * n
                if n % 2 == 0:
                    emptied(dve, ticket0[f"uw{tt}"])
                bank = filled(dve, t0)
                drained(dve.tensor_tensor(v_new[r, :], u_tok[r, tt].rearrange("p h d -> p (h d)"), bank[r, :], ALU.subtract), t0)
                bank = filled(dve, t0 + 2)
                for h in range(4):
                    if h == 0:
                        dve.wait_ge(S("g_state"), 4 * n + 1)
                    ins = dve.scalar_tensor_tensor(g_state[:, h, :], g_state[:, h, :], gx[:, tt, 8 + 2 * h + n % 2:9 + 2 * h + n % 2],
                                                   bank[:, h * P:(h + 1) * P], ALU.mult, ALU.add)
                    ins.then_inc(S("g_state"), 1)
                dve.wait_ge(S("g_state"), 4 * n + 5)
                drained(dve.memset(small[:, 14:15], 0.0), t0 + 2)
            for m in range(4):
                emptied(dve, ticket0["norm_o"] + m)
                emptied(dve, ticket0["zg"] + m)
                dve_step(dve, dve.reciprocal(o_rt[:, m, :], o_rt[:, m, :]))
                dve_step(dve, dve.scalar_tensor_tensor(mix2[:, m, :], mix2[:, m, :], col("gdn_norm_w_2"), o_rt[:, m, :], ALU.mult, ALU.mult))
                dve.tensor_tensor(mix2[:, m, :], mix2[:, m, :], zT[:, m, :], ALU.mult).then_inc(S("y_gdn"), 1)
            for m in range(8):
                t = ticket0["w_out2"] + m
                bank = filled(dve, t)
                drained(dve.tensor_tensor(xT[:, m, 0:NL], xT[:, m, 0:NL], bank[:, :], ALU.add), t)

            norm_scale(dve, "mem", memT, TBM, mem_h, lambda k, s: col("norm_mem_w_2", k), rs=rstd_mem)
            norm_scale(dve, "xat", xT, TBL, hT, lambda k, s: col("norm_xattn_w_2", k))
            for n in range(17):
                if n < 16:
                    st = stat[:, n % 2]
                    bank = filled(dve, ticket0[f"xscore{n}"])
                    if n >= 2:
                        dve.wait_ge(S("xat_prob"), n - 1)
                    dve_step(dve, dve.tensor_reduce(st[:, 0:1], bank[:, 0:MEM], AX_X, ALU.max))
                    dve.tensor_scalar(st[:, 3:4], st[:, 0:1], -xat_scale, None, ALU.mult).then_inc(S("xat_max"), 1)
                if n >= 1:
                    st = stat[:, (n - 1) % 2]
                    emptied(dve, ticket0[f"xscore{n - 1}"])
                    dve_step(dve, dve.reciprocal(st[:, 5:6], st[:, 4:5]))
                    dve.tensor_scalar(xprob[:, (n - 1) % 2, :], xprob[:, (n - 1) % 2, :], st[:, 5:6], None, ALU.mult).then_inc(S("xat_prob"), 1)
            for m in range(KD):
                t = ticket0["wo"] + m
                bank = filled(dve, t)
                drained(dve.tensor_tensor(xT[:, m, 0:NL], xT[:, m, 0:NL], bank[:, :], ALU.add), t)

            norm_scale(dve, "ffn", xT, TBL, hT, lambda k, s: col("norm_ffn_w_2", k))
            dve.memset(fin[:, 5:6], 0.0).then_inc(S("u_used"), ERING)
            dve.memset(fin[:, 6:7], 0.0).then_inc(S("v_used"), ERING)
            LOWEST = -3.4e38

            def top16(values, top, index, release=None):
                n = len(values)
                for r in (slice(0, 8), slice(8, 16)):
                    for v in range(n):
                        last = dve.max(top[v][:, r], values[v])
                    dve_step(dve, last)
                    for v in range(n):
                        last = dve.max_index(index[v][:, r], top[v][:, r], values[v])
                    if r.start == 0:
                        dve_step(dve, last)
                        for v in range(n):
                            last = dve.match_replace(values[v], top[v][:, r], values[v], LOWEST)
                        dve_step(dve, last)
                    elif release:
                        last.then_inc(S(release), 1)
                    else:
                        dve_step(dve, last)

            dve.wait_ge(S("peer_landed"), 16 * 3)
            for m in range(KD):
                emptied(dve, ticket0["wo"] + m)
            for u, (j, t) in enumerate(UNITS):
                emptied(dve, ticket0[f"psc{j}"] + t)
                vec = [(h, s) for h in range(2) for s in range(2)]
                top16([psc[:, u % 2, v, :] for v in range(4)], [s_top[:, h, s, :] for h, s in vec], [i_top[:, h, s, :] for h, s in vec], "psc_used")
                dve.wait_ge(S("psc_used"), u + 1)
                dve.tensor_copy(i_f, i_top)
                for h in range(2):
                    last = dve.tensor_tensor(cand[:, h, :].rearrange("p (a b) -> p a b", a=PTOPK), bcast(s_top[:, h, 0, :], PTOPK),
                                             s_top[:, h, 1, :].unsqueeze(1).to_broadcast([P, PTOPK, PTOPK]), ALU.add)
                dve_step(dve, last)
                top16([cand[:, h, :] for h in range(2)], [best[:, t, 2 * j + h, :] for h in range(2)], [pos_u[:, h, :] for h in range(2)])
                dve_step(dve, dve.tensor_copy(pos_f, pos_u))
                dve_step(dve, dve.tensor_scalar(pos_r, pos_f, 1.0 / PTOPK, -0.46875, ALU.mult, ALU.add))
                dve_step(dve, dve.tensor_scalar(pos_r, pos_r, 12582912.0, None, ALU.add))
                dve_step(dve, dve.tensor_scalar(pos_hi, pos_r, -12582912.0, None, ALU.add))
                dve_step(dve, dve.scalar_tensor_tensor(pos_lo, pos_hi, -float(PTOPK), pos_f, ALU.mult, ALU.add))
                pick = ((0, pos_hi), (1, pos_lo))
                for s, sel in pick:
                    for h in range(2):
                        last = dve.tensor_tensor(onehot[:, s, h], bcast(sel[:, h, :], PTOPK), iota16.unsqueeze(1).to_broadcast([P, PTOPK, PTOPK]), ALU.is_equal)
                dve_step(dve, last)
                for s, sel in pick:
                    for h in range(2):
                        last = dve.tensor_tensor(onehot[:, s, h], onehot[:, s, h], i_f[:, h, s, :].unsqueeze(1).to_broadcast([P, PTOPK, PTOPK]), ALU.mult)
                dve_step(dve, last)
                dve_step(dve, dve.tensor_reduce(e_half, onehot, AX_X, ALU.add))
                dve.scalar_tensor_tensor(idxs[:, t, 32 * j:32 * j + 32].rearrange("p (h k) -> p h k", h=2), e_half[:, 0], float(PNK), e_half[:, 1],
                                         ALU.mult, ALU.add).then_inc(S("peer_idx"), 1)
            dve.wait_ge(S("peer_idx"), len(UNITS))
            dve_step(dve, dve.memset(wide_ident, 0.0))
            dve.tensor_copy(wide_ident[:, 3 * P:4 * P], ident[:, :]).then_inc(S("wide_ident"), 1)
            g_ = gate.rearrange("p t (h k) -> p (t h) k", h=PH)
            b_ = best.rearrange("p t h k -> p (t h) k")
            dve_step(dve, dve.tensor_copy(gate_sum, b_[:, :, 0]))
            dve.tensor_tensor(b_, b_, bcast(gate_sum, PTOPK), ALU.subtract).then_inc(S("best_ready"), 1)
            dve.wait_ge(S("gate_exp"), 1)
            dve_step(dve, dve.tensor_reduce(gate_sum, g_, AX_X, ALU.add))
            dve_step(dve, dve.reciprocal(gate_sum, gate_sum))
            dve_step(dve, dve.tensor_tensor(g_, g_, bcast(gate_sum, PTOPK), ALU.mult))
            for n in range(8):
                emptied(dve, ticket0["htok"] + n)
            for T_ in range(NTL):
                with dve.Fori(0, EGROUPS) as i:
                    for s in range(ERING):
                        dve.wait_ge(S(f"u_landed{s}"), i * 16 + 16 * (EGROUPS * T_ + 1))
                        dve.scalar_tensor_tensor(u_row[s], u_row[s], 1.0, h_tok[:, T_, :], ALU.mult, ALU.mult, accum_out=dots[:, s:s + 1]).then_inc(S("u_used"), 1)
                    dve.wait_ge(S("gelus_ready"), i + EGROUPS * T_ + 1)
                    dve.tensor_tensor(acts, gelus, gate[:, T_, bass.ds(i * ERING, ERING)], ALU.mult).then_inc(S("acts_ready"), 1)
                dve.wait_ge(S("fin_sq"), T_ + 1)
                dve.tensor_tensor(fin[:, 2:3], fin[:, 0:1], fin[:, 1:2], ALU.add).then_inc(S("fin_sum"), 1)
                dve.wait_ge(S("fin_root"), T_ + 1)
                dve_step(dve, dve.reciprocal(fin[:, 4:5], fin[:, 3:4]))
                if T_ >= 1:
                    dve.wait_ge(S("out_done"), 16 * T_)
                for g in range(2):
                    last = dve.scalar_tensor_tensor(out_tile[:, 512 * g:512 * g + 512], filled(dve, ticket0["ffn"] + 2 * T_ + g)[:, :], fin[:, 4:5],
                                                    w_final[:, 512 * g:512 * g + 512], ALU.mult, ALU.mult)
                last.then_inc(S("out_ready"), 1)


        @block_.tensor
        def _(pe):
            pe.wait_ge(S("small_landed"), 16 * SMALL_LOADS)
            pe.wait_ge(S("x_landed"), 16 * 6)
            for n in range(12):
                t, g = n // 2, n % 2
                bank = claim(pe, ticket0["x_in"] + n)
                for j in range(4):
                    last = pe.transpose(bank[:, j * P:(j + 1) * P], x_in[:, t, (4 * g + j) * P:(4 * g + j + 1) * P], ident[:, :])
                fill(last, ticket0["x_in"] + n)
            for i, (rows, _, n) in enumerate(vec_rows):
                bank = claim(pe, ticket0["vecs"] + i)
                fill(pe.transpose(bank[:, 0:n], rows[0:n, :], ident[0:n, 0:n]), ticket0["vecs"] + i)
            pe.wait_ge(S("act_done"), 2)
            for l in range(2):
                with pe.Fori(0, 3) as i:
                    for s in range(NSLOT):
                        w = block(pe, block0[f"ada{l}"] + s, KD, extra=i)
                        for j in range(2):
                            t = ticket0[f"ada{l}"] + 2 * s + j
                            bank = claim(pe, t, i)
                            for m in range(2):
                                for k in range(KD):
                                    last = pe.matmul(bank[:, 2 * m:2 * m + 2], w[:, k, (2 * j + m) * P:(2 * j + m + 1) * P],
                                                     silu_c[:, k, :], start=(k == 0), stop=(k == KD - 1))
                            fill(last, t)
            norm_sums(pe, "l0a", TBS, hT)
            w = block(pe, block0["w_in0"], KD, n=MLA_IN)
            for m in range(4):
                a, n = (m * P, P) if m < 3 else (Q_LORA + KV_LORA, ROPE)
                for b, (lo, hi) in enumerate(TBS):
                    t = ticket0["z_q"] + 2 * m + b
                    bank = claim(pe, t)
                    o = bank[:, 0:hi - lo] if m < 3 else bank[NOPE:QK, 0:hi - lo]
                    for k in range(KD):
                        pe.wait_ge(S("l0a_ready"), 2 * k + 2)
                        last = pe.matmul(o, w[:, k, a:a + n], hT[:, k, lo:hi], start=(k == 0), stop=(k == KD - 1))
                    fill(last, t)
            norm_sums(pe, "cq", TBS, sqs, 2, per=2)
            norm_sums(pe, "ckv", TBS, prob, 1, per=2)
            wv = block(pe, block0["ukv"], 1, n=1024)[:, 0, :].rearrange("p (h two v) -> p h two v", h=H_A, two=2)
            pe.wait_ge(S("ckv_mul"), 2)
            for t in range(6):
                bank = claim(pe, ticket0["v_tok"] + t)
                fill(pe.matmul(bank[:, :].rearrange("p (h v) -> p h v", h=H_A), ckvT[:, t * P:(t + 1) * P], wv[:, :, 1, :],
                               start=True, stop=True), ticket0["v_tok"] + t)
            wq = block(pe, block0["uq"], 2, n=H_A * QK)
            for step, n in mla_order():
                t0 = ticket0[f"{step}{n}"]
                h = n if step in ("proj", "norm", "rot") else n // 6
                if step == "proj":
                    if h == 0:
                        pe.wait_ge(S("cq_mul"), 4)
                    for b, (lo, hi) in enumerate(TBS):
                        bank = claim(pe, t0 + b)
                        for k in range(2):
                            last = pe.matmul(bank[0:QK, 0:hi - lo], wq[:, k, h * QK:(h + 1) * QK], cqT[:, k, lo:hi],
                                             start=(k == 0), stop=(k == 1))
                        fill(last, t0 + b)
                    for b, (lo, hi) in enumerate(TBS):
                        bank = claim(pe, t0 + 2 + b)
                        fill(pe.matmul(bank[0:NOPE, 0:hi - lo], wv[:, h, 0, :], ckvT[:, lo:hi], start=True, stop=True), t0 + 2 + b)
                elif step == "norm":
                    for j in range(2):
                        pe.wait_ge(S("qk_sq"), h + 1)
                        for b, (lo, hi) in enumerate(TBS):
                            bank = claim(pe, t0 + 2 * j + b)
                            fill(pe.matmul(bank[0:QK, 0:hi - lo], ones[0:QK, 0:QK], sqs[0:QK, j, lo:hi], start=True, stop=True),
                                 t0 + 2 * j + b)
                elif step == "rot":
                    pe.wait_ge(S("mla_tables"), 16 * MLA_LOADS)
                    for j, x in enumerate((qh, kh)):
                        pe.wait_ge(S("qk_normed"), 4 * h + 2 * j + 2)
                        bank = claim(pe, t0 + j)
                        fill(pe.matmul(bank[0:QK, :], rot_mla[0:QK, 0:QK], x[0:QK, h % 2, 0:NL], start=True, stop=True), t0 + j)
                elif step == "scores":
                    pe.wait_ge(S("qk_ready"), 2 * h + 2)
                    q = qh[0:QK, h % 2, (n % 6) * P:(n % 6 + 1) * P]
                    for b, keys in enumerate(KEYS if n % 6 < 4 else KEYS[1:]):
                        bank = claim(pe, t0 + b)
                        k = kh[0:QK, h % 2, keys]
                        fill(pe.matmul(bank[:, 0:k.shape[1]], q, k, start=True, stop=True), t0 + b)
                elif step == "turn":
                    pe.wait_ge(S("prob_ready"), n + 1)
                    for b, tiles in enumerate(((0, 1, 2, 3), (4, 5)) if n % 6 < 4 else ((4, 5),)):
                        bank = claim(pe, t0 + b)
                        for j, t in enumerate(tiles):
                            last = pe.transpose(bank[:, j * P:(j + 1) * P], prob[:, n % 2, t * P:(t + 1) * P], ident[:, :])
                        fill(last, t0 + b)
                else:
                    tiles = range(6) if n % 6 < 4 else (4, 5)
                    bank = claim(pe, t0)
                    tt = ticket0[f"turn{n}"]
                    for b in range(mla_tickets("turn", n)):
                        emptied(pe, tt + b)
                    for t in tiles:
                        last = pe.matmul(bank[HEADROWS[h], 0:P], v_tok[:, t, h * 64:(h + 1) * 64], probT[:, n % 2, t, :],
                                         start=(t == tiles[0]), stop=(t == 5))
                    fill(last, t0)
            for j, name in enumerate(("z_rq", "z_rk", "z_rv", "z_rg")):
                w = block(pe, block0["w_in_r"] + j, KD)
                if name == "z_rv":
                    for t in range(6):
                        bank = claim(pe, ticket0[name] + t)
                        for k in range(KD):
                            last = pe.matmul(bank[:, :], hT[:, k, t * P:(t + 1) * P], w[:, k, :], start=(k == 0), stop=(k == KD - 1))
                        fill(last, ticket0[name] + t)
                    continue
                for m in range(4):
                    for b, (lo, hi) in enumerate(TBS):
                        t = ticket0[name] + 2 * m + b
                        bank = claim(pe, t)
                        for k in range(KD):
                            last = pe.matmul(bank[:, 0:hi - lo], w[:, k, m * P:(m + 1) * P], hT[:, k, lo:hi],
                                             start=(k == 0), stop=(k == KD - 1))
                        fill(last, t)
            pe.wait_ge(S("ret_tables"), 48)
            for j, (name, x) in enumerate((("z_rq", rqT), ("z_rk", rkT))):
                for m in range(4):
                    emptied(pe, ticket0[name] + 2 * m)
                    t = ticket0["rrot"] + 4 * j + m
                    fill(pe.matmul(claim(pe, t)[:, :], rot_ret, x[:, m, 0:NL], start=True, stop=True), t)
            for b in range(6):
                emptied(pe, ticket0["z_rv"] + b)
            for step, m in ret_order():
                h, j = m // 8, m % 8
                r, c = HEADROWS[h], h // 2
                lat = j < 6
                q = slice(0, NL) if lat else KEYS[1]
                kt = j if lat else j - 2
                if step == "rscore":
                    if h % 2 == 0 and j == 0:
                        pe.wait_ge(S("rot_done"), 5 + c)
                    t = ticket0[f"rscore{m}"]
                    bank = claim(pe, t)
                    fill(pe.matmul(bank[:, 0:q.stop - q.start], rkT[r, c, kt * P:(kt + 1) * P], rqT[r, c, q], start=True, stop=True), t)
                else:
                    t = ticket0[f"rout{h}_{j // 6}"]
                    if j in (0, 6):
                        claim(pe, t)
                    emptied(pe, ticket0[f"rscore{m}"])
                    last = pe.matmul(ps[t % NBANK][r, 0:q.stop - q.start], rv[:, kt, h * 64:(h + 1) * 64],
                                     decayed[:, m % 4, 0:q.stop - q.start], start=j in (0, 6), stop=j in (5, 7))
                    if j in (5, 7):
                        fill(last, t)
            for c in range(4):
                for b, (lo, hi) in enumerate(TBS):
                    for h in (2 * c, 2 * c + 1):
                        emptied(pe, ticket0[f"rout{h}_{b}"])
                    t = ticket0["rmean"] + 2 * c + b
                    fill(pe.matmul(claim(pe, t)[:, 0:hi - lo], blk64[:, :], mixT[:, 4 + c, lo:hi], start=True, stop=True), t)
            for c in range(4):
                for b, (lo, hi) in enumerate(TBS):
                    pe.wait_ge(S("ret_sq"), 2 * c + b + 1)
                    t = ticket0["rvar"] + 2 * c + b
                    fill(pe.matmul(claim(pe, t)[:, 0:hi - lo], blk64[:, :], rqT[:, c, lo:hi], start=True, stop=True), t)
            for j in range(2):
                w = block(pe, block0["w_out"] + j, 8)
                for m in range(4):
                    for b, (lo, hi) in enumerate(TBS):
                        t = ticket0["w_out"] + 8 * j + 2 * m + b
                        bank = claim(pe, t)
                        for k in range(8):
                            if j == 0 and k >= 4:
                                pe.wait_ge(S("ret_gated"), 2 * (k - 4) + b + 1)
                            last = pe.matmul(bank[:, 0:hi - lo], w[:, k, m * P:(m + 1) * P], mixT[:, k, lo:hi],
                                             start=(k == 0), stop=(k == 7))
                        fill(last, t)
            norm_sums(pe, "l0b", TBS, hT)
            for k in range(KD):
                pe.wait_ge(S("l0b_ready"), 2 * k + 2)
            mlp_products(pe, 0, TBS)
            norm_sums(pe, "l1a", TBS, hT)
            pe.wait_ge(S("s5_landed"), 16 * S5_LOADS)
            pe.wait_ge(S("s5_dt_rows"), 2)
            for d in range(2):
                t = ticket0["s5_prm"] + d
                fill(pe.transpose(claim(pe, t)[:, 0:96], prm_rows[0:96, d, :], ident[0:96, 0:96]), t)
            for n in range(8):
                a, half = n // 2, n % 2
                t = ticket0["s5_c"] + n
                bank = claim(pe, t)
                for j in range(4):
                    last = pe.transpose(bank[:, j * P:(j + 1) * P], c_rows[:, a, 4 * half + j, :], ident[:, :])
                fill(last, t)
            for k in range(KD):
                pe.wait_ge(S("l1a_ready"), 2 * k + 2)
            with pe.Fori(0, 8) as i:
                pe.wait_ge(S("s5_hs"), i + 1)
                hs = s5_hs[:, 0:NT].rearrange("p (c t) -> p t c", t=8)
                for n in range(4):
                    t = s5_t(T_U + n)
                    bank = claim(pe, t, 3 * i)
                    for j in range(2):
                        last = pe.transpose(bank[0:NCH, j * P:(j + 1) * P], hs[:, 2 * n + j, :], ident[:, :])
                    fill(last, t)
                for n in range(4):
                    emptied(pe, s5_t(T_U + n), 3 * i)
                for n in range(2):
                    t = s5_t(T_UT + n)
                    bank = claim(pe, t, 3 * i)
                    for j in range(4):
                        g = 4 * n + j
                        last = pe.transpose(bank[:, j * NCH:(j + 1) * NCH], s5_utok[0:NCH, g * P:(g + 1) * P], ident[0:NCH, 0:NCH])
                    fill(last, t)
                for d in range(2):
                    pe.wait_ge(S("s5_F"), 2 * i + d + 1)
                    for c in range(2):
                        t = s5_t(T_FT[d] + c)
                        bank = claim(pe, t, 3 * i)
                        for r in range(4):
                            last = pe.transpose(bank[:, r * P:(r + 1) * P], s5_F[:, d, c, r, :], ident[:, :])
                        fill(last, t)
                    for c in range(2):
                        emptied(pe, s5_t(T_FT[d] + c), 3 * i)
                        if d == 0:
                            emptied(pe, s5_t(T_UT + c), 3 * i)
                    for c in range(2):
                        t = s5_t(T_FI[d] + c)
                        bank = claim(pe, t, 3 * i)
                        for r in range(4):
                            for par in range(2):
                                last = pe.matmul(bank[64 * par:64 * par + 64, r * NCH:(r + 1) * NCH],
                                                 s5_FT[:, c, r, 64 * par:64 * par + 64], s5_u[:, 2 * r + par, :], start=True, stop=True)
                        fill(last, t)
                for d in range(2):
                    pe.wait_ge(S("pool_done"), i * (1 + 7 * 6 + 2 * 6) + 4 + 7 * 6 + 6 * (d + 1))
                    for n in range(2):
                        t = s5_t(T_MM[d] + n)
                        bank = claim(pe, t, 3 * i)
                        for j in range(4):
                            rows = slice(64 * n, 64 * n + 64)
                            for c in range(2):
                                last = pe.matmul(bank[:, j * P:(j + 1) * P], s5_F[rows, d, c, j, :], s5_E[rows, d, c, j, :],
                                                 start=(c == 0), stop=(c == 1))
                        fill(last, t)
                pe.wait_ge(S("s5_M"), 2 * i + 2)
                pe.wait_ge(S("s5_turned"), 2 * i + 3)
                for n in range(4):
                    t = s5_t(T_Y + n)
                    bank = claim(pe, t, 3 * i)
                    for j in range(2):
                        g = 2 * (2 * (n // 2) + j) + n % 2
                        rows = slice(64 * (g % 2), 64 * (g % 2) + 64)
                        o = bank[0:LCH, j * P:(j + 1) * P]
                        pe.matmul(o, s5_u[:, g, CCH:NCH], s5_M[:, g, :], start=True, stop=False)
                        for d in range(2):
                            for c in range(2):
                                last = pe.matmul(o, s5_s[rows, d, c, g // 2, :], s5_E[rows, d, c, g // 2, :], start=False,
                                                 stop=(d == 1 and c == 1))
                    fill(last, t)
                for n in range(4):
                    emptied(pe, s5_t(T_Y + n), 3 * i)
                for n in range(2):
                    t = s5_t(T_YB + n)
                    bank = claim(pe, t, 3 * i)
                    pe.nop(nofuse=True)
                    for j in range(4):
                        tk = 4 * n + j
                        last = pe.transpose(bank[:, j * LCH:(j + 1) * LCH], s5_ytok[0:LCH, tk * P:(tk + 1) * P], ident[0:LCH, 0:LCH])
                    fill(last, t)
            for j in range(2):
                w = [block(pe, block0["glu"] + 2 * j + half, KD) for half in range(2)]
                for m in range(4):
                    for half in range(2):
                        t = ticket0["glu"] + 8 * j + 2 * m + half
                        bank = claim(pe, t)
                        for k in range(KD):
                            pe.wait_ge(S("gelu"), k + 1)
                            last = pe.matmul(bank[:, :], w[half][:, k, m * P:(m + 1) * P], hT[:, k, 0:NL],
                                             start=(k == 0), stop=(k == KD - 1))
                        fill(last, t)

            norm_sums(pe, "l1b", TBL, hT)
            for k in range(KD):
                pe.wait_ge(S("l1b_ready"), k + 1)
            mlp_products(pe, 1, TBL)
            norm_sums(pe, "mix", TBL, hT)
            for name, blk, count in (("qkv", "w_in2", 3), ("zg", "w_in2", 1), ("ab", "w_ab", 1), ("xr", "w_xg", 1), ("gate", "w_xg", 1)):
                for j in range(count):
                    bi = block0[blk] + j + (3 if name == "zg" else 1 if name == "gate" else 0)
                    if name == "ab":
                        w = block(pe, bi, KD, n=8)
                        bank = claim(pe, ticket0["ab"])
                        for t in range(NTL):
                            for k in range(KD):
                                last = pe.matmul(bank[:, 8 * t:8 * t + 8], hT[:, k, t * P:(t + 1) * P], w[:, k, :],
                                                 start=(k == 0), stop=(k == KD - 1))
                        fill(last, ticket0["ab"])
                        continue
                    w = block(pe, bi, KD)
                    for m in range(4):
                        t = ticket0[name] + 4 * j + m
                        bank = claim(pe, t)
                        for k in range(KD):
                            pe.wait_ge(S("mix_mul"), k + 1)
                            last = pe.matmul(bank[:, :], w[:, k, m * P:(m + 1) * P], hT[:, k, 0:NL], start=(k == 0), stop=(k == KD - 1))
                        fill(last, t)
            pe.wait_ge(S("mix2_landed"), 16 * MIX2_LOADS)
            for a, name in enumerate(("lru_r", "lru_i")):
                for m in range(4):
                    emptied(pe, ticket0["xr"] + m)
                    t = ticket0[name] + m
                    fill(pe.matmul(claim(pe, t)[:, :], lru_w[:, a, m, :], xrT[:, m, :], start=True, stop=True), t)
            for m in range(8):
                pe.wait_ge(S("gq_sq"), m + 1)
                t = ticket0["gnorm"] + m
                fill(pe.matmul(claim(pe, t)[:, :], ones[:, :], qk_sq[:, m, :], start=True, stop=True), t)
            for name, m0 in (("ktok", 4), ("vtok", 8)):
                if name == "ktok":
                    pe.wait_ge(S("g_normed"), 8)
                else:
                    pe.wait_ge(S("qkv_silu"), 12)
                for t in range(NTL):
                    tk = ticket0[name] + t
                    bank = claim(pe, tk)
                    for h in range(4):
                        last = pe.transpose(bank[:, h * P:(h + 1) * P], qkvT[:, m0 + h, t * P:(t + 1) * P], ident[:, :])
                    fill(last, tk)
            pe.wait_ge(S("g_masks"), 16 * 9)
            pe.wait_ge(S("g_ready"), 1)
            for pair in range(2):
                for tt in (2 * pair, 2 * pair + 1):
                    t0, x = ticket0[f"gpre{tt}"], tt % 2
                    tok = slice(tt * P, (tt + 1) * P)
                    pe.wait_ge(S("g_bcast"), tt + 1)
                    bank = claim(pe, t0)
                    pe.matmul(bank[:, 0:4], tri_incl, gt[:, G_G, tt, :], start=True, stop=True)
                    pe.matmul(bank[:, 4:8], g_suffix, gt[:, G_G, tt, :], start=True, stop=True)
                    for h in range(4):
                        last = pe.matmul(bank[:, 8 + 2 * h:10 + 2 * h], g_bc[:, h, :], g_ind, start=True, stop=True)
                    fill(last, t0)
                    bank = claim(pe, t0 + 1)
                    for h in range(4):
                        last = pe.matmul(bank[:, h * P:(h + 1) * P], g_bc[:, h, :], tri_incl, start=True, stop=True)
                    fill(last, t0 + 1)
                    pe.wait_ge(S("g_kb"), tt + 1)
                    bank = claim(pe, t0 + 2)
                    for h in range(4):
                        last = pe.transpose(bank[:, h * P:(h + 1) * P], g_kw[:, h, :], ident[:, :])
                    fill(last, t0 + 2)
                    emptied(pe, t0 + 2)
                    bank = claim(pe, t0 + 3)
                    for h in range(4):
                        last = pe.matmul(bank[:, h * P:(h + 1) * P], qkvT[:, 4 + h, tok], g_kbT[:, h, :], start=True, stop=True)
                    fill(last, t0 + 3)
                    bank = claim(pe, t0 + 4)
                    for h in range(4):
                        last = pe.matmul(bank[:, h * P:(h + 1) * P], qkvT[:, 4 + h, tok], qkvT[:, h, tok], start=True, stop=True)
                    fill(last, t0 + 4)
                for lv in range(6):
                    t0 = ticket0[f"inv{pair}_{lv}"]
                    for x in range(2):
                        pe.wait_ge(S("g_level"), 12 * pair + 2 * lv + x + 1)
                        if lv > 0:
                            emptied(pe, ticket0[f"inv{pair}_{lv - 1}"] + 2 + 2 * x)
                            emptied(pe, ticket0[f"inv{pair}_{lv - 1}"] + 3 + 2 * x)
                        else:
                            pe.wait_ge(S("g_eye"), pair + 1)
                        bank = claim(pe, t0 + x)
                        for h in range(4):
                            last = pe.matmul(bank[:, h * P:(h + 1) * P], g_lvl[:, x, h, :], inv_x[:, x, h, :], start=True, stop=True)
                        fill(last, t0 + x)
                    for x in range(2):
                        emptied(pe, t0 + x)
                        bank = claim(pe, t0 + 2 + 2 * x)
                        for h in range(4):
                            last = pe.matmul(bank[:, h * P:(h + 1) * P], inv_xt[:, x, h, :], inv_y[:, x, h, :], start=True, stop=True)
                        fill(last, t0 + 2 + 2 * x)
                        bank = claim(pe, t0 + 3 + 2 * x)
                        for h in range(4):
                            last = pe.matmul(bank[:, h * P:(h + 1) * P], inv_y[:, x, h, :], inv_xt[:, x, h, :], start=True, stop=True)
                        fill(last, t0 + 3 + 2 * x)
                for tt in (2 * pair, 2 * pair + 1):
                    t0, x = ticket0[f"uw{tt}"], tt % 2
                    for b in range(4):
                        emptied(pe, ticket0[f"inv{pair}_5"] + 2 + b)
                    emptied(pe, ticket0["vtok"] + tt)
                    bank = claim(pe, t0)
                    for h in range(4):
                        last = pe.matmul(bank[:, h * P:(h + 1) * P], inv_xt[:, x, h, :], u_tok[:, tt, h, :], start=True, stop=True)
                    fill(last, t0)
                    pe.wait_ge(S("g_kw"), tt + 1)
                    bank = claim(pe, t0 + 1)
                    for h in range(4):
                        last = pe.matmul(bank[:, h * P:(h + 1) * P], g_kw[:, h, :], inv_xt[:, x, h, :], start=True, stop=True)
                    fill(last, t0 + 1)
            pe.wait_ge(S("g_qdec"), 4)
            pe.wait_ge(S("g_kdec"), 4)
            for n in range(8):
                tt, r = n // 2, GHALF[n % 2]
                tok = slice(n * GCH, (n + 1) * GCH)
                t0 = ticket0["gscan"] + 3 * n
                pe.wait_ge(S("g_state"), 4 * n + 1)
                if n % 2 == 0:
                    emptied(pe, ticket0[f"uw{tt}"] + 1)
                for h in range(4):
                    pe.wait_ge(S("g_state"), 4 * n + 1 if n == 0 else 4 * (n - 1) + 1 + h + 1)
                bank = claim(pe, t0)
                for h in range(4):
                    last = pe.matmul(bank[r, h * P:(h + 1) * P], wT[:, h, tok], g_state[:, h, :], start=True, stop=True)
                fill(last, t0)
                emptied(pe, t0)
                bank = claim(pe, t0 + 1)
                for h in range(4):
                    o = bank[:, h * GCH:(h + 1) * GCH]
                    pe.matmul(o, g_state[:, h, :], qkvT[:, h, tok], start=True, stop=False)
                    last = pe.matmul(o, v_new[r, h * P:(h + 1) * P], attnT[r, tt, h, r], start=False, stop=True)
                fill(last, t0 + 1)
                bank = claim(pe, t0 + 2)
                for h in range(4):
                    last = pe.matmul(bank[:, h * P:(h + 1) * P], k_tok[r, tt, h, :], v_new[r, h * P:(h + 1) * P], start=True, stop=True)
                fill(last, t0 + 2)
            for m in range(4):
                pe.wait_ge(S("o_sq"), m + 1)
                t = ticket0["norm_o"] + m
                fill(pe.matmul(claim(pe, t)[:, :], ones[:, :], qkvT[:, m, :], start=True, stop=True), t)
            for j in range(2):
                w = block(pe, block0["w_out2"] + j, 8)
                for m in range(4):
                    t = ticket0["w_out2"] + 4 * j + m
                    bank = claim(pe, t)
                    for k in range(8):
                        if j == 0 and m == 0:
                            pe.wait_ge(S("y_gdn"), min(k + 1, 4))
                        last = pe.matmul(bank[:, :], w[:, k, m * P:(m + 1) * P], mix2[:, k, :], start=(k == 0), stop=(k == 7))
                    fill(last, t)
            pe.wait_ge(S("mem_landed"), 32)
            for n in range(4):
                t, g = n // 2, n % 2
                bank = claim(pe, ticket0["mem_in"] + n)
                for j in range(4):
                    last = pe.transpose(bank[:, j * P:(j + 1) * P], mem_in[:, t, (4 * g + j) * P:(4 * g + j + 1) * P], ident[:, :])
                fill(last, ticket0["mem_in"] + n)
            norm_sums(pe, "mem", TBM, mem_h)
            pe.wait_ge(S("mem_mul"), KD)
            for j in range(2):
                w = block(pe, block0["xkv"] + j, KD)
                for n in range(2):
                    t = ticket0["xk"] + 2 * j + n
                    bank = claim(pe, t)
                    for m in range(2):
                        for k in range(KD):
                            last = pe.matmul(bank[:, m * MEM:(m + 1) * MEM], w[:, k, (2 * n + m) * P:(2 * n + m + 1) * P], mem_h[:, k, :],
                                             start=(k == 0), stop=(k == KD - 1))
                    fill(last, t)
            for j in range(2):
                w = block(pe, block0["xkv"] + 2 + j, KD)
                for tt in range(2):
                    t = ticket0["xv"] + 2 * j + tt
                    bank = claim(pe, t)
                    for k in range(KD):
                        last = pe.matmul(bank[:, :], mem_h[:, k, tt * P:(tt + 1) * P], w[:, k, :], start=(k == 0), stop=(k == KD - 1))
                    fill(last, t)
            norm_sums(pe, "xat", TBL, hT)
            for j in range(2):
                w = block(pe, block0["xq"] + j, KD)
                for m in range(4):
                    t = ticket0["xq"] + 4 * j + m
                    bank = claim(pe, t)
                    for k in range(KD):
                        pe.wait_ge(S("xat_mul"), k + 1)
                        last = pe.matmul(bank[:, :], w[:, k, m * P:(m + 1) * P], hT[:, k, 0:NL], start=(k == 0), stop=(k == KD - 1))
                    fill(last, t)
            for step, n in XAT_ORDER:
                t, h, tok = ticket0[f"{step}{n}"], n // 4, slice(n % 4 * P, (n % 4 + 1) * P)
                bank = None
                if step == "xscore":
                    for c in range(2):
                        emptied(pe, ticket0["xq"] + 2 * h + c)
                    emptied(pe, ticket0["xk"] + h)
                    bank = claim(pe, t)
                    for c in range(2):
                        last = pe.matmul(bank[:, 0:MEM], xqT[:, 2 * h + c, tok], xkT[:, 2 * h + c, :], start=(c == 0), stop=(c == 1))
                elif step == "xturn":
                    pe.wait_ge(S("xat_prob"), n + 1)
                    bank = claim(pe, t)
                    for j in range(2):
                        last = pe.transpose(bank[:, j * P:(j + 1) * P], xprob[:, n % 2, j * P:(j + 1) * P], ident[:, :])
                else:
                    emptied(pe, ticket0[f"xturn{n}"])
                    for tt in range(2):
                        emptied(pe, ticket0["xv"] + 2 * (h // 2) + tt)
                    bank = claim(pe, t)
                    for c in range(2):
                        for tt in range(2):
                            last = pe.matmul(bank[:, c * P:(c + 1) * P], xv_tok[:, tt, h * XDH + c * P:h * XDH + (c + 1) * P], xprobT[:, n % 2, tt, :],
                                             start=(tt == 0), stop=(tt == 1))
                fill(last, t)
            for j in range(2):
                w = block(pe, block0["wo"] + j, KD)
                for m in range(4):
                    t = ticket0["wo"] + 4 * j + m
                    bank = claim(pe, t)
                    for k in range(KD):
                        if j == 0 and m == 0:
                            for qt in range(4):
                                emptied(pe, ticket0[f"xout{4 * (k // 2) + qt}"])
                        last = pe.matmul(bank[:, :], w[:, k, m * P:(m + 1) * P], xoT[:, k, :], start=(k == 0), stop=(k == KD - 1))
                    fill(last, t)
            pe.wait_ge(S("peer_landed"), 16 * 3)
            for n in range(4):
                bank = claim(pe, ticket0["subk"] + n)
                for v in range(4):
                    last = pe.transpose(bank[:, v * P:(v + 1) * P], sub_rows[:, 4 * n + v, :], ident[:, :])
                fill(last, ticket0["subk"] + n)
            norm_sums(pe, "ffn", TBL, hT)
            for j in range(4):
                w = block(pe, block0["peer_wq"] + j, KD)
                for v in range(4):
                    t = ticket0[f"pq{j}"] + v
                    bank = claim(pe, t)
                    for k in range(KD):
                        pe.wait_ge(S("ffn_mul"), k + 1)
                        last = pe.matmul(bank[:, :], w[:, k, v * P:(v + 1) * P], hT[:, k, 0:NL], start=(k == 0), stop=(k == KD - 1))
                    fill(last, t)
                emptied(pe, ticket0["subk"] + j)
                for t in range(NTL):
                    tk = ticket0[f"psc{j}"] + t
                    for v in range(4):
                        emptied(pe, ticket0[f"pq{j}"] + v)
                    bank = claim(pe, tk)
                    for v in range(4):
                        last = pe.matmul(bank[:, v * P:(v + 1) * P], pqT[:, j % 2, v, t * P:(t + 1) * P], subT[:, 4 * j + v, :], start=True, stop=True)
                    fill(last, tk)
            for n in range(8):
                tk, t = ticket0["htok"] + n, n // 2
                bank = claim(pe, tk)
                for c in range(4):
                    last = pe.transpose(bank[:, c * P:(c + 1) * P], hT[:, 4 * (n % 2) + c, t * P:(t + 1) * P], ident[:, :])
                fill(last, tk)
            pe.wait_ge(S("wide_ident"), 1)
            for T_ in range(NTL):
                banks = [claim(pe, ticket0["ffn"] + 2 * T_ + g) for g in range(2)]

                def residual(g, c):
                    return pe.matmul(banks[g][:, :], xT[:, 4 * g + c, T_ * P:(T_ + 1) * P], wide_ident[:, (3 - c) * P:(7 - c) * P],
                                     start=(c == 0), stop=(c == 3))

                for g in range(2):
                    for c in range(3):
                        residual(g, c)
                with pe.Fori(0, EGROUPS) as i:
                    for s in range(ERING):
                        pe.wait_ge(S(f"v_landed{s}"), i * 16 + 16 * (EGROUPS * T_ + 1))
                        pe.wait_ge(S("diag_ready"), i * ERING + T_ * EXPERTS + s + 1)
                        pe.matmul(banks[0][:, :], diag[:, s, :], v_row[s][:, 0:512], start=False, stop=False)
                        pe.matmul(banks[1][:, :], diag[:, s, :], v_row[s][:, 512:1024], start=False, stop=False).then_inc(S("v_used"), 1)
                for g in range(2):
                    fill(residual(g, 3), ticket0["ffn"] + 2 * T_ + g)


def kernel(**inputs):
    import numpy as _np
    import concourse.bacc as _bacc
    from concourse import mybir as _mybir
    from concourse.bass_utils import run_bass_kernel_spmd as _run

    nc = _bacc.Bacc("TRN2", target_bir_lowering=False, num_devices=1)
    arrays, aps = {}, {}
    for name, value in inputs.items():
        a = _np.ascontiguousarray(value)
        arrays[f"in_{name}"] = a
        aps[name] = nc.dram_tensor(f"in_{name}", a.shape, _mybir.dt.from_np(a.dtype), kind="ExternalInput").ap()
    table = _np.concatenate(list(shape_constants().values()), axis=1)
    arrays["shape_consts"] = table
    consts = nc.dram_tensor("shape_consts", table.shape, _mybir.dt.float32, kind="ExternalInput").ap()
    out = nc.dram_tensor("out_0", (1, NL, D), _mybir.dt.float32, kind="ExternalOutput").ap()
    build(nc, aps, consts, out)
    r = _run(nc, [arrays], core_ids=[0])
    return r.results[0]["out_0"]
```

```python
from contextlib import ExitStack

import numpy as np

import concourse.bass as bass
from concourse import mybir

F32 = mybir.dt.float32
I32 = mybir.dt.int32
U32 = mybir.dt.uint32
ALU = mybir.AluOpType
ACT = mybir.ActivationFunctionType
AX_X = mybir.AxisListType.X

P = 128
D = 1024
KD = D // P
NL = 512
NC = 256
NT = NL + NC
TBS = ((0, NL), (NL, NT))
EPS = 1e-6
GRID_W = 64
ROPE_BASE = 10000.0
H_A, Q_LORA, KV_LORA, NOPE, ROPE, V_DIM = 8, 256, 128, 64, 32, 64
QK = NOPE + ROPE
MLA_IN = Q_LORA + KV_LORA + ROPE
H_R, DK_R = 8, 64
RET_W = H_R * DK_R
S5_CH = 8
S5_DVE_STEPS = 43
MEM = 256
GH = 4
GCH = 64
XA_H = 4
PH, PNK, PTOPK = 8, 128, 16
NBANK = 8
ARENA = 22 * 1024
NSLOT = 4
ADA_ROW = (0, 1, 3, 5)
ADA_COL = (2, 4, 6, 7)
SLOT = 4096


def shape_constants():
    p = np.arange(P)
    c = {}
    c["ident"] = np.eye(P)
    c["ones"] = np.ones((P, P))
    same64 = (p[:, None] // 64) == (p[None, :] // 64)
    c["blk64"] = same64 / 64.0
    rot = np.zeros((P, P))
    for i in range(ROPE // 2):
        rot[NOPE + ROPE // 2 + i, NOPE + i] = -1.0
        rot[NOPE + i, NOPE + ROPE // 2 + i] = 1.0
    c["rot_mla"] = rot
    rot = np.zeros((P, P))
    for b in range(2):
        for i in range(DK_R // 2):
            rot[64 * b + 32 + i, 64 * b + i] = -1.0
            rot[64 * b + i, 64 * b + 32 + i] = 1.0
    c["rot_ret"] = rot
    nf = ROPE // 4
    f = (np.float32(ROPE_BASE) ** (-np.arange(nf, dtype=np.float32) / np.float32(nf))).astype(np.float32)
    t = np.arange(NL)
    ang = np.concatenate([(t // GRID_W).astype(np.float32)[:, None] * f,
                          (t % GRID_W).astype(np.float32)[:, None] * f], axis=-1).astype(np.float32)
    cm, sm = np.zeros((P, NL)), np.zeros((P, NL))
    for half in range(2):
        cm[NOPE + 16 * half:NOPE + 16 * half + 16] = np.cos(ang.astype(np.float64)).T
        sm[NOPE + 16 * half:NOPE + 16 * half + 16] = np.sin(ang.astype(np.float64)).T
    c["cos_mla"], c["sin_mla"] = cm, sm
    nf = DK_R // 2
    th = (np.float32(ROPE_BASE) ** (-np.arange(nf, dtype=np.float32) / np.float32(nf))).astype(np.float32)
    ang = (t.astype(np.float32)[:, None] * th).astype(np.float32).astype(np.float64)
    c["cos_ret"] = np.tile(np.cos(ang).T, (4, 1))
    c["sin_ret"] = np.tile(np.sin(ang).T, (4, 1))
    x = np.arange(896)
    c["ret_dist"] = x[None, :] - 384.0 - p[:, None]
    tau = p // 16
    c["s5_fwd"] = np.tile((tau[:, None] <= tau[None, :]) * 1.0, (1, 4))
    c["s5_bwd"] = np.tile((tau[:, None] >= tau[None, :]) * 1.0, (1, 4))
    same = (p[:, None] // GCH) == (p[None, :] // GCH)
    c["tri_incl"] = (same & (p[:, None] <= p[None, :])) * 1.0
    c["tri_strict"] = (same & (p[:, None] < p[None, :])) * 1.0
    c["suffix"] = (same & (p[:, None] > p[None, :])) * 1.0
    c["chunk_ind"] = ((p[:, None] // GCH) == np.arange(2)[None, :]) * 1.0
    for lv in range(6):
        s = 1 << lv
        blk = (p[:, None] // (2 * s)) == (p[None, :] // (2 * s))
        c[f"merge{lv}"] = (blk & ((p[:, None] // s) % 2 == 0) & ((p[None, :] // s) % 2 == 1)) * 1.0
    c["iota16"] = np.tile(np.arange(16.0), (P, 1))
    return {k: np.ascontiguousarray(v, dtype=np.float32) for k, v in c.items()}


CONST_COLS = {}
_at = 0
for _k, _v in shape_constants().items():
    CONST_COLS[_k] = (_at, _v.shape[1])
    _at += _v.shape[1]
CONST_W = _at


def mla_order():
    yield "proj", 0
    for step in ("nsum", "norm", "rot"):
        for j in range(2):
            yield step, j
    for n in range(6 * H_A + 3):
        if n < 6 * H_A:
            yield "scores", n
        for lag, step in ((1, "scale"), (2, "turn"), (3, "out")):
            if 0 <= n - lag < 6 * H_A:
                yield step, n - lag
        h = n // 6 + 1
        if h < H_A:
            for at, step, m in ((0, "proj", h), (1, "nsum", 2 * h), (1, "nsum", 2 * h + 1), (2, "norm", 2 * h),
                                (3, "norm", 2 * h + 1), (3, "rot", 2 * h), (4, "rot", 2 * h + 1)):
                if n % 6 == at:
                    yield step, m


def mla_tickets(step, n):
    lat = n % 6 < 4
    return {"proj": 4, "nsum": 2, "norm": 0, "rot": 1, "scores": 2 if lat else 1, "scale": 0, "turn": 2 if lat else 1, "out": 1}[step]


def ret_order():
    for m in range(8 * H_R + 2):
        if m < 8 * H_R:
            yield "rscore", m
        if m >= 2:
            yield "rval", m - 2


PLAN_TICKETS = [
    ("x_in", 12),
    ("vecs", 3),
    ("ada0", 24),
    ("norm_l0a", 2),
    ("ada1_0", 4),
    ("z_q", 4), ("z_kv", 2), ("z_kr", 2),
    ("norm_cq", 2), ("norm_ckv", 2),
    ("ada1_1", 4),
    ("v_tok", 6),
    *[(f"{step}{n}", mla_tickets(step, n)) for step, n in mla_order()],
    ("z_rq", 8), ("z_rk", 8), ("z_rv", 6), ("z_rg", 8),
    ("rrot", 8),
    *[t for step, m in ret_order() for t in ([(f"rscore{m}", 1)] if step == "rscore" else
                                             [(f"rout{m // 8}_{m % 8 // 6}", 1)] if m % 8 in (0, 6) else [])],
    ("rmean", 8), ("rvar", 8),
    ("w_out", 16),
    ("norm_l0b", 2),
    ("ada1_2", 4),
    ("s5_prm", 2), ("s5_c", 8),
    ("mlp0", 128),
    ("norm_l1a", 2),
    ("ada1_3", 4),
    ("s5_u0", 6), ("s5", 7 * 24), ("s5_end", 18),
    ("ada1_4", 4),
    ("glu", 16),
    ("norm_l1b", 1),
    ("ada1_5", 4),
    ("mlp1", 64),
    ("norm_mix", 1),
    ("qkv", 12), ("zg", 4), ("ab", 1), ("xr", 4), ("gate", 4),
    ("lru_r", 4), ("lru_i", 4),
    ("gnorm", 8),
    ("ktok", 4), ("vtok", 4),
    *[t for pair in range(2) for t in (
        [(f"gpre{tt}", 5) for tt in (2 * pair, 2 * pair + 1)]
        + [(f"inv{pair}_{lv}", 6) for lv in range(6)]
        + [(f"uw{tt}", 2) for tt in (2 * pair, 2 * pair + 1)])],
    ("gscan", 24),
    ("norm_o", 4),
    ("w_out2", 8),
    ("mem_in", 4), ("norm_mem", 1), ("xk", 4), ("xv", 4),
    ("norm_xat", 1), ("xq", 8),
    *[t for n in range(18) for t in ([(f"xscore{n}", 1)] * (n < 16) + [(f"xturn{n - 1}", 1)] * (1 <= n <= 16) + [(f"xout{n - 2}", 1)] * (n >= 2))],
    ("wo", 8),
    ("subk", 4), ("norm_ffn", 1),
    *[t for j in range(4) for t in ((f"pq{j}", 4), (f"psc{j}", 4))],
    ("htok", 8), ("ffn", 8),
]

PLAN_BLOCKS = [
    ("ada0", 12, lambda j: ("ada0", 8 * (j // 4) + ADA_ROW[j % 4])),
    ("ada1_0", 2, lambda j: ("ada1_0", j)),
    ("w_in0", 1, lambda j: ("z_kr", 1)),
    ("ada1_1", 2, lambda j: ("ada1_1", j)),
    ("uq", 1, lambda j: (f"proj{H_A - 1}", 1)),
    ("ukv", 1, lambda j: (f"proj{H_A - 1}", 3)),
    ("w_in_r", 4, lambda j: (("z_rq", "z_rk", "z_rv", "z_rg")[j], (7, 7, 5, 7)[j])),
    ("w_out", 2, lambda j: ("w_out", 8 * j + 7)),
    ("ada1_2", 2, lambda j: ("ada1_2", j)),
    ("mlp0", 16, lambda j: ("mlp0", 32 * (j // 4) + 8 * (j % 4) + 7)),
    ("ada1_3", 2, lambda j: ("ada1_3", j)),
    ("ada1_4", 2, lambda j: ("ada1_4", j)),
    ("glu", 4, lambda j: ("glu", 8 * (j // 2) + 7)),
    ("ada1_5", 2, lambda j: ("ada1_5", j)),
    ("mlp1", 16, lambda j: ("mlp1", 16 * (j // 4) + 4 * (j % 4) + 3)),
    ("w_in2", 4, lambda j: ("qkv", 4 * j + 3) if j < 3 else ("zg", 3)),
    ("w_ab", 1, lambda j: ("ab", 0)),
    ("w_xg", 2, lambda j: (("xr", 3), ("gate", 3))[j]),
    ("w_out2", 2, lambda j: ("w_out2", 4 * j + 3)),
    ("xkv", 4, lambda j: ("xk", 2 * j + 1) if j < 2 else ("xv", 2 * (j - 2) + 1)),
    ("xq", 2, lambda j: ("xq", 4 * j + 3)),
    ("wo", 2, lambda j: ("wo", 4 * j + 3)),
    ("peer_wq", 4, lambda j: (f"pq{j}", 3)),
]


def build(nc, I, consts, out):
    ctx = ExitStack()
    with ctx:
        def sb(name, shape, dt=F32):
            return ctx.enter_context(nc.sbuf_tensor(name, shape, dt))

        sems = {}

        def S(name):
            if name not in sems:
                sems[name] = ctx.enter_context(nc.semaphore(name))
            return sems[name]

        def cst(name, rows=slice(0, P)):
            a, w = CONST_COLS[name]
            return consts[rows, a:a + w]

        def bcast(ap, n):
            return ap.unsqueeze(len(ap.shape)).to_broadcast(list(ap.shape) + [n])

        ps = [ctx.enter_context(nc.psum_tensor(f"bank{b}", [P, 512], F32)) for b in range(NBANK)]
        ticket0 = {}
        _n = 0
        for _name, _count in PLAN_TICKETS:
            ticket0[_name] = _n
            _n += _count

        def claim(pe, t, extra=0):
            if t >= NBANK:
                pe.wait_ge(S(f"bank{t % NBANK}_free"), t // NBANK + extra)
            return ps[t % NBANK]

        def fill(ins, t):
            ins.then_inc(S(f"bank{t % NBANK}_full"), 1)

        def filled(eng, t, extra=0):
            eng.wait_ge(S(f"bank{t % NBANK}_full"), t // NBANK + 1 + extra)
            return ps[t % NBANK]

        def drained(ins, t):
            ins.then_inc(S(f"bank{t % NBANK}_free"), 1)

        def emptied(eng, t, extra=0):
            eng.wait_ge(S(f"bank{t % NBANK}_free"), t // NBANK + 1 + extra)

        ring = sb("ring", [P, NSLOT, SLOT])
        block0, last_use = {}, []
        for _name, _count, _uses in PLAN_BLOCKS:
            block0[_name] = len(last_use)
            for _j in range(_count):
                _t, _o = _uses(_j)
                last_use.append(ticket0[_t] + _o)

        def load_block(eng, b, src, extra=0):
            if b >= NSLOT:
                filled(eng, last_use[b - NSLOT], extra)
            n = 1
            for s in src.shape[1:]:
                n *= s
            dst = ring[0:src.shape[0], b % NSLOT, 0:n]
            if len(src.shape) == 3:
                dst = dst.rearrange("p (a b) -> p a b", a=src.shape[1])
            if len(src.shape) == 4:
                dst = dst.rearrange("p (a b c) -> p a b c", a=src.shape[1], b=src.shape[2])
            eng.dma_start(dst, src).then_inc(S(f"weights{b % NSLOT}"), 16)

        def block(pe, b, k, extra=0, n=None):
            pe.wait_ge(S(f"weights{b % NSLOT}"), 16 * (b // NSLOT + 1) + 16 * extra)
            n = n or SLOT // k
            return ring[:, b % NSLOT, 0:k * n].rearrange("p (k n) -> p k n", k=k)

        class Steps:

            def __init__(self, name):
                self.name, self.n, self.off = name, 0, 0

            def __call__(self, eng, ins):
                self.n += 1
                ins.then_inc(S(self.name), 1)
                eng.wait_ge(S(self.name), self.n + self.off)

            def loop(self, i, per):
                self.start, self.per, self.off = self.n, per, i * per

            def end_loop(self, times):
                assert self.n - self.start == self.per, (self.name, self.n - self.start, self.per)
                self.n, self.off = self.start + self.per * times, 0

        arena = sb("arena", [P, ARENA])

        def at(off, n, parts=slice(0, P)):
            assert off + n <= ARENA, (off, n)
            return arena[parts, off:off + n]

        xT = sb("xT", [P, KD, NT])
        hT = sb("hT", [P, KD, NT])
        ident = sb("ident", [P, P])
        ones = sb("ones", [P, P])
        blk64 = sb("blk64", [P, P])
        small = sb("small", [P, 16])
        eps_col, nhalf_pi = small[:, 0:1], small[:, 1:2]
        x_in = at(0, 6 * D).rearrange("p (t d) -> p t d", t=6)
        VEC_A = [("ada_b", I["ada_b"].rearrange("l (r c) -> (l r) c", c=P)),
                 ("norm1_g", I["norm1_g"].rearrange("l (r c) -> (l r) c", c=P)),
                 ("norm2_g", I["norm2_g"].rearrange("l (r c) -> (l r) c", c=P))]
        VEC_B = [("c", I["c"].rearrange("o (r c) -> (o r) c", c=P)),
                 ("c_ctx", I["c_ctx"].rearrange("(r c) -> r c", c=P))]
        VEC_B += [(n, I[n].rearrange("o (r c) -> (o r) c", c=P)) for n in (
            "mla_q_norm_g", "mla_kv_norm_g", "s5_d", "norm_mix_w_2", "norm_xattn_w_2", "norm_mem_w_2",
            "norm_ffn_w_2", "lru_conv_b_2", "lru_ba_2", "lru_bx_2", "lru_lambda_2", "gdn_norm_w_2")]
        VEC_B += [("lru_conv_w_2", I["lru_conv_w_2"].rearrange("o j (r c) -> (o j r) c", c=P))]
        VEC_C = [("conv_qkv_w_2", I["conv_qkv_w_2"].rearrange("o j (r c) -> (o j r) c", c=P))]
        col_of = {}
        vec_rows, vec_cols = [], []
        for _i, _vec in enumerate((VEC_A, VEC_B, VEC_C)):
            _n = sum(v.shape[0] for _, v in _vec)
            vec_rows.append((at(6 * D + _i * P, P), _vec, _n))
            vec_cols.append(sb(f"vec_cols{_i}", [P, _n]))
            _r = 0
            for _name, _v in _vec:
                col_of[_name] = (_i, _r)
                _r += _v.shape[0]

        def col(name, j=0, n=1):
            i, r = col_of[name]
            return vec_cols[i][:, r + j:r + j + n]

        ACT_VECS = [n for _, v, _ in vec_rows for n, _ in v][::2]
        SMALL_LOADS = sum(len(v) for _, v, _ in vec_rows) + 2 - len(ACT_VECS)
        dve_step, act_step, pool_step = Steps("dve_done"), Steps("act_done"), Steps("pool_done")
        silu_c = sb("silu_c", [P, KD, 2])
        modT = [sb(f"modT{l}", [P, 6 * KD, 2]) for l in range(2)]
        gain1 = [sb(f"gain1_{l}", [P, KD, 2]) for l in range(2)]
        gain2 = [sb(f"gain2_{l}", [P, KD, 2]) for l in range(2)]
        ada_rows = at(9984, 2 * 512, slice(0, 2)).rearrange("p (b n) -> p b n", b=2)
        ada1_rows = [at(o, 2 * 512, slice(0, 2)).rearrange("p (b n) -> p b n", b=2) for o in (0, 0, 0, 3840, 3840, 3840)]
        ada_w = [I["ada_w"][l].rearrange("(k p) n -> p k n", p=P) for l in range(2)]

        def ada1_load(sp, q):
            for j in range(2):
                load_block(sp, block0[f"ada1_{q}"] + j, ada_w[1][:, :, (2 * q + j) * 512:(2 * q + j + 1) * 512])

        def ada1_products(pe, q):
            t = ticket0[f"ada1_{q}"]
            for j in range(2):
                w = block(pe, block0[f"ada1_{q}"] + j, KD)
                bank = claim(pe, t + j)
                for k in range(KD):
                    last = pe.matmul(bank[0:2, :], silu_c[:, k, :], w[:, k, :], start=(k == 0), stop=(k == KD - 1))
                fill(last, t + j)
            for j in range(2):
                emptied(pe, t + j)
                bank = claim(pe, t + 2 + j)
                for m in range(4):
                    last = pe.transpose(bank[:, 2 * m:2 * m + 2], ada1_rows[q][:, j, m * P:(m + 1) * P], ident[0:2, 0:2])
                fill(last, t + 2 + j)

        def ada1_columns(dve, q):
            t = ticket0[f"ada1_{q}"]
            for j in range(2):
                bank = filled(dve, t + j)
                drained(dve.tensor_copy(ada1_rows[q][:, j, :], bank[0:2, :]), t + j)
            for j in range(2):
                bank = filled(dve, t + 2 + j)
                n = 8 * q + 4 * j
                drained(dve.tensor_tensor(modT[1][:, n:n + 4, :], bank[:, 0:8].rearrange("p (m s) -> p m s", s=2),
                                          bcast(col("ada_b", 6 * KD + n, 4), 2), ALU.add), t + 2 + j)
            for j in range(2):
                emptied(dve, t + 2 + j)

        def norm_gains(dve, l, gain, norm, at_):
            dve_step(dve, dve.tensor_scalar(gain[:, :, :], modT[l][:, at_ * KD:(at_ + 1) * KD, :], 1.0, None, ALU.add))
            dve_step(dve, dve.tensor_tensor(gain[:, :, :], gain[:, :, :], bcast(col(norm, KD * l, KD), 2), ALU.mult))
        rstd = sb("rstd", [P, NT])

        def norm_squares(act, tag, x, tbs, h, ready=None):
            n = tbs[-1][1]
            for k in range(KD):
                if ready:
                    ready(k)
                act.activation(h[:, k, 0:n], x[:, k, 0:n], ACT.Square).then_inc(S(f"{tag}_sq"), 1)

        def norm_sums(pe, tag, tbs, h, kd=KD, per=1):
            t0 = ticket0[f"norm_{tag}"]
            for b, (lo, hi) in enumerate(tbs):
                bank = claim(pe, t0 + b)
                for k in range(kd):
                    pe.wait_ge(S(f"{tag}_sq"), per * k + 1 + (b if per > 1 else 0))
                    last = pe.matmul(bank[:, 0:hi - lo], ones[:, :], h[:, k, lo:hi], start=(k == 0), stop=(k == kd - 1))
                fill(last, t0 + b)

        def norm_roots(act, tag, tbs, width=D, rs=rstd):
            t0 = ticket0[f"norm_{tag}"]
            for b, (lo, hi) in enumerate(tbs):
                bank = filled(act, t0 + b)
                drained(act.activation(rs[:, lo:hi], bank[:, 0:hi - lo], ACT.Sqrt, bias=eps_col, scale=1.0 / width), t0 + b)

        def rsqrt_start(act, bank, v, y, t, width, rows=slice(0, P)):
            act.activation(v, bank, ACT.Identity, bias=eps_col[rows], scale=1.0 / width)
            drained(act.activation(y, bank, ACT.Ln, bias=eps_col[rows], scale=1.0 / width), t)

        def rsqrt_guess(act, y, y2, ready):
            ins = act.activation(y, y, ACT.Exp, scale=-0.5)
            ins.then_inc(S(ready), 1)
            n = guesses[ready] = guesses.get(ready, 0) + 2
            act.wait_ge(S(ready), n - 1)
            act.activation(y2, y, ACT.Square).then_inc(S(ready), 1)

        guesses = {}

        def rsqrt_newton(dve, v, y, y2, ready, n):
            dve.wait_ge(S(ready), 2 * n + 2)
            dve_step(dve, dve.scalar_tensor_tensor(y2, y2, -0.5, v, ALU.mult, ALU.mult))
            dve_step(dve, dve.scalar_tensor_tensor(y, y2, 1.5, y, ALU.add, ALU.mult))

        def norm_scale(dve, tag, x, tbs, h, gain, kd=KD, rs=rstd):
            t0 = ticket0[f"norm_{tag}"]
            n = tbs[-1][1]
            for b in range(len(tbs)):
                emptied(dve, t0 + b)
            dve_step(dve, dve.reciprocal(rs[:, 0:n], rs[:, 0:n]))
            for k in range(kd):
                for s, (lo, hi) in enumerate(tbs):
                    last = dve.scalar_tensor_tensor(h[:, k, lo:hi], x[:, k, lo:hi], gain(k, s), rs[:, lo:hi],
                                                    ALU.mult, ALU.mult)
                    last.then_inc(S(f"{tag}_mul"), 1)

        def norm_shift(act, tag, tbs, h, shift):
            for k in range(KD):
                for s, (lo, hi) in enumerate(tbs):
                    act.wait_ge(S(f"{tag}_mul"), k * len(tbs) + s + 1)
                    act.activation(h[:, k, lo:hi], h[:, k, lo:hi], ACT.Identity, bias=shift(k, s))\
                       .then_inc(S(f"{tag}_ready"), 1)

        def shift_of(l, which):
            return lambda k, s: modT[l][:, which * KD + k, s:s + 1]
        mixT = at(0, 8 * NT).rearrange("p (k n) -> p k n", k=8)
        cqT = at(6144, 2 * NT).rearrange("p (k n) -> p k n", k=2)
        ckvT = at(7680, NT)
        sqs = at(8448, 2 * NT).rearrange("p (k n) -> p k n", k=2)
        krT = at(9984, NT)
        v_tok = at(10752, 6 * 512).rearrange("p (t c) -> p t c", t=6)
        qh = at(13824, 2 * NT).rearrange("p (b n) -> p b n", b=2)
        kh = at(15360, 2 * NT).rearrange("p (b n) -> p b n", b=2)
        prob = at(16896, 2 * NT).rearrange("p (b n) -> p b n", b=2)
        probT = at(18432, 2 * NT).rearrange("p (b t n) -> p b t n", b=2, t=6)
        cos_mla, sin_mla = at(19968, NL), at(20480, NL)
        rot_mla = at(20992, P)
        rope_tmp = at(21120, NL)
        rstd_qk = at(4 * NT, 2 * NT).rearrange("p (b n) -> p b n", b=2)
        var_qk = at(6 * NT, 2 * NT).rearrange("p (b n) -> p b n", b=2)
        prob_of = [prob[:, 0, :], prob[:, 1, :], at(21632, NT)]
        stat = sb("stat", [P, 3, 8])
        MLA_LOADS = 5
        KEYS = (slice(0, NL), slice(NL, NT))
        att_scale = QK ** -0.5
        HEADROWS = [slice(64 * (h % 2), 64 * (h % 2) + 64) for h in range(H_A)]
        rqT = at(6144, 4 * NT).rearrange("p (k n) -> p k n", k=4)
        rkT = at(9216, 4 * NT).rearrange("p (k n) -> p k n", k=4)
        rv = at(12288, 6 * 512).rearrange("p (t c) -> p t c", t=6)
        rgT = at(15360, 4 * NT).rearrange("p (k n) -> p k n", k=4)
        cos_ret, sin_ret = at(18432, NL), at(18944, NL)
        rot_ret = at(19456, P)
        decayed = at(19584, 4 * NL).rearrange("p (b n) -> p b n", b=4)
        h_flat = hT[:, :, :].rearrange("p k n -> p (k n)")
        ret_dist = h_flat[:, 0:896]
        decay_lat = [h_flat[:, 896 + 1536 * b:1792 + 1536 * b] for b in range(2)]
        decay_ctx = [h_flat[:, 1792 + 1536 * b:2432 + 1536 * b] for b in range(2)]
        decay_tmp = h_flat[:, 3968:4864]
        decay_ctx2 = h_flat[:, 4864:5504]
        lg = sb("lg", [P, 10, 2 * H_R])
        LG_RAW, LG_E, LG_U, LG_D, LG, LG_512, LG_256, LG_NEG = range(8)

        def ret_decay_slice(m):
            b, j = (m // 8) % 2, m % 8
            if j < 4:
                return decay_lat[b][:, 384 - P * j:384 - P * j + NL]
            if j < 6:
                return decay_ctx[b][:, P - P * (j - 4):P - P * (j - 4) + NL]
            return decay_lat[b][:, 384 - P * (j - 6):384 - P * (j - 6) + NC]
        MLP_Q = 4
        hid = at(0, 8 * NT).rearrange("p (m n) -> p m n", m=8)

        def mlp_loads(sp, l):
            w1 = I["mlp_w1"][l].rearrange("(k p) n -> p k n", p=P)
            w2 = I["mlp_w2"][l].rearrange("(k p) n -> p k n", p=P)

            def quarter(b0, q, extra):
                for j in range(2):
                    load_block(sp, b0 + j, w1[:, :, bass.ds(q * 1024 + j * 512, 512)], extra)
                for j in range(2):
                    load_block(sp, b0 + 2 + j, w2[:, bass.ds(q * 8, 8), j * 512:(j + 1) * 512], extra)

            quarter(block0[f"mlp{l}"], 0, 0)
            tickets = 16 * (2 if l == 0 else 1)
            with sp.Fori(0, MLP_Q - 1) as i:
                quarter(block0[f"mlp{l}"] + NSLOT, i + 1, i * (tickets // NBANK))

        def mlp_products(pe, l, tbs):
            nb = len(tbs)
            t0, uses, b0 = ticket0[f"mlp{l}"], 16 * nb // NBANK, block0[f"mlp{l}"]
            with pe.Fori(0, MLP_Q) as i:
                for part, x in enumerate((hT, hid)):
                    for j in range(2):
                        bi = b0 + 2 * part + j
                        pe.wait_ge(S(f"weights{bi % NSLOT}"), i * 16 + 16 * (bi // NSLOT + 1))
                        w = ring[:, bi % NSLOT, :].rearrange("p (k n) -> p k n", k=8)
                        for m in range(4):
                            for b, (lo, hi) in enumerate(tbs):
                                t = t0 + part * 8 * nb + (4 * j + m) * nb + b
                                bank = claim(pe, t, i * uses)
                                for k in range(8):
                                    if part == 1 and j == 0 and m == 0:
                                        pe.wait_ge(S(f"mlp{l}_hid"), i * (8 * nb) + k * nb + b + 1)
                                    last = pe.matmul(bank[:, 0:hi - lo], w[:, k, m * P:(m + 1) * P], x[:, k, lo:hi],
                                                     start=(k == 0), stop=(k == 7))
                                fill(last, t)

        def mlp_relu(act, l, tbs):
            nb = len(tbs)
            t0, uses = ticket0[f"mlp{l}"], 16 * nb // NBANK
            with act.Fori(0, MLP_Q) as i:
                for m in range(8):
                    for b, (lo, hi) in enumerate(tbs):
                        t = t0 + m * nb + b
                        bank = filled(act, t, i * uses)
                        drained(act.activation(hid[:, m, lo:hi], bank[:, 0:hi - lo], ACT.Relu), t)

        def mlp_square_and_add(dve, l, tbs):
            nb = len(tbs)
            t0, uses = ticket0[f"mlp{l}"], 16 * nb // NBANK
            with dve.Fori(0, MLP_Q) as i:
                for m in range(8):
                    for b, (lo, hi) in enumerate(tbs):
                        emptied(dve, t0 + m * nb + b, i * uses)
                        dve.tensor_tensor(hid[:, m, lo:hi], hid[:, m, lo:hi], hid[:, m, lo:hi], ALU.mult)\
                           .then_inc(S(f"mlp{l}_hid"), 1)
                for m in range(8):
                    for b, (lo, hi) in enumerate(tbs):
                        t = t0 + 8 * nb + m * nb + b
                        bank = filled(dve, t, i * uses)
                        drained(dve.scalar_tensor_tensor(xT[:, m, lo:hi], bank[:, 0:hi - lo], modT[l][:, 5 * KD + m, b:b + 1],
                                                         xT[:, m, lo:hi], ALU.mult, ALU.add), t)

        def tickets_emptied(eng, name, k, nb, first=0):
            for b in range(nb):
                emptied(eng, ticket0[name] + first + k * nb + b)
        NPR = 32
        NCH, LCH, CCH = NT // S5_CH, NL // S5_CH, NC // S5_CH
        DIRS = ("f", "b")
        _next = [0]
        def s5_buf(n):
            _next[0] += n
            return at(_next[0] - n, n)
        s5_hs = s5_buf(1024)
        s5_ytok = s5_hs
        s5_utok = s5_buf(1024)
        s5_un = s5_buf(8 * NCH).rearrange("p (g c) -> p g c", g=8)
        s5_FT = s5_buf(1024).rearrange("p (c r x) -> p c r x", c=2, r=4)
        s5_M = s5_buf(1024).rearrange("p (g x) -> p g x", g=8)
        s5_u = s5_buf(8 * LCH).rearrange("p (g c) -> p g c", g=8)
        s5_g = s5_buf(768).rearrange("p (c r n) -> p c r n", c=2, r=4)
        s5_w = s5_g
        assert _next[0] <= 8 * NT
        _next[0] = 8 * NT
        s5_b = s5_buf(2048).rearrange("p (d c r h) -> p d c r h", d=2, c=2, r=NPR)
        s5_c = s5_buf(2048).rearrange("p (d c r h) -> p d c r h", d=2, c=2, r=NPR)
        s5_pw = s5_buf(1152).rearrange("p (c d r k) -> p c d r k", c=2, d=2, r=NPR)
        s5_qp = s5_buf(896).rearrange("p (k c d r) -> p k c d r", k=7, c=2, d=2)
        s5_r8 = s5_buf(64).rearrange("p (d r) -> p d r", d=2)
        prm_at = _next[0]
        s5_prm = s5_buf(192).rearrange("p (d j r) -> p d j r", d=2, j=3)
        s5_qi = at(prm_at, 112).rearrange("p (k c d r) -> p k c d r", k=7, c=2, d=2)
        s5_mask = s5_buf(2 * P).rearrange("p (d x) -> p d x", d=2)
        rows_at = _next[0]
        s5_F = s5_buf(2048).rearrange("p (d c r x) -> p d c r x", d=2, c=2, r=4)
        s5_E = s5_buf(2048).rearrange("p (d c r x) -> p d c r x", d=2, c=2, r=4)
        prep_at = _next[0]
        s5_tab = s5_buf(1536).rearrange("p (c d r n) -> p c d r n", c=2, d=2, r=4)
        prm_rows_at = _next[0]
        s5_decay = s5_buf(768).rearrange("p (d r n) -> p d r n", d=2, r=4)
        prep_big_at = _next[0]
        s5_s = s5_buf(1024).rearrange("p (d c r n) -> p d c r n", d=2, c=2, r=4)
        s5_tmp = s5_buf(1024)
        s5_tmpP = s5_buf(1024)
        c_rows = at(rows_at, 4096).rearrange("p (a t x) -> p a t x", a=4, t=8)
        prep = at(prep_at, 24 * 64).rearrange("p (j d r) -> p j d r", j=24, d=2)
        prm_rows = at(prm_rows_at, 256).rearrange("p (d x) -> p d x", d=2)
        dt_rows = at(prm_rows_at + 256, 4, slice(64, 96)).rearrange("p (d x) -> p d x", d=2)
        prep_big = at(prep_big_at, 2048).rearrange("p (j r h) -> p j r h", j=4, r=NPR)
        S5_LOADS = 2 * (2 + 4 + 2) + 2
        glu_sig = at(0, 4 * NL).rearrange("p (b n) -> p b n", b=4)
        T_FT, T_FI, T_MM, T_U, T_UT, T_Y, T_YB = (0, 4), (2, 6), (8, 10), 12, 16, 18, 22

        def s5_t(i, n):
            if isinstance(i, int):
                return (ticket0["s5_end"] + (n - 6 if n >= T_Y else n), 0) if i == 7 else (ticket0["s5_u0"] + n - T_U, 0)
            return ticket0["s5"] + n, 3 * i

        def lead(ap, n):
            return ap.unsqueeze(2).to_broadcast([ap.shape[0], ap.shape[1], n, ap.shape[2]])
        def s5_output_side(eng, i, d, tmp, step, last=None):
            pr, pi = (bcast(s5_pw[:, c, d, bass.ds(i * 4, 4), slice(d, 8 + d)], 16) for c in range(2))
            cr, ci = (lead(s5_c[:, d, c, bass.ds(i * 4, 4), :], 8) for c in range(2))
            t1, t2, er, ei = (x.rearrange("p (r k h) -> p r k h", r=4, k=8) for x in (
                tmp[:, 0:512], tmp[:, 512:1024], s5_E[:, d, 0].rearrange("p r x -> p (r x)"), s5_E[:, d, 1].rearrange("p r x -> p (r x)")))
            if d == 1:
                er, ei = er[:, :, ::-1, :], ei[:, :, ::-1, :]
            for o, a, b, op in ((er, cr, ci, ALU.add), (ei, ci, cr, ALU.subtract)):
                for t, x, y in ((t1, pr, a), (t2, pi, b)):
                    if d == 0:
                        eng.nop(nofuse=True)
                    step(eng, eng.tensor_tensor(t, x, y, ALU.mult))
                ins = eng.tensor_tensor(o, t1, t2, op)
                if last and op == ALU.subtract:
                    ins.then_inc(S(last), 1)
                else:
                    step(eng, ins)
        TBL = TBS[:1]
        NTL = NL // P
        qkvT = at(0, 12 * NL).rearrange("p (m n) -> p m n", m=12)
        zT = at(6144, 4 * NL).rearrange("p (m n) -> p m n", m=4)
        k_tok = at(8192, 2048).rearrange("p (t h d) -> p t h d", t=4, h=4)
        u_tok = at(10240, 2048).rearrange("p (t h d) -> p t h d", t=4, h=4)
        mix2 = at(12288, 4096).rearrange("p (m n) -> p m n", m=8)
        xrT = at(16384, 2048).rearrange("p (m n) -> p m n", m=4)
        gateT = at(18432, 2048).rearrange("p (m n) -> p m n", m=4)
        lru_w = at(20480, 1024).rearrange("p (a m j) -> p a m j", a=2, m=4)
        lru_r, lru_i, lru_a, lru_th, lru_h = (h_flat[:, 512 * n:512 * n + 512] for n in range(5))
        inv_x = at(4096, 1024).rearrange("p (t h c) -> p t h c", t=2, h=4)
        inv_xt = at(5120, 1024).rearrange("p (t h c) -> p t h c", t=2, h=4)
        g_at = at(16384, 1024).rearrange("p (t h c) -> p t h c", t=2, h=4)
        inv_y = at(17408, 1024).rearrange("p (t h c) -> p t h c", t=2, h=4)
        attnT = at(18432, 2048).rearrange("p (t h c) -> p t h c", t=4, h=4)
        g_dec = at(20480, 1024).rearrange("p (t h c) -> p t h c", t=2, h=4)
        g_kbT = at(21504, 512).rearrange("p (h c) -> p h c", h=4)
        g_bc = at(22016, 512).rearrange("p (h c) -> p h c", h=4)
        g_masks = h_flat[:, 0:1026]
        tri_incl, g_suffix, g_ind = g_masks[:, 0:P], g_masks[:, P:2 * P], g_masks[:, 1024:1026]
        merge = [g_masks[:, 256 + P * lv:256 + P * (lv + 1)] for lv in range(6)]
        v_new = h_flat[:, 1028:1540]
        g_lvl = h_flat[:, 1540:2564].rearrange("p (t h c) -> p t h c", t=2, h=4)
        wT = h_flat[:, 2564:4612].rearrange("p (h n) -> p h n", h=4)
        g_kw = h_flat[:, 4612:5124].rearrange("p (h d) -> p h d", h=4)
        g_state = h_flat[:, 5124:5636].rearrange("p (h d) -> p h d", h=4)
        spare = h_flat[:, 7 * NT + NL:8 * NT]
        gt = spare[:, 0:160].rearrange("p (v t h) -> p v t h", v=10, t=4)
        G_A, G_B, G_E, G_U, G_LN, G_G, G_BETA, G_ABS, G_T, G_BE = range(10)
        qk_sq = at(8192, 4096).rearrange("p (m n) -> p m n", m=8)
        qk_rt = [at(12288, 2048).rearrange("p (m n) -> p m n", m=4)[:, m] if m < 4 else h_flat[:, 2564 + 512 * (m - 4):3076 + 512 * (m - 4)] for m in range(8)]
        qk_y2 = at(16384, 4096).rearrange("p (m n) -> p m n", m=8)
        o_var = at(18432, 2048).rearrange("p (m n) -> p m n", m=4)
        o_y2 = at(10240, 2048).rearrange("p (m n) -> p m n", m=4)
        o_rt = h_flat[:, 2564:4612].rearrange("p (m n) -> p m n", m=4)
        gs = spare[:, 160:224].rearrange("p (t c) -> p t c", t=4)
        gx = sb("gx", [P, 4, 16])
        gpar = sb("gpar", [P, 2, 4])
        lam = spare[:, 224:256].rearrange("p (v m) -> p v m", v=8)
        MIX2_LOADS = 6
        GHALF = (slice(0, GCH), slice(GCH, P))
        def bc4(ap):
            return ap.unsqueeze(1).to_broadcast([P, 4, ap.shape[1]])
        def bc24(ap):
            return ap.unsqueeze(1).to_broadcast([P, 8, ap.shape[1]])
        def pair8(ap):
            return ap.rearrange("p t h c -> p (t h) c")
        mem_in = at(0, 2 * D).rearrange("p (t d) -> p t d", t=2)
        memT = at(2048, KD * MEM).rearrange("p (k n) -> p k n", k=KD)
        mem_h = at(4096, KD * MEM).rearrange("p (k n) -> p k n", k=KD)
        xqT = at(6144, KD * NL).rearrange("p (k n) -> p k n", k=KD)
        xkT = at(10240, KD * MEM).rearrange("p (k n) -> p k n", k=KD)
        xoT = at(12288, KD * NL).rearrange("p (k n) -> p k n", k=KD)
        xv_tok = at(16384, 2 * D).rearrange("p (t d) -> p t d", t=2)
        xprob = at(18432, 2 * MEM).rearrange("p (b n) -> p b n", b=2)
        xprobT = at(18944, 2 * MEM).rearrange("p (b t n) -> p b t n", b=2, t=2)
        rstd_mem = at(19456, MEM)
        TBM = ((0, MEM),)
        XDH = D // XA_H
        xat_scale = XDH ** -0.5
        XAT_ORDER = [(s, n - o) for n in range(18) for o, s in enumerate(("xscore", "xturn", "xout")) if 0 <= n - o < 16]
        NVEC = 2 * PH
        h_tok = at(0, NTL * D).rearrange("p (t d) -> p t d", t=NTL)
        pqT = at(4096, 4096).rearrange("p (b v n) -> p b v n", b=2, v=4)
        subT = at(8192, NVEC * P).rearrange("p (v n) -> p v n", v=NVEC)
        sub_rows = at(10240, NVEC * P).rearrange("p (v d) -> p v d", v=NVEC)
        psc = at(12288, 1024).rearrange("p (b v n) -> p b v n", b=2, v=4)
        s_top = at(13312, 64).rearrange("p (h s k) -> p h s k", h=2, s=2)
        i_top = at(13376, 64).bitcast(U32).rearrange("p (h s k) -> p h s k", h=2, s=2)
        i_f = at(21776, 128).rearrange("p (b h s k) -> p b h s k", b=2, h=2, s=2)
        cand = at(13504, 512).rearrange("p (h c) -> p h c", h=2)
        pos_u = at(14016, 32).bitcast(U32).rearrange("p (h k) -> p h k", h=2)
        pos_f, pos_r = (at(14048 + 32 * n, 32).rearrange("p (h k) -> p h k", h=2) for n in range(2))
        pos_half = at(21904, 128).rearrange("p (b s h k) -> p b s h k", b=2, s=2, h=2)
        onehot = [at(o, 1024).rearrange("p (s h k j) -> p s h k j", s=2, h=2, k=PTOPK) for o in (14176, 17904)]
        e_half = at(15200, 64).rearrange("p (s h k) -> p s h k", s=2, h=2)
        best = at(15264, 512).rearrange("p (t h k) -> p t h k", t=NTL, h=PH)
        idxs = at(15776, 512).bitcast(U32).rearrange("p (t e) -> p t e", t=NTL)
        gate = at(16288, 512).rearrange("p (t e) -> p t e", t=NTL)
        gate_sum = at(16800, 32)
        iota16 = at(16832, 16)
        dots, gelus, acts = (at(16848 + 8 * n, 8) for n in range(3))
        fin = at(16872, 8)
        wide_ident = at(4096, 7 * P)
        idx_now = [at(21760 + 8 * n, 8).bitcast(U32) for n in range(2)]
        diag = at(16880, 1024).rearrange("p (s n) -> p s n", s=8)
        sq_junk = at(17904, D)
        w_final, out_tile = at(19712, D), at(20736, D)
        ERING = 8
        u_row = [ring[:, s // 4, s % 4 * D:(s % 4 + 1) * D] for s in range(ERING)]
        v_row = [ring[:, 2 + s // 4, s % 4 * D:(s % 4 + 1) * D] for s in range(ERING)]
        EXPERTS = PH * PTOPK
        EGROUPS = EXPERTS // ERING
        UNITS = [(j, t) for j in range(4) for t in range(NTL)]

        block_ = ctx.enter_context(nc.Block())

        @block_.sync
        def _(sp):
            sp.dma_start(ident[:, :], cst("ident")).then_inc(S("x_landed"), 16)
            for t in range(6):
                src = I["x"][0, t * P:(t + 1) * P, :] if t < 4 else I["ctx"][0, (t - 4) * P:(t - 3) * P, :]
                sp.dma_start(x_in[:, t, :], src).then_inc(S("x_landed"), 16)
            sp.wait_ge(S("small_landed"), 16 * SMALL_LOADS)
            sp.wait_ge(S("vecs_landed"), 16 * len(ACT_VECS))
            for s in range(NSLOT):
                load_block(sp, block0["ada0"] + s, ada_w[0][:, :, s * 512:(s + 1) * 512])
            with sp.Fori(0, 2) as i:
                for s in range(NSLOT):
                    load_block(sp, block0["ada0"] + NSLOT + s, ada_w[0][:, :, bass.ds((i + 1) * (NSLOT * 512) + s * 512, 512)],
                               extra=i)
            ada1_load(sp, 0)
            load_block(sp, block0["w_in0"], I["w_in"][0].rearrange("(k p) n -> p k n", p=P)[:, :, 0:MLA_IN])
            ada1_load(sp, 1)
            load_block(sp, block0["uq"], I["mla_w_uq"][0].rearrange("(k p) n -> p k n", p=P))
            load_block(sp, block0["ukv"], I["mla_w_ukv"][0])
            w_in_v = I["w_in"][0].rearrange("(k p) n -> p k n", p=P)
            for j in range(4):
                load_block(sp, block0["w_in_r"] + j, w_in_v[:, :, MLA_IN + j * RET_W:MLA_IN + (j + 1) * RET_W])
            for j in range(2):
                load_block(sp, block0["w_out"] + j, I["w_out"][0].rearrange("(k p) n -> p k n", p=P)[:, :, j * 512:(j + 1) * 512])
            ada1_load(sp, 2)
            mlp_loads(sp, 0)
            ada1_load(sp, 3)
            ada1_load(sp, 4)
            for j in range(4):
                load_block(sp, block0["glu"] + j, I["s5_w_glu"][0].rearrange("(k p) n -> p k n", p=P)[
                    :, :, D * (j % 2) + 512 * (j // 2):D * (j % 2) + 512 * (j // 2) + 512])
            ada1_load(sp, 5)
            mlp_loads(sp, 1)
            w_in2 = I["w_in_2"][0].rearrange("(k p) n -> p k n", p=P)
            for j in range(4):
                load_block(sp, block0["w_in2"] + j, w_in2[:, :, j * 512:(j + 1) * 512])
            load_block(sp, block0["w_ab"], w_in2[:, :, 2048:2056])
            for j in range(2):
                load_block(sp, block0["w_xg"] + j, w_in2[:, :, 2056 + j * 512:2568 + j * 512])
            for j in range(2):
                load_block(sp, block0["w_out2"] + j, I["w_out_2"][0].rearrange("(k p) n -> p k n", p=P)[:, :, j * 512:(j + 1) * 512])
            filled(sp, ticket0["norm_o"] + 3)
            for t in range(2):
                sp.dma_start(mem_in[:, t, :], I["mem_2"][0, t * P:(t + 1) * P, :]).then_inc(S("mem_landed"), 16)
            wkv = I["xattn_wkv_2"][0].rearrange("(k p) n -> p k n", p=P)
            for j in range(4):
                load_block(sp, block0["xkv"] + j, wkv[:, :, j * 512:(j + 1) * 512])
            for name, src in (("xq", "xattn_wq_2"), ("wo", "xattn_wo_2")):
                for j in range(2):
                    load_block(sp, block0[name] + j, I[src][0].rearrange("(k p) n -> p k n", p=P)[:, :, j * 512:(j + 1) * 512])
            filled(sp, ticket0["xscore15"])
            for dst, src in ((sub_rows, I["peer_subkeys_2"][0].rearrange("h s k d -> k (h s) d")), (iota16, cst("iota16")),
                             (w_final, I["norm_final_w_2"].partition_broadcast(P))):
                sp.dma_start(dst, src).then_inc(S("peer_landed"), 16)
            for j in range(4):
                load_block(sp, block0["peer_wq"] + j, I["peer_wq_2"][0].rearrange("(k p) n -> p k n", p=P)[:, :, j * 512:(j + 1) * 512])
            for T_ in range(NTL):
                sp.wait_ge(S("out_ready"), T_ + 1)
                sp.dma_start(out[0, T_ * P:(T_ + 1) * P, :], out_tile).then_inc(S("out_done"), 16)
            sp.wait_ge(S("out_done"), 16 * NTL)

        @block_.gpsimd
        def _(pool):
            for tile, name in ((ones, "ones"), (blk64, "blk64")):
                pool.dma_start(tile[:, :], cst(name)).then_inc(S("small_landed"), 16)
            for tile, vec, _ in vec_rows:
                r = 0
                for name, v in vec:
                    if name not in ACT_VECS:
                        pool.dma_start(tile[r:r + v.shape[0], :], v).then_inc(S("small_landed"), 16)
                    r += v.shape[0]
            for n in range(12):
                emptied(pool, ticket0["x_in"] + n)
            for i in range(3):
                emptied(pool, ticket0["vecs"] + i)
            for tile, name in ((cos_mla, "cos_mla"), (sin_mla, "sin_mla"), (rot_mla, "rot_mla")):
                pool.dma_start(tile, cst(name)).then_inc(S("mla_tables"), 16)
            for j, name in ((2, "mla_qn_g"), (3, "mla_kn_g")):
                pool.dma_start(small[0:QK, j:j + 1], I[name].rearrange("o q -> q o")).then_inc(S("mla_tables"), 16)
            for j, name in enumerate(("ret_lg_f", "ret_lg_b")):
                pool.dma_start(lg[:, LG_RAW, j * H_R:(j + 1) * H_R], I[name][0].partition_broadcast(P)).then_inc(S("lg_landed"), 16)
            emptied(pool, ticket0[f"out{6 * H_A - 1}"])
            emptied(pool, ticket0["z_rq"])
            for tile, name in ((cos_ret, "cos_ret"), (sin_ret, "sin_ret"), (rot_ret, "rot_ret")):
                pool.dma_start(tile, cst(name)).then_inc(S("ret_tables"), 16)
            for j in range(8):
                filled(pool, ticket0["z_rg"] + j)
            pool.dma_start(ret_dist, cst("ret_dist")).then_inc(S("dist_landed"), 16)
            for b in range(2):
                filled(pool, ticket0["w_out"] + b)
            for d, x in enumerate(DIRS):
                for c, part in enumerate(("re", "im")):
                    pool.dma_start(s5_b[:, d, c], I[f"s5_b_{part}_{x}"][0].rearrange("(r two) p h -> (two p) r h", two=2))\
                        .then_inc(S("s5_landed"), 16)
                    for half in range(2):
                        pool.dma_start(c_rows[:, 2 * d + c, :, 64 * half:64 * half + 64],
                                       I[f"s5_c_{part}_{x}"][0].rearrange("(t g) h p -> (g h) t p", t=8)).then_inc(S("s5_landed"), 16)
                for j, part in enumerate(("re", "im")):
                    pool.dma_start(prm_rows[32 * j:32 * j + 32, d, :], I[f"s5_a_{part}_{x}"][0].rearrange("(r two) p -> r (two p)", two=2))\
                        .then_inc(S("s5_landed"), 16)
                pool.dma_start(dt_rows[:, d, :], I[f"s5_log_dt_{x}"][0].rearrange("(r two) -> r two", two=2)).then_inc(S("s5_dt"), 16)
            for d, x in enumerate(("s5_fwd", "s5_bwd")):
                pool.dma_start(s5_mask[:, d, :], cst(x)[:, 0:P]).then_inc(S("s5_landed"), 16)
            pool.wait_ge(S("s5_dt"), 32)
            for d in range(2):
                pool.tensor_copy(prm_rows[64:96, d, :].rearrange("r (two p) -> r two p", two=2), bcast(dt_rows[:, d, :], 64)).then_inc(S("s5_dt_rows"), 1)
            pool.wait_ge(S("s5_prep"), 1)
            pool_step(pool, pool.memset(s5_tab[:, 0, :, :, 0:1], 1.0))
            pool_step(pool, pool.memset(s5_tab[:, 1, :, :, 0:1], 0.0))
            pool_step(pool, pool.memset(s5_decay[:, :, :, NCH - 1:NCH], 0.0))
            with pool.Fori(0, 8) as i:
                pool_step.loop(i, 1 + 7 * 6 + 6)
                pool.wait_ge(S("s5_turned"), 2 * i + 1)
                pool.nop(nofuse=True)
                pool_step(pool, pool.tensor_copy(s5_qi, s5_qp[:, :, :, :, bass.ds(i * 4, 4)]))
                pool.nop(nofuse=True)
                for d in range(2):
                    pool.tensor_copy(s5_decay[:, d, :, 0:NCH - 1], bcast(s5_r8[:, d, bass.ds(i * 4, 4)], NCH - 1)).then_inc(S("s5_decays"), 1)
                for k in range(7):
                    n = min(1 << k, NCH - (1 << k))
                    lo, hi = slice(0, n), slice(1 << k, (1 << k) + n)
                    re, im = s5_tab[:, 0], s5_tab[:, 1]
                    qr, qi = (bcast(s5_qi[:, k, c], n) for c in range(2))
                    t1 = s5_tmpP[:, 0:8 * n].rearrange("p (d r n) -> p d r n", d=2, r=4)
                    t2 = s5_tmpP[:, 512:512 + 8 * n].rearrange("p (d r n) -> p d r n", d=2, r=4)
                    pool_step(pool, pool.tensor_tensor(t1, re[:, :, :, lo], qr, ALU.mult))
                    pool_step(pool, pool.tensor_tensor(t2, im[:, :, :, lo], qi, ALU.mult))
                    pool_step(pool, pool.tensor_tensor(re[:, :, :, hi], t1, t2, ALU.subtract))
                    pool_step(pool, pool.tensor_tensor(t1, re[:, :, :, lo], qi, ALU.mult))
                    pool_step(pool, pool.tensor_tensor(t2, im[:, :, :, lo], qr, ALU.mult))
                    ins = pool.tensor_tensor(im[:, :, :, hi], t1, t2, ALU.add)
                    pool_step(pool, ins)
                filled(pool, ticket0["s5"] + T_Y + 3, (i - 1) * 3)
                s5_output_side(pool, i, 0, s5_tmpP, pool_step)
                pool_step.end_loop(8)
            pool.dma_start(gpar[:, 0, :], I["gdn_a_log_2"][0].partition_broadcast(P)).then_inc(S("mix2_landed"), 16)
            pool.dma_start(gpar[:, 1, :], I["gdn_dt_bias_2"][0].partition_broadcast(P)).then_inc(S("mix2_landed"), 16)
            for n in range(8):
                emptied(pool, ticket0["mlp1"] + 56 + n)
            pool_step(pool, pool.memset(lru_w[:, :, :, :], 0.0))
            for a, name in enumerate(("lru_wa_2", "lru_wx_2")):
                for b in range(2):
                    pool.dma_start(lru_w[64 * b:64 * b + 64, a, :, 64 * b:64 * b + 64],
                                   I[name][0].rearrange("(c two) i j -> two i c j", two=2)[b]).then_inc(S("mix2_landed"), 16)
            pool.wait_ge(S("lru_done"), 4)
            for j, name in enumerate(["tri_incl", "suffix"] + [f"merge{lv}" for lv in range(6)] + ["chunk_ind"]):
                pool.dma_start(g_masks[:, P * j:P * j + CONST_COLS[name][1]], cst(name)).then_inc(S("g_masks"), 16)
            pool.wait_ge(S("peer_landed"), 16 * 3)
            for u, (j, t) in enumerate(UNITS):
                pool.wait_ge(S("onehot_ready"), u + 1)
                for s in range(2):
                    for h in range(2):
                        one = onehot[u % 2][:, s, h]
                        last = pool.tensor_tensor(one, one, i_f[:, u % 2, h, s, :].unsqueeze(1).to_broadcast([P, PTOPK, PTOPK]), ALU.mult)
                pool_step(pool, last)
                rows = onehot[u % 2].rearrange("p s h k j -> p (s h k) j")
                for n in (8, 4, 2):
                    pool_step(pool, pool.tensor_tensor(rows[:, :, 0:n], rows[:, :, 0:n], rows[:, :, n:2 * n], ALU.add))
                pool_step(pool, pool.tensor_tensor(e_half.rearrange("p s h k -> p (s h k)"), rows[:, :, 0], rows[:, :, 1], ALU.add))
                pool_step(pool, pool.tensor_scalar(e_half[:, 0], e_half[:, 0], float(PNK), None, ALU.mult))
                pool_step(pool, pool.tensor_tensor(e_half[:, 0], e_half[:, 0], e_half[:, 1], ALU.add))
                pool.tensor_copy(idxs[:, t, 32 * j:32 * j + 32].rearrange("p (h k) -> p h k", h=2), e_half[:, 0]).then_inc(S("peer_idx"), 1)
                if u + 1 < len(UNITS):
                    pool.wait_ge(S("peer_idx"), u + 1)
            filled(pool, ticket0["pq3"] + 3)
            for T_ in range(NTL):
                pool.wait_ge(S("peer_idx"), len(UNITS) - NTL + T_ + 1)
                with pool.Fori(0, EGROUPS // 2) as i:
                    pool_step.loop(i, 2)
                    for half in range(2):
                        pool_step(pool, pool.tensor_copy(idx_now[half], idxs[:, T_, bass.ds(i * (2 * ERING) + half * ERING, ERING)]))
                        for rows, table, used, landed in ((u_row, "peer_u_2", "u_used", "u_landed"), (v_row, "peer_v_2", "v_used", "v_landed")):
                            for s in range(ERING):
                                pool.wait_ge(S(used), i * (2 * ERING) + T_ * EXPERTS + half * ERING + s + 1)
                                pool.nop(nofuse=True)
                                pool.indirect_dma_start(rows[s], None, I[table][0], bass.IndirectOffsetOnAxis(idx_now[half][:, s:s + 1], 0))\
                                    .then_inc(S(f"{landed}{s}"), 16)
                    pool_step.end_loop(EGROUPS // 2)

        @block_.scalar
        def _(act):
            for tile, vec, _ in vec_rows:
                r = 0
                for name, v in vec:
                    if name in ACT_VECS:
                        act.dma_start(tile[r:r + v.shape[0], :], v).then_inc(S("vecs_landed"), 16)
                    r += v.shape[0]
            for n in range(1, 12, 2):
                t, g = n // 2, n % 2
                bank = filled(act, ticket0["x_in"] + n)
                drained(act.activation(xT[:, 4 * g:4 * g + 4, t * P:(t + 1) * P],
                                       bank[:, :].rearrange("p (k n) -> p k n", k=4), ACT.Copy), ticket0["x_in"] + n)
            for i in range(3):
                emptied(act, ticket0["vecs"] + i)
            for s, name in enumerate(("c", "c_ctx")):
                act_step(act, act.activation(silu_c[:, :, s], col(name, 0, KD), ACT.Silu))
            for n in range(12):
                emptied(act, ticket0["x_in"] + n)
            norm_squares(act, "l0a", xT, TBS, hT)
            with act.Fori(0, 3) as i:
                for s in range(NSLOT):
                    t = ticket0["ada0"] + ADA_ROW[s]
                    bank = filled(act, t, i)
                    if s >= 2:
                        filled(act, ticket0["ada0"] + ADA_COL[s - 2], i)
                    drained(act.activation(ada_rows[:, s % 2, :], bank[0:2, :], ACT.Copy), t)
            norm_roots(act, "l0a", TBS)
            norm_shift(act, "l0a", TBS, hT, shift_of(0, 0))
            for m in range(4):
                for b, (lo, hi) in enumerate(TBS):
                    t = ticket0["z_q"] + 2 * m + b
                    bank = filled(act, t)
                    if m < 3:
                        sq, raw = (sqs[:, m, lo:hi], cqT[:, m, lo:hi]) if m < 2 else (prob[:, 0, lo:hi], ckvT[:, lo:hi])
                        act.activation(sq, bank[:, 0:hi - lo], ACT.Square).then_inc(S("cq_sq" if m < 2 else "ckv_sq"), 1)
                        drained(act.activation(raw, bank[:, 0:hi - lo], ACT.Copy), t)
                    else:
                        drained(act.activation(krT[NOPE:QK, lo:hi], bank[NOPE:QK, 0:hi - lo], ACT.Copy), t)
            norm_roots(act, "cq", TBS, Q_LORA)
            norm_roots(act, "ckv", TBS, KV_LORA, rs=rstd_qk[:, 0, :])
            for t in range(1, 6, 2):
                bank = filled(act, ticket0["v_tok"] + t)
                drained(act.activation(v_tok[:, t, :], bank[:, :], ACT.Copy), ticket0["v_tok"] + t)
            for step, n in mla_order():
                t0 = ticket0[f"{step}{n}"]
                if step == "proj":
                    if n >= 1:
                        act.wait_ge(S("qk_normed"), 4 * n)
                    for b, (lo, hi) in enumerate(TBS):
                        bank = filled(act, t0 + b)
                        act.activation(qh[0:QK, n % 2, lo:hi], bank[0:QK, 0:hi - lo], ACT.Copy).then_inc(S("q_raw"), 1)
                        drained(act.activation(sqs[0:QK, 0, lo:hi], bank[0:QK, 0:hi - lo], ACT.Square), t0 + b)
                    for b, (lo, hi) in enumerate(TBS):
                        bank = filled(act, t0 + 2 + b)
                        act.activation(sqs[0:NOPE, 1, lo:hi], bank[0:NOPE, 0:hi - lo], ACT.Square)
                        drained(act.activation(kh[0:NOPE, n % 2, lo:hi], bank[0:NOPE, 0:hi - lo], ACT.Copy), t0 + 2 + b)
                    act_step(act, act.activation(kh[NOPE:QK, n % 2, :], krT[NOPE:QK, :], ACT.Copy))
                    act.activation(sqs[NOPE:QK, 1, :], krT[NOPE:QK, :], ACT.Square).then_inc(S("qk_sq"), 1)
                elif step == "nsum":
                    j = n % 2
                    for b, (lo, hi) in enumerate(TBS):
                        bank = filled(act, t0 + b)
                        rsqrt_start(act, bank[0:QK, 0:hi - lo], var_qk[0:QK, j, lo:hi], rstd_qk[0:QK, j, lo:hi], t0 + b, QK, slice(0, QK))
                    if j == 1:
                        for jj in range(2):
                            for b in range(2):
                                emptied(act, ticket0[f"nsum{n - 1 + jj}"] + b)
                            rsqrt_guess(act, rstd_qk[0:QK, jj, :], sqs[0:QK, jj, :], "qk_guess")
                elif step == "scores":
                    act.wait_ge(S("score_max"), n + 1)
                    for b, keys in enumerate(KEYS if n % 6 < 4 else KEYS[1:]):
                        bank = filled(act, t0 + b)
                        drained(act.activation(prob_of[n % 3][:, keys], bank[:, 0:keys.stop - keys.start], ACT.Exp,
                                               bias=stat[:, n % 3, 3:4], scale=att_scale,
                                               accum_out=stat[:, n % 3, 4 + b:5 + b]), t0 + b)
                elif step == "turn":
                    b = mla_tickets("turn", n) - 1
                    bank = filled(act, t0 + b)
                    drained(act.activation(probT[:, n % 2, 4:6, :], bank[:, 0:2 * P].rearrange("p (t n) -> p t n", t=2), ACT.Copy),
                            t0 + b)
            for name, x, scale in (("z_rq", rqT, 1.0), ("z_rk", rkT, DK_R ** -0.5)):
                for m in range(4):
                    for b, (lo, hi) in enumerate(TBS):
                        t = ticket0[name] + 2 * m + b
                        bank = filled(act, t)
                        drained(act.activation(x[:, m, lo:hi], bank[:, 0:hi - lo], ACT.Copy, scale=scale), t)
            for m in range(4):
                for b, (lo, hi) in enumerate(TBS):
                    t = ticket0["z_rg"] + 2 * m + b
                    bank = filled(act, t)
                    drained(act.activation(rgT[:, m, lo:hi], bank[:, 0:hi - lo], ACT.Silu), t)
            act.wait_ge(S("lg_landed"), 32)
            act.activation(lg[:, LG_E, :], lg[:, LG_RAW, :], ACT.Exp, scale=float(np.log(2.0))).then_inc(S("lg_exp"), 1)
            act.wait_ge(S("lg_u"), 1)
            act.activation(lg[:, LG, :], lg[:, LG_U, :], ACT.Ln).then_inc(S("lg_ln"), 1)
            act.wait_ge(S("dist_landed"), 16)
            act.wait_ge(S("lg_ready"), 1)
            for step, m in ret_order():
                h, j = m // 8, m % 8
                if step == "rscore" and j == 0:
                    for sc, of, dst in ((LG, LG_512, decay_ctx[h % 2]), (LG_NEG, LG_256, None)):
                        d = h if sc == LG else H_R + h
                        if h >= 2:
                            emptied(act, ticket0[f"rscore{8 * (h - 1) - 1}"])
                        if dst is None:
                            dst = decay_ctx2
                            if h >= 1:
                                act.wait_ge(S("decay_ready"), h)
                        act.activation(dst, ret_dist[:, 0:640], ACT.Exp, bias=lg[:, of, d:d + 1],
                                       scale=lg[:, sc, d:d + 1]).then_inc(S("decay_exp"), 1)
                    act.wait_ge(S("decay_arg"), h + 1)
                    act.activation(decay_lat[h % 2], decay_tmp, ACT.Exp).then_inc(S("decay_exp"), 1)
                elif step == "rval" and j in (5, 7):
                    t = ticket0[f"rout{h}_{j // 6}"]
                    bank = filled(act, t)
                    q = slice(0, NL) if j == 5 else KEYS[1]
                    drained(act.activation(mixT[HEADROWS[h], 4 + h // 2, q], bank[HEADROWS[h], 0:q.stop - q.start], ACT.Copy), t)
            for c in range(4):
                for b, (lo, hi) in enumerate(TBS):
                    emptied(act, ticket0["rmean"] + 2 * c + b)
                    act.activation(rqT[:, c, lo:hi], mixT[:, 4 + c, lo:hi], ACT.Square).then_inc(S("ret_sq"), 1)
            for c in range(4):
                for b, (lo, hi) in enumerate(TBS):
                    t = ticket0["rvar"] + 2 * c + b
                    bank = filled(act, t)
                    rsqrt_start(act, bank[:, 0:hi - lo], rqT[:, c, lo:hi], rkT[:, c, lo:hi], t, 1)
            for c in range(4):
                for b, (lo, hi) in enumerate(TBS):
                    emptied(act, ticket0["rvar"] + 2 * c + b)
                    if c >= 2:
                        act.wait_ge(S("ret_gated"), 2 * (c - 2) + b + 1)
                    rsqrt_guess(act, rkT[:, c, lo:hi], decayed[:, 2 * (c % 2) + b, 0:hi - lo], "ret_guess")
            norm_squares(act, "l0b", xT, TBS, hT, lambda k: tickets_emptied(act, "w_out", k, 2))
            norm_roots(act, "l0b", TBS)
            norm_shift(act, "l0b", TBS, hT, shift_of(0, 3))
            for n in range(8):
                a, half = n // 2, n % 2
                t = ticket0["s5_c"] + n
                bank = filled(act, t)
                for par in range(2):
                    rows = slice(64 * par, 64 * par + 64)
                    ins = act.activation(s5_c[rows, a // 2, a % 2, 16 * half:16 * half + 16, :],
                                         bank[rows, :].rearrange("p (r two h) -> p r two h", r=16, two=2)[:, :, par, :],
                                         ACT.Copy, scale=1.0 - 2.0 * (a % 2))
                drained(ins, t)
            act.wait_ge(S("s5_prm_ready"), 1)
            act.activation(prep[:, 0], s5_prm[:, :, 2, :], ACT.Exp).then_inc(S("s5_act"), 1)
            act.wait_ge(S("s5_args"), 1)
            act.activation(prep[:, 4], prep[:, 1], ACT.Exp).then_inc(S("s5_act"), 1)
            act.activation(prep[:, 5], prep[:, 1], ACT.Exp, scale=-1.0).then_inc(S("s5_act"), 1)
            act.activation(s5_r8, prep[:, 1], ACT.Exp, scale=float(S5_CH)).then_inc(S("s5_act"), 1)
            act.activation(prep[:, 6], prep[:, 2], ACT.Sin).then_inc(S("s5_act"), 1)
            act.activation(prep[:, 7], prep[:, 3], ACT.Sin).then_inc(S("s5_act"), 1)
            mlp_relu(act, 0, TBS)
            norm_squares(act, "l1a", xT, TBS, hT, lambda k: tickets_emptied(act, "mlp0", k, 2, 112))
            norm_roots(act, "l1a", TBS)
            norm_shift(act, "l1a", TBS, hT, shift_of(1, 0))
            def s5_tokens(i, at_):
                act.activation(s5_hs[:, 0:NT], hT[:, bass.ds(i, 1), :].squeeze(1), ACT.Copy).then_inc(S("s5_hs"), 1)
                ut = s5_utok.rearrange("p (g t h) -> p t g h", g=8, t=8)
                for n in range(4):
                    t, x = s5_t(at_, T_U + n)
                    bank = filled(act, t, x)
                    for j in range(2):
                        ins = act.activation(ut[0:NCH, 2 * n + j], bank[0:NCH, j * P:(j + 1) * P].rearrange("p (g h) -> p g h", g=8), ACT.Copy)
                    drained(ins, t)
                for n in range(2):
                    t, x = s5_t(at_, T_UT + n)
                    bank = filled(act, t, x)[:, 0:4 * NCH].rearrange("p (g c) -> p g c", g=4)
                    act.activation(s5_un[:, 4 * n:4 * n + 4, CCH:NCH], bank[:, :, 0:LCH], ACT.Copy)
                    drained(act.activation(s5_un[:, 4 * n:4 * n + 4, 0:CCH], bank[:, :, LCH:NCH], ACT.Copy), t)

            def s5_token_copy(at_):
                for n in range(2):
                    emptied(act, *s5_t(at_, T_UT + n))
                act.activation(s5_u[:, :, :], s5_un[:, :, CCH:NCH], ACT.Copy).then_inc(S("s5_ucopy"), 1)

            def s5_turn_F(i):
                for d in range(2):
                    for c in range(2):
                        t, x = s5_t(i, T_FT[d] + c)
                        bank = filled(act, t, x)
                        drained(act.activation(s5_FT[:, c], bank[:, :].rearrange("p (r x) -> p r x", r=4), ACT.Copy), t)

            def s5_evict_y(i):
                yt = s5_ytok.rearrange("p (t g h) -> p g t h", t=8, g=8)
                for n in range(4):
                    t, x = s5_t(i, T_Y + n)
                    bank = filled(act, t, x)
                    for j in range(2):
                        ins = act.activation(yt[0:LCH, 2 * (2 * (n // 2) + j) + n % 2], bank[0:LCH, j * P:(j + 1) * P].rearrange("p (t h) -> p t h", t=8), ACT.Copy)
                    drained(ins, t)

            act.wait_ge(S("l1a_ready"), 2 * KD)
            s5_tokens(0, 0)
            s5_token_copy(0)
            with act.Fori(0, 7) as i:
                s5_turn_F(i)
                filled(act, ticket0["s5"] + T_YB + 1, (i - 1) * 3)
                s5_tokens(i + 1, i)
                s5_evict_y(i)
                s5_token_copy(i)
            s5_turn_F(7)
            filled(act, ticket0["s5"] + T_YB + 1, 3 * 6)
            s5_evict_y(7)
            for n in range(2):
                emptied(act, *s5_t(7, T_YB + n))
            for k in range(KD):
                act.activation(hT[:, k, 0:NL], hT[:, k, 0:NL], ACT.Gelu_apprx_tanh).then_inc(S("gelu"), 1)
            for m in range(8):
                t = ticket0["glu"] + 2 * m + 1
                bank = filled(act, t)
                if m >= 4:
                    act.wait_ge(S("glu_gated"), m - 3)
                drained(act.activation(glu_sig[:, m % 4, :], bank[:, :], ACT.Sigmoid), t)
            norm_squares(act, "l1b", xT, TBL, hT, lambda k: act.wait_ge(S("glu_gated"), k + 1))
            norm_roots(act, "l1b", TBL)
            norm_shift(act, "l1b", TBL, hT, shift_of(1, 3))
            mlp_relu(act, 1, TBL)
            norm_squares(act, "mix", xT, TBL, hT, lambda k: tickets_emptied(act, "mlp1", k, 1, 56))
            norm_roots(act, "mix", TBL)
            for m in range(12):
                emptied(act, ticket0["qkv"] + m)
                act.activation(qkvT[:, m, :], qkvT[:, m, :], ACT.Silu).then_inc(S("qkv_silu"), 1)
            for name, o, func in (("zg", zT, ACT.Silu), ("gate", gateT, ACT.Gelu_apprx_tanh)):
                for m in range(4):
                    t = ticket0[name] + m
                    bank = filled(act, t)
                    drained(act.activation(o[:, m, :], bank[:, :], func), t)
            for m in range(8):
                act.wait_ge(S("qkv_silu"), m + 1)
                act.activation(qk_sq[:, m, :], qkvT[:, m, :], ACT.Square).then_inc(S("gq_sq"), 1)
            act.wait_ge(S("sp_abs"), 1)
            act.activation(lam[:, 2, :], lam[:, 1, :], ACT.Exp, scale=-1.0).then_inc(S("sp_act"), 1)
            act.activation(gt[:, G_E], gt[:, G_ABS], ACT.Exp, scale=-1.0).then_inc(S("sp_act"), 1)
            act.activation(gpar[:, 0, :], gpar[:, 0, :], ACT.Exp).then_inc(S("sp_act"), 1)
            act.wait_ge(S("sp_u"), 1)
            act.activation(lam[:, 4, :], lam[:, 3, :], ACT.Ln).then_inc(S("sp_act"), 1)
            act.activation(gt[:, G_LN], gt[:, G_U], ACT.Ln).then_inc(S("sp_act"), 1)
            act.activation(gt[:, G_BETA], gt[:, G_B], ACT.Sigmoid).then_inc(S("sp_act"), 1)
            act.wait_ge(S("g_ready"), 1)
            for m in range(4):
                if m >= 1:
                    act.wait_ge(S("lru_done"), m)
                tr, ti = ticket0["lru_r"] + m, ticket0["lru_i"] + m
                bank = filled(act, tr)
                drained(act.activation(lru_r, bank[:, :], ACT.Sigmoid, bias=col("lru_ba_2", m)), tr)
                bank = filled(act, ti)
                drained(act.activation(lru_i, bank[:, :], ACT.Sigmoid, bias=col("lru_bx_2", m)), ti)
                emptied(act, tr)
                act.activation(lru_a, lru_r, ACT.Exp, scale=lam[:, 7, m:m + 1]).then_inc(S("lru_exp"), 1)
                act.activation(lru_th, lru_r, ACT.Tanh, scale=lam[:, 7, m:m + 1]).then_inc(S("lru_exp"), 1)
                act.wait_ge(S("lru_gap"), m + 1)
                act.activation(lru_th, lru_th, ACT.Sqrt, scale=-1.0).then_inc(S("lru_root"), 1)
            for m in range(8):
                t = ticket0["gnorm"] + m
                bank = filled(act, t)
                rsqrt_start(act, bank[:, :], qk_sq[:, m, :], qk_rt[m], t, 1)
            act.wait_ge(S("lru_done"), 4)
            for m in range(8):
                emptied(act, ticket0["gnorm"] + m)
                rsqrt_guess(act, qk_rt[m], qk_y2[:, m, :], "gnorm_guess")
            for t in range(NTL):
                tk = ticket0["ktok"] + t
                bank = filled(act, tk)
                drained(act.activation(k_tok[:, t], bank[:, :].rearrange("p (h d) -> p h d", h=4), ACT.Copy), tk)
            for pair in range(2):
                for tt in (2 * pair, 2 * pair + 1):
                    t0 = ticket0[f"gpre{tt}"]
                    bank = filled(act, t0)
                    act.activation(gs[:, tt, :], bank[:, 0:16], ACT.Copy)
                    drained(act.activation(gx[:, tt, :], bank[:, 0:16], ACT.Exp), t0)
                    bank = filled(act, t0 + 1)
                    act.wait_ge(S("g_diff"), tt + 1)
                    act.activation(g_dec[:, tt % 2], g_dec[:, tt % 2], ACT.Exp).then_inc(S("g_dexp"), 1)
                    drained(act.activation(g_bc, bank[:, :].rearrange("p (h c) -> p h c", h=4), ACT.Exp), t0 + 1)
                    bank = filled(act, t0 + 2)
                    drained(act.activation(g_kbT, bank[:, :].rearrange("p (h c) -> p h c", h=4), ACT.Copy), t0 + 2)
                for lv in range(6):
                    for x in range(2):
                        t = ticket0[f"inv{pair}_{lv}"] + x
                        bank = filled(act, t)
                        drained(act.activation(inv_y[:, x], bank[:, :].rearrange("p (h c) -> p h c", h=4), ACT.Copy), t)
                for tt in (2 * pair, 2 * pair + 1):
                    t0 = ticket0[f"uw{tt}"]
                    bank = filled(act, t0)
                    drained(act.activation(u_tok[:, tt], bank[:, :].rearrange("p (h d) -> p h d", h=4), ACT.Copy), t0)
                    bank = filled(act, t0 + 1)
                    drained(act.activation(wT[:, :, tt * P:(tt + 1) * P], bank[:, :].rearrange("p (h c) -> p h c", h=4), ACT.Copy), t0 + 1)
            for n in range(8):
                t = ticket0["gscan"] + 3 * n + 1
                bank = filled(act, t)
                drained(act.activation(mix2[:, 0:4, n * GCH:(n + 1) * GCH], bank[:, 0:4 * GCH].rearrange("p (h c) -> p h c", h=4), ACT.Copy), t)
            emptied(act, ticket0["gscan"] + 22)
            for m in range(4):
                act.activation(qkvT[:, m, :], mix2[:, m, :], ACT.Square).then_inc(S("o_sq"), 1)
            for m in range(4):
                t = ticket0["norm_o"] + m
                bank = filled(act, t)
                rsqrt_start(act, bank[:, :], o_var[:, m, :], o_rt[:, m, :], t, P)
            for m in range(4):
                emptied(act, ticket0["norm_o"] + m)
                rsqrt_guess(act, o_rt[:, m, :], o_y2[:, m, :], "o_guess")
            for n in range(4):
                t, g = n // 2, n % 2
                bank = filled(act, ticket0["mem_in"] + n)
                drained(act.activation(memT[:, 4 * g:4 * g + 4, t * P:(t + 1) * P], bank[:, :].rearrange("p (k n) -> p k n", k=4), ACT.Copy),
                        ticket0["mem_in"] + n)
            for n in range(4):
                emptied(act, ticket0["mem_in"] + n)
            norm_squares(act, "mem", memT, TBM, mem_h)
            norm_roots(act, "mem", TBM, rs=rstd_mem)
            for n in range(4):
                t = ticket0["xk"] + n
                bank = filled(act, t)
                drained(act.activation(xkT[:, 2 * n:2 * n + 2, :], bank[:, :].rearrange("p (m n) -> p m n", m=2), ACT.Copy), t)
            for n in range(4):
                t = ticket0["xv"] + n
                bank = filled(act, t)
                drained(act.activation(xv_tok[:, n % 2, (n // 2) * 512:(n // 2 + 1) * 512], bank[:, :], ACT.Copy), t)
            norm_squares(act, "xat", xT, TBL, hT, lambda k: emptied(act, ticket0["w_out2"] + k))
            norm_roots(act, "xat", TBL)
            for m in range(KD):
                t = ticket0["xq"] + m
                bank = filled(act, t)
                drained(act.activation(xqT[:, m, :], bank[:, :], ACT.Copy), t)
            for step, n in XAT_ORDER:
                t = ticket0[f"{step}{n}"]
                if step == "xscore":
                    act.wait_ge(S("xat_max"), n + 1)
                    bank = filled(act, t)
                    drained(act.activation(xprob[:, n % 2, :], bank[:, 0:MEM], ACT.Exp, bias=stat[:, n % 2, 3:4], scale=xat_scale,
                                           accum_out=stat[:, n % 2, 4:5]), t)
                else:
                    bank = filled(act, t)
                    o = xprobT[:, n % 2] if step == "xturn" else xoT[:, 2 * (n // 4):2 * (n // 4) + 2, n % 4 * P:(n % 4 + 1) * P]
                    drained(act.activation(o, bank[:, 0:2 * P].rearrange("p (t n) -> p t n", t=2), ACT.Copy), t)
            for n in range(4):
                t = ticket0["subk"] + n
                bank = filled(act, t)
                drained(act.activation(subT[:, 4 * n:4 * n + 4, :], bank[:, :].rearrange("p (v n) -> p v n", v=4), ACT.Copy), t)
            norm_squares(act, "ffn", xT, TBL, hT, lambda k: emptied(act, ticket0["wo"] + k))
            norm_roots(act, "ffn", TBL)
            for j in range(4):
                for v in range(4):
                    t = ticket0[f"pq{j}"] + v
                    bank = filled(act, t)
                    drained(act.activation(pqT[:, j % 2, v, :], bank[:, :], ACT.Copy), t)
                for t in range(NTL):
                    u = NTL * j + t
                    if u >= 2:
                        act.wait_ge(S("psc_used"), u - 1)
                    bank = filled(act, ticket0[f"psc{j}"] + t)
                    drained(act.activation(psc[:, u % 2], bank[:, :].rearrange("p (v n) -> p v n", v=4), ACT.Copy), ticket0[f"psc{j}"] + t)
            for n in range(8):
                tk = ticket0["htok"] + n
                bank = filled(act, tk)
                drained(act.activation(h_tok[:, n // 2, n % 2 * 512:(n % 2 + 1) * 512], bank[:, :], ACT.Copy), tk)
            act.wait_ge(S("best_ready"), 1)
            act.activation(gate, best.rearrange("p t h k -> p t (h k)"), ACT.Exp).then_inc(S("gate_exp"), 1)
            for T_ in range(NTL):
                with act.Fori(0, EGROUPS) as i:
                    act.wait_ge(S("u_used"), i * ERING + T_ * EXPERTS + 2 * ERING)
                    act.activation(gelus, dots, ACT.Gelu_apprx_tanh).then_inc(S("gelus_ready"), 1)
                    act.wait_ge(S("acts_ready"), i + EGROUPS * T_ + 1)
                    for s in range(ERING):
                        act.wait_ge(S("v_used"), i * ERING + T_ * EXPERTS + s + 1)
                        act.activation(diag[:, s, :], ident[:, :], ACT.Copy, scale=acts[:, s:s + 1]).then_inc(S("diag_ready"), 1)
                if T_ >= 1:
                    act.wait_ge(S("out_ready"), T_)
                for g in range(2):
                    last = act.activation(sq_junk[:, 512 * g:512 * g + 512], filled(act, ticket0["ffn"] + 2 * T_ + g)[:, :], ACT.Square, accum_out=fin[:, g:g + 1])
                last.then_inc(S("fin_sq"), 1)
                act.wait_ge(S("fin_sum"), T_ + 1)
                act.activation(fin[:, 3:4], fin[:, 2:3], ACT.Sqrt, bias=eps_col, scale=1.0 / D).then_inc(S("fin_root"), 1)

        @block_.vector
        def _(dve):
            dve_step(dve, dve.memset(eps_col, EPS))
            for n in range(0, 12, 2):
                t, g = n // 2, n % 2
                bank = filled(dve, ticket0["x_in"] + n)
                drained(dve.tensor_copy(xT[:, 4 * g:4 * g + 4, t * P:(t + 1) * P],
                                        bank[:, :].rearrange("p (k n) -> p k n", k=4)), ticket0["x_in"] + n)
            for i, (_, _, n) in enumerate(vec_rows):
                t = ticket0["vecs"] + i
                bank = filled(dve, t)
                drained(dve.tensor_copy(vec_cols[i][:, :], bank[:, 0:n]), t)
                emptied(dve, t)

            with dve.Fori(0, 3) as i:
                for s in range(NSLOT):
                    t = ticket0["ada0"] + ADA_COL[s]
                    bank = filled(dve, t, i)
                    ci, r = col_of["ada_b"]
                    bias = vec_cols[ci][:, bass.ds(i * 16 + (r + 4 * s), 4)]
                    drained(dve.tensor_tensor(modT[0][:, bass.ds(i * 16 + 4 * s, 4), :],
                                              bank[:, 0:8].rearrange("p (m s) -> p m s", s=2), bcast(bias, 2), ALU.add), t)
            for n in range(16, 24):
                emptied(dve, ticket0["ada0"] + n)
            norm_gains(dve, 0, gain1[0], "norm1_g", 1)
            norm_gains(dve, 0, gain2[0], "norm2_g", 4)

            norm_scale(dve, "l0a", xT, TBS, hT, lambda k, s: gain1[0][:, k, s:s + 1])
            ada1_columns(dve, 0)

            norm_scale(dve, "cq", cqT, TBS, cqT, lambda k, s: col("mla_q_norm_g", k), kd=2)
            norm_scale(dve, "ckv", ckvT.unsqueeze(1), TBS, ckvT.unsqueeze(1), lambda k, s: col("mla_kv_norm_g"), kd=1,
                       rs=rstd_qk[:, 0, :])
            ada1_columns(dve, 1)
            for t in range(0, 6, 2):
                bank = filled(dve, ticket0["v_tok"] + t)
                drained(dve.tensor_copy(v_tok[:, t, :], bank[:, :]), ticket0["v_tok"] + t)
            dve.wait_ge(S("mla_tables"), 16 * MLA_LOADS)
            for step, n in mla_order():
                t0 = ticket0[f"{step}{n}"]
                j, head = n % 2, n // 2
                x = (qh, kh)[j][:, head % 2, :]
                if step == "norm":
                    rsqrt_newton(dve, var_qk[0:QK, j, :], rstd_qk[0:QK, j, :], sqs[0:QK, j, :], "qk_guess", n)
                    for lo, hi in TBS:
                        dve.scalar_tensor_tensor(x[0:QK, lo:hi], x[0:QK, lo:hi], small[0:QK, 2 + j:3 + j], rstd_qk[0:QK, j, lo:hi],
                                                 ALU.mult, ALU.mult).then_inc(S("qk_normed"), 1)
                elif step == "rot":
                    r = slice(NOPE, QK)
                    bank = filled(dve, t0)
                    if n >= 1:
                        dve.wait_ge(S("qk_ready"), n)
                    drained(dve.tensor_tensor(rope_tmp[r], bank[r, :], sin_mla[r], ALU.mult), t0)
                    emptied(dve, t0)
                    dve_step(dve, dve.tensor_tensor(x[r, 0:NL], x[r, 0:NL], cos_mla[r], ALU.mult))
                    dve.tensor_tensor(x[r, 0:NL], x[r, 0:NL], rope_tmp[r], ALU.add).then_inc(S("qk_ready"), 1)
                elif step == "scores":
                    st = stat[:, n % 3, :]
                    two = n % 6 < 4
                    for b in range(2 if two else 1):
                        bank = filled(dve, t0 + b)
                        w = NL if two and b == 0 else NC
                        dve_step(dve, dve.reduce_max(st[:, b:b + 1], bank[:, 0:w], AX_X))
                    if two:
                        dve_step(dve, dve.tensor_tensor(st[:, 0:1], st[:, 0:1], st[:, 1:2], ALU.max))
                    dve.tensor_scalar(st[:, 3:4], st[:, 0:1], -att_scale, None, ALU.mult).then_inc(S("score_max"), 1)
                elif step == "scale":
                    st = stat[:, n % 3, :]
                    two = n % 6 < 4
                    for b in range(2 if two else 1):
                        emptied(dve, ticket0[f"scores{n}"] + b)
                    if two:
                        dve_step(dve, dve.tensor_tensor(st[:, 4:5], st[:, 4:5], st[:, 5:6], ALU.add))
                    dve_step(dve, dve.reciprocal(st[:, 6:7], st[:, 4:5]))
                    keys = slice(0, NT) if two else KEYS[1]
                    dve.tensor_scalar(prob_of[n % 3][:, keys], prob_of[n % 3][:, keys], st[:, 6:7], None, ALU.mult)\
                       .then_inc(S("prob_ready"), 1)
                elif step == "turn" and n % 6 < 4:
                    bank = filled(dve, t0)
                    drained(dve.tensor_copy(probT[:, n % 2, 0:4, :], bank[:, :].rearrange("p (t n) -> p t n", t=4)), t0)
                elif step == "out":
                    h, rows = n // 6, HEADROWS[n // 6]
                    bank = filled(dve, t0)
                    drained(dve.tensor_copy(mixT[rows, h // 2, (n % 6) * P:(n % 6 + 1) * P], bank[rows, 0:P]), t0)

            for t in range(6):
                bank = filled(dve, ticket0["z_rv"] + t)
                drained(dve.tensor_copy(rv[:, t, :], bank[:, :]), ticket0["z_rv"] + t)
            dve.wait_ge(S("ret_tables"), 48)
            for j, x in enumerate((rqT, rkT)):
                for m in range(4):
                    t = ticket0["rrot"] + 4 * j + m
                    bank = filled(dve, t)
                    drained(dve.tensor_tensor(decayed[:, m, :], bank[:, :], sin_ret, ALU.mult), t)
                    emptied(dve, t)
                    dve_step(dve, dve.tensor_tensor(x[:, m, 0:NL], x[:, m, 0:NL], cos_ret, ALU.mult))
                    dve.tensor_tensor(x[:, m, 0:NL], x[:, m, 0:NL], decayed[:, m, :], ALU.add).then_inc(S("rot_done"), 1)
            dve.wait_ge(S("rot_done"), 8)
            dve.wait_ge(S("lg_exp"), 1)
            dve.tensor_scalar(lg[:, LG_U, :], lg[:, LG_E, :], -1.0, 1.0, ALU.mult, ALU.add).then_inc(S("lg_u"), 1)
            dve.wait_ge(S("lg_u"), 1)
            dve_step(dve, dve.tensor_scalar(lg[:, LG_D, :], lg[:, LG_U, :], -1.0, -1e-30, ALU.add, ALU.add))
            dve_step(dve, dve.reciprocal(lg[:, LG_D, :], lg[:, LG_D, :]))
            dve_step(dve, dve.tensor_tensor(lg[:, LG_D, :], lg[:, LG_D, :], lg[:, LG_E, :], ALU.mult))
            dve.wait_ge(S("lg_ln"), 1)
            dve_step(dve, dve.tensor_scalar(lg[:, LG, :], lg[:, LG, :], -1e-30, -1.0, ALU.add, ALU.mult))
            dve_step(dve, dve.tensor_tensor(lg[:, LG, :], lg[:, LG, :], lg[:, LG_D, :], ALU.mult))
            dve_step(dve, dve.tensor_scalar(lg[:, LG_512, :], lg[:, LG, :], 512.0, None, ALU.mult))
            dve_step(dve, dve.tensor_scalar(lg[:, LG_256, :], lg[:, LG, :], 256.0, None, ALU.mult))
            dve.tensor_scalar(lg[:, LG_NEG, :], lg[:, LG, :], -1.0, None, ALU.mult).then_inc(S("lg_ready"), 1)
            dve.wait_ge(S("lg_ready"), 1)
            dve.wait_ge(S("dist_landed"), 16)
            for step, m in ret_order():
                h, j = m // 8, m % 8
                if step == "rscore":
                    if j == 0:
                        if h >= 1:
                            dve.wait_ge(S("decay_exp"), 3 * h)
                        dve_step(dve, dve.tensor_scalar(decay_tmp, ret_dist, lg[:, LG, h:h + 1], None, ALU.mult))
                        dve.scalar_tensor_tensor(decay_tmp, ret_dist, lg[:, LG_NEG, H_R + h:H_R + h + 1], decay_tmp,
                                                 ALU.mult, ALU.min).then_inc(S("decay_arg"), 1)
                        dve.wait_ge(S("decay_exp"), 3 * h + 2)
                        dve.tensor_tensor(decay_ctx[h % 2], decay_ctx[h % 2], decay_ctx2, ALU.add).then_inc(S("decay_ready"), 1)
                        dve.wait_ge(S("decay_ready"), h + 1)
                        dve.wait_ge(S("decay_exp"), 3 * h + 3)
                    t = ticket0[f"rscore{m}"]
                    bank = filled(dve, t)
                    w = NL if j < 6 else NC
                    drained(dve.tensor_tensor(decayed[:, m % 4, 0:w], bank[:, 0:w], ret_decay_slice(m), ALU.mult), t)
            for c in range(4):
                for b, (lo, hi) in enumerate(TBS):
                    t = ticket0["rmean"] + 2 * c + b
                    bank = filled(dve, t)
                    drained(dve.tensor_tensor(mixT[:, 4 + c, lo:hi], mixT[:, 4 + c, lo:hi], bank[:, 0:hi - lo], ALU.subtract), t)
            for c in range(4):
                for b, (lo, hi) in enumerate(TBS):
                    rsqrt_newton(dve, rqT[:, c, lo:hi], rkT[:, c, lo:hi], decayed[:, 2 * (c % 2) + b, 0:hi - lo], "ret_guess", 2 * c + b)
                    dve_step(dve, dve.tensor_tensor(rkT[:, c, lo:hi], rkT[:, c, lo:hi], rgT[:, c, lo:hi], ALU.mult))
                    dve.tensor_tensor(mixT[:, 4 + c, lo:hi], mixT[:, 4 + c, lo:hi], rkT[:, c, lo:hi], ALU.mult)\
                       .then_inc(S("ret_gated"), 1)
            for m in range(8):
                for b, (lo, hi) in enumerate(TBS):
                    t = ticket0["w_out"] + 2 * m + b
                    bank = filled(dve, t)
                    drained(dve.scalar_tensor_tensor(xT[:, m, lo:hi], bank[:, 0:hi - lo], modT[0][:, 2 * KD + m, b:b + 1],
                                                     xT[:, m, lo:hi], ALU.mult, ALU.add), t)

            norm_scale(dve, "l0b", xT, TBS, hT, lambda k, s: gain2[0][:, k, s:s + 1])
            ada1_columns(dve, 2)

            for d in range(2):
                t = ticket0["s5_prm"] + d
                bank = filled(dve, t)
                drained(dve.tensor_copy(s5_prm[:, d], bank[:, 0:96].rearrange("p (j r) -> p j r", j=3)), t)
            for d in range(2):
                emptied(dve, ticket0["s5_prm"] + d)
            dve_step(dve, dve.memset(prep[:, 23], 0.0))
            dve.memset(small[:, 14:15], 0.0).then_inc(S("s5_prm_ready"), 1)
            are, aim = s5_prm[:, :, 0, :], s5_prm[:, :, 1, :]
            DT, LR, SIN_IN, COS_IN, RAD, RADI, SIN, COS = (prep[:, j] for j in range(8))
            T = [prep[:, j] for j in range(8, 23)]

            def mul(o, a, b):
                dve_step(dve, dve.tensor_tensor(o, a, b, ALU.mult))

            def add(o, a, b):
                dve_step(dve, dve.tensor_tensor(o, a, b, ALU.add))

            def sub(o, a, b):
                dve_step(dve, dve.tensor_tensor(o, a, b, ALU.subtract))

            def cmul(o_re, o_im, a, b, t1, t2):
                mul(t1, a[0], b[0])
                mul(t2, a[1], b[1])
                sub(o_re, t1, t2)
                mul(t1, a[0], b[1])
                mul(t2, a[1], b[0])
                add(o_im, t1, t2)

            def wrap(o, x):
                magic, two_pi = 12582912.0, 2.0 * np.pi
                dve_step(dve, dve.tensor_scalar(T[0], x, 1.0 / two_pi, None, ALU.mult))
                dve_step(dve, dve.tensor_scalar(T[0], T[0], magic, None, ALU.add))
                dve_step(dve, dve.tensor_scalar(T[0], T[0], -magic, None, ALU.add))
                dve_step(dve, dve.scalar_tensor_tensor(T[1], T[0], -6.28125, x, ALU.mult, ALU.add))
                dve_step(dve, dve.scalar_tensor_tensor(o, T[0], -(two_pi - 6.28125), T[1], ALU.mult, ALU.add))
                dve_step(dve, dve.tensor_scalar(o, o, 3.1415925, -3.1415925, ALU.min, ALU.max))

            dve.wait_ge(S("s5_act"), 1)
            mul(T[2], are, DT)
            dve_step(dve, dve.tensor_scalar(LR, T[2], -21.0, None, ALU.max))
            mul(T[2], aim, DT)
            wrap(SIN_IN, T[2])
            dve_step(dve, dve.tensor_scalar(T[3], SIN_IN, float(np.pi / 2), None, ALU.add))
            wrap(COS_IN, T[3])
            dve.memset(small[:, 14:15], 0.0).then_inc(S("s5_args"), 1)
            dve.wait_ge(S("s5_act"), 6)
            A1, AI = (T[2], T[3]), (T[4], T[5])
            mul(A1[0], RAD, COS)
            mul(A1[1], RAD, SIN)
            mul(AI[0], RADI, COS)
            mul(AI[1], RADI, SIN)
            dve_step(dve, dve.tensor_scalar(AI[1], AI[1], -1.0, None, ALU.mult))
            mul(T[0], are, are)
            mul(T[1], aim, aim)
            add(T[0], T[0], T[1])
            dve_step(dve, dve.reciprocal(T[0], T[0]))
            dve_step(dve, dve.tensor_scalar(T[6], A1[0], -1.0, None, ALU.add))
            mul(T[1], T[6], are)
            mul(T[7], A1[1], aim)
            add(T[1], T[1], T[7])
            mul(T[8], T[1], T[0])
            mul(T[1], A1[1], are)
            mul(T[7], T[6], aim)
            sub(T[1], T[1], T[7])
            mul(T[9], T[1], T[0])
            for d in range(2):
                q = [bcast(T[8 + c][:, d, :], 16) for c in range(2)]
                cmul(prep_big[:, 2], prep_big[:, 3], q, (s5_b[:, d, 0], s5_b[:, d, 1]), prep_big[:, 0], prep_big[:, 1])
                for c in range(2):
                    dve_step(dve, dve.tensor_copy(s5_b[:, d, c], prep_big[:, 2 + c]))
            pw = [[s5_pw[:, c, :, :, k] for c in range(2)] for k in range(9)]
            dve_step(dve, dve.memset(s5_pw[:, 0, :, :, 4], 1.0))
            dve_step(dve, dve.memset(s5_pw[:, 1, :, :, 4], 0.0))
            for base, sgn in ((A1, 1), (AI, -1)):
                for c in range(2):
                    dve_step(dve, dve.tensor_copy(pw[4 + sgn][c], base[c]))
                cmul(*pw[4 + 2 * sgn], base, base, T[0], T[1])
                cmul(*pw[4 + 3 * sgn], pw[4 + 2 * sgn], base, T[0], T[1])
                cmul(*pw[4 + 4 * sgn], pw[4 + 2 * sgn], pw[4 + 2 * sgn], T[0], T[1])
            u = (COS, SIN)
            for n in range(9):
                o = (s5_qp[:, n - 2, 0], s5_qp[:, n - 2, 1]) if n >= 2 else (T[6 + 2 * n], T[7 + 2 * n])
                cmul(*o, u, u, T[0], T[1])
                u = o
            dve.memset(small[:, 14:15], 0.0).then_inc(S("s5_prep"), 1)
            dve.wait_ge(S("s5_prep"), 1)
            dve.memset(small[:, 14:15], 0.0).then_inc(S("s5_turned"), 1)
            for n in range(8):
                emptied(dve, ticket0["s5_c"] + n)
            rev = lambda ap, lo, hi: ap[:, :, hi - 1:(lo - 1 if lo else None):-1]
            def s5_forward(i):
                ta, tb = s5_tmp[:, 0:512], s5_tmp[:, 512:1024]
                for d in range(2):
                    ks = slice(1, 9) if d == 0 else slice(0, 8)
                    p = [bcast(s5_pw[:, c, d, bass.ds(i * 4, 4), ks], 16) for c in range(2)]
                    b = [lead(s5_b[:, d, c, bass.ds(i * 4, 4), :], 8) for c in range(2)]
                    t1, t2, fr, fi = (x.rearrange("p (r k h) -> p r k h", r=4, k=8) for x in (
                        ta, tb, s5_F[:, d, 0].rearrange("p r x -> p (r x)"), s5_F[:, d, 1].rearrange("p r x -> p (r x)")))
                    if d == 0:
                        fr, fi = fr[:, :, ::-1, :], fi[:, :, ::-1, :]
                    mul(t1, p[0], b[0])
                    mul(t2, p[1], b[1])
                    sub(fr, t1, t2)
                    mul(t1, p[0], b[1])
                    mul(t2, p[1], b[0])
                    dve.tensor_tensor(fi, t1, t2, ALU.add).then_inc(S("s5_F"), 1)
                    dve.wait_ge(S("s5_F"), 2 * i + d + 1)

            s5_forward(0)
            s5_output_side(dve, 0, 1, s5_tmp, dve_step, "s5_E1")
            dve.wait_ge(S("s5_E1"), 1)
            mlp_square_and_add(dve, 0, TBS)

            norm_gains(dve, 1, gain1[1], "norm1_g", 1)
            norm_scale(dve, "l1a", xT, TBS, hT, lambda k, s: gain1[1][:, k, s:s + 1])
            ada1_columns(dve, 3)
            def s5_scans(i):
                ta, tb = s5_tmp[:, 0:512], s5_tmp[:, 512:1024]
                for d in range(2):
                    if d == 0:
                        pool_done = i * (1 + 7 * 6 + 6) + 4 + 7 * 6
                        dve.wait_ge(S("pool_done"), pool_done)
                        dve.wait_ge(S("s5_decays"), 2 * i + 2)
                    banks = [filled(dve, *s5_t(i, T_FI[d] + c))[:, 0:4 * NCH].rearrange("p (r n) -> p r n", r=4) for c in range(2)]
                    tab = [s5_tab[:, c, d] for c in range(2)]
                    parts = ((0, NCH),) if d == 0 else ((0, CCH), (CCH, NCH))
                    t1, t2 = (x[:, 0:4 * NCH].rearrange("p (r n) -> p r n", r=4) for x in (ta, tb))
                    order = (lambda ap, lo, hi: ap[:, :, lo:hi]) if d == 0 else rev
                    for lo, hi in parts:
                        x = [b_[:, :, lo:hi] for b_ in banks]
                        c_, s_ = (order(t_, lo, hi) for t_ in tab)
                        o1, o2 = t1[:, :, lo:hi], t2[:, :, lo:hi]
                        mul(o1, x[0], c_)
                        mul(o2, x[1], s_)
                        add(order(s5_g[:, 0], lo, hi), o1, o2)
                        if hi < NCH:
                            mul(o1, x[1], c_)
                            mul(o2, x[0], s_)
                        else:
                            drained(dve.tensor_tensor(o1, x[1], c_, ALU.mult), s5_t(i, T_FI[d] + 1)[0])
                            drained(dve.tensor_tensor(o2, x[0], s_, ALU.mult), s5_t(i, T_FI[d])[0])
                            for c in range(2):
                                emptied(dve, *s5_t(i, T_FI[d] + c))
                        sub(order(s5_g[:, 1], lo, hi), o1, o2)
                    for c in range(2):
                        dve_step(dve, dve.tensor_tensor_scan(s5_w[:, c].rearrange("p r n -> p (r n)"), s5_g[:, c].rearrange("p r n -> p (r n)"),
                                                             s5_decay[:, d].rearrange("p r n -> p (r n)"), 0.0, ALU.add, ALU.mult))
                    w = [s5_w[:, c, :, CCH - 1:NCH - 1] if d == 0 else s5_w[:, c, :, NCH - 2:CCH - 2:-1] for c in range(2)]
                    t_ = [x[:, :, CCH:NCH] if d == 0 else x[:, :, NCH - 1:CCH - 1:-1] for x in tab]
                    o1, o2 = t1[:, :, 0:LCH], t2[:, :, 0:LCH]
                    mul(o1, w[0], t_[0])
                    mul(o2, w[1], t_[1])
                    sub(s5_s[:, d, 0], o1, o2)
                    mul(o1, w[0], t_[1])
                    mul(o2, w[1], t_[0])
                    dve.tensor_tensor(s5_s[:, d, 1], o1, o2, ALU.add).then_inc(S("s5_turned"), 1)
                    dve.wait_ge(S("s5_turned"), 2 * i + d + 2)
                for d in range(2):
                    for n in range(2):
                        t, ahead = s5_t(i, T_MM[d] + n)
                        bank = filled(dve, t, ahead)[:, :].rearrange("p (g x) -> p g x", g=4)
                        mask = s5_mask[:, d, :].unsqueeze(1).to_broadcast([P, 4, P])
                        o = s5_M.rearrange("p (r two) x -> p two r x", two=2)[:, n]
                        o_ = o if d == 0 else s5_tmp[:, 512 * n:512 * n + 512].rearrange("p (g x) -> p g x", g=4)
                        drained(dve.tensor_tensor(o_, bank, mask, ALU.mult), t)
                        emptied(dve, t, ahead)
                        if d == 1:
                            dve.tensor_tensor(o, o, o_, ALU.add).then_inc(S("s5_M"), 1)

            def s5_outputs(i):
                ci, r = col_of["s5_d"]
                for n in range(2):
                    t, ahead = s5_t(i, T_YB + n)
                    bank = filled(dve, t, ahead)[:, 0:4 * LCH].rearrange("p (t c) -> p t c", t=4)
                    hv = hT[:, bass.ds(i, 1), 0:NL].squeeze(1).rearrange("p (c t) -> p t c", t=8)[:, 4 * n:4 * n + 4, :]
                    drained(dve.scalar_tensor_tensor(hv, hv, vec_cols[ci][:, bass.ds(i + r, 1)], bank, ALU.mult, ALU.add), t)

            with dve.Fori(0, 7) as i:
                dve_step.loop(i, S5_DVE_STEPS)
                s5_scans(i)
                dve.wait_ge(S("s5_M"), 2 * i + 2)
                s5_forward(i + 1)
                s5_outputs(i)
                s5_output_side(dve, i + 1, 1, s5_tmp, dve_step, "s5_E1")
                dve.wait_ge(S("s5_E1"), i + 2)
                dve_step.end_loop(7)
            s5_scans(7)
            s5_outputs(7)
            ada1_columns(dve, 4)
            norm_gains(dve, 1, gain2[1], "norm2_g", 4)
            for m in range(8):
                t = ticket0["glu"] + 2 * m
                bank = filled(dve, t)
                emptied(dve, t + 1)
                drained(dve.tensor_tensor(glu_sig[:, m % 4, :], bank[:, :], glu_sig[:, m % 4, :], ALU.mult), t)
                emptied(dve, t)
                dve.scalar_tensor_tensor(xT[:, m, 0:NL], glu_sig[:, m % 4, :], modT[1][:, 2 * KD + m, 0:1], xT[:, m, 0:NL],
                                         ALU.mult, ALU.add).then_inc(S("glu_gated"), 1)
            norm_scale(dve, "l1b", xT, TBL, hT, lambda k, s: gain2[1][:, k, 0:1])
            ada1_columns(dve, 5)
            mlp_square_and_add(dve, 1, TBL)

            norm_scale(dve, "mix", xT, TBL, hT, lambda k, s: col("norm_mix_w_2", k))

            def conv(bank, t, o, w, bias=None):
                if bias is None:
                    dve_step(dve, dve.tensor_scalar(o, bank[:, :], w(3), None, ALU.mult))
                else:
                    dve_step(dve, dve.tensor_scalar(o, bank[:, :], w(3), bias, ALU.mult, ALU.add))
                for j in (2, 1):
                    s = 3 - j
                    dve_step(dve, dve.scalar_tensor_tensor(o[:, s:NL], bank[:, 0:NL - s], w(j), o[:, s:NL], ALU.mult, ALU.add))
                drained(dve.scalar_tensor_tensor(o[:, 3:NL], bank[:, 0:NL - 3], w(0), o[:, 3:NL], ALU.mult, ALU.add), t)

            for m in range(12):
                t = ticket0["qkv"] + m
                conv(filled(dve, t), t, qkvT[:, m, :], lambda j: col("conv_qkv_w_2", 12 * j + m))
            dve.wait_ge(S("mix2_landed"), 16 * MIX2_LOADS)
            t = ticket0["ab"]
            ab = filled(dve, t)[:, 0:8 * NTL].rearrange("p (t c) -> p t c", t=NTL)
            dve_step(dve, dve.tensor_tensor(gt[:, G_A], ab[:, :, 0:4], gpar[:, 1, :].unsqueeze(1).to_broadcast([P, NTL, 4]), ALU.add))
            drained(dve.tensor_copy(gt[:, G_B], ab[:, :, 4:8]), t)
            dve_step(dve, dve.tensor_scalar(lam[:, 0, :], col("lru_lambda_2", 0, 4), -1.0, None, ALU.mult))
            SOFTPLUS = ((lam[:, 0, :], lam[:, 1, :], lam[:, 2, :], lam[:, 3, :], lam[:, 4, :], lam[:, 5, :]),
                        (gt[:, G_A], gt[:, G_ABS], gt[:, G_E], gt[:, G_U], gt[:, G_LN], gt[:, G_T]))
            for x, mag, *_ in SOFTPLUS:
                dve_step(dve, dve.scalar_tensor_tensor(mag, x, -1.0, x, ALU.mult, ALU.max))
            dve.memset(small[:, 14:15], 0.0).then_inc(S("sp_abs"), 1)
            dve.wait_ge(S("sp_act"), 3)
            for _, _, e, u, *_ in SOFTPLUS:
                dve_step(dve, dve.tensor_scalar(u, e, 1.0, None, ALU.add))
            dve.memset(small[:, 14:15], 0.0).then_inc(S("sp_u"), 1)
            for m in range(4):
                t = ticket0["xr"] + m
                conv(filled(dve, t), t, xrT[:, m, :], lambda j: col("lru_conv_w_2", 4 * j + m), col("lru_conv_b_2", m))
            dve.wait_ge(S("sp_act"), 6)
            for x, _, e, u, ln, tmp in SOFTPLUS:
                dve_step(dve, dve.tensor_scalar(tmp, u, -1.0, 1e-30, ALU.add, ALU.add))
                dve_step(dve, dve.reciprocal(tmp, tmp))
                mul(tmp, tmp, e)
                dve_step(dve, dve.scalar_tensor_tensor(tmp, ln, 1e-30, tmp, ALU.add, ALU.mult))
                dve_step(dve, dve.scalar_tensor_tensor(tmp, x, 0.0, tmp, ALU.max, ALU.add))
            dve_step(dve, dve.tensor_scalar(lam[:, 7, :], lam[:, 5, :], -8.0, None, ALU.mult))
            dve_step(dve, dve.tensor_tensor(gt[:, G_T], gt[:, G_T], gpar[:, 0, :].unsqueeze(1).to_broadcast([P, NTL, 4]), ALU.mult))
            dve.tensor_scalar(gt[:, G_G], gt[:, G_T], -1.0, None, ALU.mult).then_inc(S("g_ready"), 1)
            dve.wait_ge(S("g_ready"), 1)
            for m in range(4):
                dve.wait_ge(S("lru_exp"), 2 * m + 2)
                mul(lru_h, lru_a, lru_a)
                dve.scalar_tensor_tensor(lru_th, lru_h, 1.0, lru_th, ALU.add, ALU.mult).then_inc(S("lru_gap"), 1)
                emptied(dve, ticket0["lru_i"] + m)
                emptied(dve, ticket0["xr"] + m)
                mul(lru_i, lru_i, xrT[:, m, :])
                dve.wait_ge(S("lru_root"), m + 1)
                mul(lru_i, lru_i, lru_th)
                dve_step(dve, dve.tensor_tensor_scan(lru_h, lru_a, lru_i, 0.0, ALU.mult, ALU.add))
                emptied(dve, ticket0["gate"] + m)
                dve.tensor_tensor(mix2[:, 4 + m, :], lru_h, gateT[:, m, :], ALU.mult).then_inc(S("lru_done"), 1)
            for m in range(8):
                rsqrt_newton(dve, qk_sq[:, m, :], qk_rt[m], qk_y2[:, m, :], "gnorm_guess", m)
                dve.scalar_tensor_tensor(qkvT[:, m, :], qkvT[:, m, :], float(P ** -0.5) if m < 4 else 1.0, qk_rt[m],
                                         ALU.mult, ALU.mult).then_inc(S("g_normed"), 1)
            for t in range(NTL):
                tk = ticket0["vtok"] + t
                bank = filled(dve, tk)
                drained(dve.tensor_tensor(u_tok[:, t], bank[:, :].rearrange("p (h d) -> p h d", h=4), bcast(gt[:, G_BETA, t, :], P), ALU.mult), tk)
            dve.memset(g_state, 0.0).then_inc(S("g_state"), 1)
            dve.wait_ge(S("lru_done"), 4)
            dve.wait_ge(S("g_masks"), 16 * 9)
            for pair in range(2):
                for tt in (2 * pair, 2 * pair + 1):
                    t0, x = ticket0[f"gpre{tt}"], tt % 2
                    tok = slice(tt * P, (tt + 1) * P)
                    if tt > 0:
                        dve.wait_ge(S("g_qdec"), tt)
                        filled(dve, ticket0[f"gpre{tt - 1}"] + 2)
                    if tt == 2:
                        filled(dve, ticket0["uw1"] + 1)
                    dve.tensor_copy(g_bc, bcast(gt[:, G_G, tt, :], P)).then_inc(S("g_bcast"), 1)
                    emptied(dve, ticket0["ktok"] + tt)
                    dve.tensor_tensor(g_kw, k_tok[:, tt], bcast(gt[:, G_BETA, tt, :], P), ALU.mult).then_inc(S("g_kb"), 1)
                    emptied(dve, t0)
                    bank = filled(dve, t0 + 1)
                    for h in range(4):
                        last = dve.tensor_scalar(g_dec[:, x, h, :], bank[:, h * P:(h + 1) * P], gs[:, tt, h:h + 1], 0.0, ALU.subtract, ALU.min)
                    last.then_inc(S("g_diff"), 1)
                    dve.wait_ge(S("g_dexp"), tt + 1)
                    dve_step(dve, dve.tensor_tensor(g_dec[:, x], g_dec[:, x], bc4(tri_incl), ALU.mult))
                    for o, t in ((g_at[:, x], t0 + 3), (attnT[:, tt], t0 + 4)):
                        bank = filled(dve, t)
                        drained(dve.tensor_tensor(o, bank[:, :].rearrange("p (h c) -> p h c", h=4), g_dec[:, x], ALU.mult), t)
                    emptied(dve, t0 + 1)
                    dve.tensor_tensor(qkvT[:, 0:4, tok], qkvT[:, 0:4, tok], g_bc, ALU.mult).then_inc(S("g_qdec"), 1)
                if pair:
                    filled(dve, ticket0["uw1"] + 1)
                for x in range(2):
                    dve.tensor_copy(inv_x[:, x], bc4(ident[:, :]))
                    last = dve.tensor_copy(inv_xt[:, x], bc4(ident[:, :]))
                last.then_inc(S("g_eye"), 1)
                dve.wait_ge(S("g_eye"), pair + 1)
                for x in range(2):
                    emptied(dve, ticket0[f"gpre{2 * pair + x}"] + 3)
                for lv in range(6):
                    for x in range(2):
                        if lv > 0:
                            filled(dve, ticket0[f"inv{pair}_{lv - 1}"] + x)
                        dve.tensor_tensor(g_lvl[:, x], g_at[:, x], bc4(merge[lv]), ALU.mult).then_inc(S("g_level"), 1)
                    for x in range(2):
                        for o, t in ((inv_x[:, x], ticket0[f"inv{pair}_{lv}"] + 2 + 2 * x), (inv_xt[:, x], ticket0[f"inv{pair}_{lv}"] + 3 + 2 * x)):
                            if lv > 0:
                                emptied(dve, t - 6)
                            bank = filled(dve, t)
                            if o is inv_x[:, x]:
                                filled(dve, t + 1)
                            drained(dve.tensor_tensor(o, o, bank[:, :].rearrange("p (h c) -> p h c", h=4), ALU.subtract), t)
                for tt in (2 * pair, 2 * pair + 1):
                    mul(gt[:, G_BE, tt, :], gt[:, G_BETA, tt, :], gx[:, tt, 0:4])
                    if tt % 2:
                        filled(dve, ticket0[f"uw{tt - 1}"] + 1)
                    dve.tensor_tensor(g_kw, k_tok[:, tt], bcast(gt[:, G_BE, tt, :], P), ALU.mult).then_inc(S("g_kw"), 1)
                    dve.wait_ge(S("g_kw"), tt + 1)
                    dve.tensor_tensor(k_tok[:, tt], k_tok[:, tt], bcast(gx[:, tt, 4:8], P), ALU.mult).then_inc(S("g_kdec"), 1)
            for n in range(8):
                tt, r = n // 2, GHALF[n % 2]
                t0 = ticket0["gscan"] + 3 * n
                if n % 2 == 0:
                    emptied(dve, ticket0[f"uw{tt}"])
                bank = filled(dve, t0)
                drained(dve.tensor_tensor(v_new[r, :], u_tok[r, tt].rearrange("p h d -> p (h d)"), bank[r, :], ALU.subtract), t0)
                bank = filled(dve, t0 + 2)
                for h in range(4):
                    if h == 0:
                        dve.wait_ge(S("g_state"), 4 * n + 1)
                    ins = dve.scalar_tensor_tensor(g_state[:, h, :], g_state[:, h, :], gx[:, tt, 8 + 2 * h + n % 2:9 + 2 * h + n % 2],
                                                   bank[:, h * P:(h + 1) * P], ALU.mult, ALU.add)
                    ins.then_inc(S("g_state"), 1)
                dve.wait_ge(S("g_state"), 4 * n + 5)
                drained(dve.memset(small[:, 14:15], 0.0), t0 + 2)
            for m in range(4):
                rsqrt_newton(dve, o_var[:, m, :], o_rt[:, m, :], o_y2[:, m, :], "o_guess", m)
                emptied(dve, ticket0["zg"] + m)
                dve_step(dve, dve.scalar_tensor_tensor(mix2[:, m, :], mix2[:, m, :], col("gdn_norm_w_2"), o_rt[:, m, :], ALU.mult, ALU.mult))
                dve.tensor_tensor(mix2[:, m, :], mix2[:, m, :], zT[:, m, :], ALU.mult).then_inc(S("y_gdn"), 1)
            for m in range(8):
                t = ticket0["w_out2"] + m
                bank = filled(dve, t)
                drained(dve.tensor_tensor(xT[:, m, 0:NL], xT[:, m, 0:NL], bank[:, :], ALU.add), t)

            norm_scale(dve, "mem", memT, TBM, mem_h, lambda k, s: col("norm_mem_w_2", k), rs=rstd_mem)
            norm_scale(dve, "xat", xT, TBL, hT, lambda k, s: col("norm_xattn_w_2", k))
            for n in range(17):
                if n < 16:
                    st = stat[:, n % 2]
                    bank = filled(dve, ticket0[f"xscore{n}"])
                    if n >= 2:
                        dve.wait_ge(S("xat_prob"), n - 1)
                    dve_step(dve, dve.tensor_reduce(st[:, 0:1], bank[:, 0:MEM], AX_X, ALU.max))
                    dve.tensor_scalar(st[:, 3:4], st[:, 0:1], -xat_scale, None, ALU.mult).then_inc(S("xat_max"), 1)
                if n >= 1:
                    st = stat[:, (n - 1) % 2]
                    emptied(dve, ticket0[f"xscore{n - 1}"])
                    dve_step(dve, dve.reciprocal(st[:, 5:6], st[:, 4:5]))
                    dve.tensor_scalar(xprob[:, (n - 1) % 2, :], xprob[:, (n - 1) % 2, :], st[:, 5:6], None, ALU.mult).then_inc(S("xat_prob"), 1)
            for m in range(KD):
                t = ticket0["wo"] + m
                bank = filled(dve, t)
                drained(dve.tensor_tensor(xT[:, m, 0:NL], xT[:, m, 0:NL], bank[:, :], ALU.add), t)

            norm_scale(dve, "ffn", xT, TBL, hT, lambda k, s: col("norm_ffn_w_2", k))
            dve.memset(fin[:, 5:6], 0.0).then_inc(S("u_used"), ERING)
            dve.memset(fin[:, 6:7], 0.0).then_inc(S("v_used"), ERING)
            LOWEST = -3.4e38

            def top16(values, top, index, release=None):
                n = len(values)
                for r in (slice(0, 8), slice(8, 16)):
                    for v in range(n):
                        last = dve.max(top[v][:, r], values[v])
                    dve_step(dve, last)
                    for v in range(n):
                        last = dve.max_index(index[v][:, r], top[v][:, r], values[v])
                    if r.start == 0:
                        dve_step(dve, last)
                        for v in range(n):
                            last = dve.match_replace(values[v], top[v][:, r], values[v], LOWEST)
                        dve_step(dve, last)
                    elif release:
                        last.then_inc(S(release), 1)
                    else:
                        dve_step(dve, last)

            dve.wait_ge(S("peer_landed"), 16 * 3)
            for m in range(KD):
                emptied(dve, ticket0["wo"] + m)
            for u, (j, t) in enumerate(UNITS):
                emptied(dve, ticket0[f"psc{j}"] + t)
                vec = [(h, s) for h in range(2) for s in range(2)]
                top16([psc[:, u % 2, v, :] for v in range(4)], [s_top[:, h, s, :] for h, s in vec], [i_top[:, h, s, :] for h, s in vec], "psc_used")
                dve.wait_ge(S("psc_used"), u + 1)
                if u >= 2:
                    dve.wait_ge(S("peer_idx"), u - 1)
                dve.tensor_copy(i_f[:, u % 2], i_top)
                for h in range(2):
                    last = dve.tensor_tensor(cand[:, h, :].rearrange("p (a b) -> p a b", a=PTOPK), bcast(s_top[:, h, 0, :], PTOPK),
                                             s_top[:, h, 1, :].unsqueeze(1).to_broadcast([P, PTOPK, PTOPK]), ALU.add)
                dve_step(dve, last)
                top16([cand[:, h, :] for h in range(2)], [best[:, t, 2 * j + h, :] for h in range(2)], [pos_u[:, h, :] for h in range(2)])
                dve_step(dve, dve.tensor_copy(pos_f, pos_u))
                dve_step(dve, dve.tensor_scalar(pos_r, pos_f, 1.0 / PTOPK, -0.46875, ALU.mult, ALU.add))
                dve_step(dve, dve.tensor_scalar(pos_r, pos_r, 12582912.0, None, ALU.add))
                dve_step(dve, dve.tensor_scalar(pos_half[:, u % 2, 0], pos_r, -12582912.0, None, ALU.add))
                dve.scalar_tensor_tensor(pos_half[:, u % 2, 1], pos_half[:, u % 2, 0], -float(PTOPK), pos_f, ALU.mult, ALU.add)\
                   .then_inc(S("pos_ready"), 1)
                dve.wait_ge(S("pos_ready"), u + 1)
                for s in range(2):
                    for h in range(2):
                        last = dve.tensor_tensor(onehot[u % 2][:, s, h], bcast(pos_half[:, u % 2, s, h, :], PTOPK),
                                                 iota16.unsqueeze(1).to_broadcast([P, PTOPK, PTOPK]), ALU.is_equal)
                last.then_inc(S("onehot_ready"), 1)
            dve.wait_ge(S("peer_idx"), len(UNITS))
            dve_step(dve, dve.memset(wide_ident, 0.0))
            dve.tensor_copy(wide_ident[:, 3 * P:4 * P], ident[:, :]).then_inc(S("wide_ident"), 1)
            g_ = gate.rearrange("p t (h k) -> p (t h) k", h=PH)
            b_ = best.rearrange("p t h k -> p (t h) k")
            dve_step(dve, dve.tensor_copy(gate_sum, b_[:, :, 0]))
            dve.tensor_tensor(b_, b_, bcast(gate_sum, PTOPK), ALU.subtract).then_inc(S("best_ready"), 1)
            dve.wait_ge(S("gate_exp"), 1)
            dve_step(dve, dve.tensor_reduce(gate_sum, g_, AX_X, ALU.add))
            dve_step(dve, dve.reciprocal(gate_sum, gate_sum))
            dve_step(dve, dve.tensor_tensor(g_, g_, bcast(gate_sum, PTOPK), ALU.mult))
            for n in range(8):
                emptied(dve, ticket0["htok"] + n)
            for T_ in range(NTL):
                with dve.Fori(0, EGROUPS) as i:
                    for s in range(ERING):
                        dve.wait_ge(S(f"u_landed{s}"), i * 16 + 16 * (EGROUPS * T_ + 1))
                        dve.scalar_tensor_tensor(u_row[s], u_row[s], 1.0, h_tok[:, T_, :], ALU.mult, ALU.mult, accum_out=dots[:, s:s + 1]).then_inc(S("u_used"), 1)
                    dve.wait_ge(S("gelus_ready"), i + EGROUPS * T_ + 1)
                    dve.tensor_tensor(acts, gelus, gate[:, T_, bass.ds(i * ERING, ERING)], ALU.mult).then_inc(S("acts_ready"), 1)
                dve.wait_ge(S("fin_sq"), T_ + 1)
                dve.tensor_tensor(fin[:, 2:3], fin[:, 0:1], fin[:, 1:2], ALU.add).then_inc(S("fin_sum"), 1)
                dve.wait_ge(S("fin_root"), T_ + 1)
                dve_step(dve, dve.reciprocal(fin[:, 4:5], fin[:, 3:4]))
                if T_ >= 1:
                    dve.wait_ge(S("out_done"), 16 * T_)
                for g in range(2):
                    last = dve.scalar_tensor_tensor(out_tile[:, 512 * g:512 * g + 512], filled(dve, ticket0["ffn"] + 2 * T_ + g)[:, :], fin[:, 4:5],
                                                    w_final[:, 512 * g:512 * g + 512], ALU.mult, ALU.mult)
                last.then_inc(S("out_ready"), 1)


        @block_.tensor
        def _(pe):
            pe.wait_ge(S("x_landed"), 16 * 7)
            for n in range(12):
                t, g = n // 2, n % 2
                bank = claim(pe, ticket0["x_in"] + n)
                for j in range(4):
                    last = pe.transpose(bank[:, j * P:(j + 1) * P], x_in[:, t, (4 * g + j) * P:(4 * g + j + 1) * P], ident[:, :])
                fill(last, ticket0["x_in"] + n)
            pe.wait_ge(S("small_landed"), 16 * SMALL_LOADS)
            pe.wait_ge(S("vecs_landed"), 16 * len(ACT_VECS))
            for i, (rows, _, n) in enumerate(vec_rows):
                bank = claim(pe, ticket0["vecs"] + i)
                fill(pe.transpose(bank[:, 0:n], rows[0:n, :], ident[0:n, 0:n]), ticket0["vecs"] + i)
            pe.wait_ge(S("act_done"), 2)
            with pe.Fori(0, 3) as i:
                for s in range(NSLOT + 1):
                    if s < NSLOT:
                        w = block(pe, block0["ada0"] + s, KD, extra=i)
                        t = ticket0["ada0"] + ADA_ROW[s]
                        bank = claim(pe, t, i)
                        for k in range(KD):
                            last = pe.matmul(bank[0:2, :], silu_c[:, k, :], w[:, k, :], start=(k == 0), stop=(k == KD - 1))
                        fill(last, t)
                    if s >= 1:
                        t = ticket0["ada0"] + ADA_COL[s - 1]
                        emptied(pe, ticket0["ada0"] + ADA_ROW[s - 1], i)
                        bank = claim(pe, t, i)
                        pe.nop(nofuse=True)
                        for m in range(4):
                            last = pe.transpose(bank[:, 2 * m:2 * m + 2], ada_rows[:, (s - 1) % 2, m * P:(m + 1) * P], ident[0:2, 0:2])
                        fill(last, t)
            norm_sums(pe, "l0a", TBS, hT)
            ada1_products(pe, 0)
            w = block(pe, block0["w_in0"], KD, n=MLA_IN)
            for m in range(4):
                a, n = (m * P, P) if m < 3 else (Q_LORA + KV_LORA, ROPE)
                for b, (lo, hi) in enumerate(TBS):
                    t = ticket0["z_q"] + 2 * m + b
                    bank = claim(pe, t)
                    o = bank[:, 0:hi - lo] if m < 3 else bank[NOPE:QK, 0:hi - lo]
                    for k in range(KD):
                        pe.wait_ge(S("l0a_ready"), 2 * k + 2)
                        last = pe.matmul(o, w[:, k, a:a + n], hT[:, k, lo:hi], start=(k == 0), stop=(k == KD - 1))
                    fill(last, t)
            norm_sums(pe, "cq", TBS, sqs, 2, per=2)
            norm_sums(pe, "ckv", TBS, prob, 1, per=2)
            ada1_products(pe, 1)
            wv = block(pe, block0["ukv"], 1, n=1024)[:, 0, :].rearrange("p (h two v) -> p h two v", h=H_A, two=2)
            pe.wait_ge(S("ckv_mul"), 2)
            for t in range(6):
                bank = claim(pe, ticket0["v_tok"] + t)
                fill(pe.matmul(bank[:, :].rearrange("p (h v) -> p h v", h=H_A), ckvT[:, t * P:(t + 1) * P], wv[:, :, 1, :],
                               start=True, stop=True), ticket0["v_tok"] + t)
            wq = block(pe, block0["uq"], 2, n=H_A * QK)
            for step, n in mla_order():
                t0 = ticket0[f"{step}{n}"]
                h = {"proj": n, "nsum": n // 2, "rot": n // 2}.get(step, n // 6)
                if step in ("scale", "norm"):
                    continue
                if step == "proj":
                    if h == 0:
                        pe.wait_ge(S("cq_mul"), 4)
                    for b, (lo, hi) in enumerate(TBS):
                        bank = claim(pe, t0 + b)
                        for k in range(2):
                            last = pe.matmul(bank[0:QK, 0:hi - lo], wq[:, k, h * QK:(h + 1) * QK], cqT[:, k, lo:hi],
                                             start=(k == 0), stop=(k == 1))
                        fill(last, t0 + b)
                    for b, (lo, hi) in enumerate(TBS):
                        bank = claim(pe, t0 + 2 + b)
                        fill(pe.matmul(bank[0:NOPE, 0:hi - lo], wv[:, h, 0, :], ckvT[:, lo:hi], start=True, stop=True), t0 + 2 + b)
                elif step == "nsum":
                    pe.wait_ge(S("qk_sq"), h + 1)
                    for b, (lo, hi) in enumerate(TBS):
                        bank = claim(pe, t0 + b)
                        fill(pe.matmul(bank[0:QK, 0:hi - lo], ones[0:QK, 0:QK], sqs[0:QK, n % 2, lo:hi], start=True, stop=True), t0 + b)
                elif step == "rot":
                    pe.wait_ge(S("mla_tables"), 16 * MLA_LOADS)
                    pe.wait_ge(S("qk_normed"), 2 * n + 2)
                    bank = claim(pe, t0)
                    fill(pe.matmul(bank[0:QK, :], rot_mla[0:QK, 0:QK], (qh, kh)[n % 2][0:QK, h % 2, 0:NL], start=True, stop=True), t0)
                elif step == "scores":
                    pe.wait_ge(S("qk_ready"), 2 * h + 2)
                    q = qh[0:QK, h % 2, (n % 6) * P:(n % 6 + 1) * P]
                    for b, keys in enumerate(KEYS if n % 6 < 4 else KEYS[1:]):
                        bank = claim(pe, t0 + b)
                        k = kh[0:QK, h % 2, keys]
                        fill(pe.matmul(bank[:, 0:k.shape[1]], q, k, start=True, stop=True), t0 + b)
                elif step == "turn":
                    pe.wait_ge(S("prob_ready"), n + 1)
                    for b, tiles in enumerate(((0, 1, 2, 3), (4, 5)) if n % 6 < 4 else ((4, 5),)):
                        bank = claim(pe, t0 + b)
                        for j, t in enumerate(tiles):
                            last = pe.transpose(bank[:, j * P:(j + 1) * P], prob_of[n % 3][:, t * P:(t + 1) * P], ident[:, :])
                        fill(last, t0 + b)
                else:
                    tiles = range(6) if n % 6 < 4 else (4, 5)
                    bank = claim(pe, t0)
                    tt = ticket0[f"turn{n}"]
                    for b in range(mla_tickets("turn", n)):
                        emptied(pe, tt + b)
                    for t in tiles:
                        last = pe.matmul(bank[HEADROWS[h], 0:P], v_tok[:, t, h * 64:(h + 1) * 64], probT[:, n % 2, t, :],
                                         start=(t == tiles[0]), stop=(t == 5))
                    fill(last, t0)
            for j, name in enumerate(("z_rq", "z_rk", "z_rv", "z_rg")):
                w = block(pe, block0["w_in_r"] + j, KD)
                if name == "z_rv":
                    for t in range(6):
                        bank = claim(pe, ticket0[name] + t)
                        for k in range(KD):
                            last = pe.matmul(bank[:, :], hT[:, k, t * P:(t + 1) * P], w[:, k, :], start=(k == 0), stop=(k == KD - 1))
                        fill(last, ticket0[name] + t)
                    continue
                for m in range(4):
                    for b, (lo, hi) in enumerate(TBS):
                        t = ticket0[name] + 2 * m + b
                        bank = claim(pe, t)
                        for k in range(KD):
                            last = pe.matmul(bank[:, 0:hi - lo], w[:, k, m * P:(m + 1) * P], hT[:, k, lo:hi],
                                             start=(k == 0), stop=(k == KD - 1))
                        fill(last, t)
            pe.wait_ge(S("ret_tables"), 48)
            for j, (name, x) in enumerate((("z_rq", rqT), ("z_rk", rkT))):
                for m in range(4):
                    emptied(pe, ticket0[name] + 2 * m)
                    t = ticket0["rrot"] + 4 * j + m
                    fill(pe.matmul(claim(pe, t)[:, :], rot_ret, x[:, m, 0:NL], start=True, stop=True), t)
            for b in range(6):
                emptied(pe, ticket0["z_rv"] + b)
            for step, m in ret_order():
                h, j = m // 8, m % 8
                r, c = HEADROWS[h], h // 2
                lat = j < 6
                q = slice(0, NL) if lat else KEYS[1]
                kt = j if lat else j - 2
                if step == "rscore":
                    if h % 2 == 0 and j == 0:
                        pe.wait_ge(S("rot_done"), 5 + c)
                    t = ticket0[f"rscore{m}"]
                    bank = claim(pe, t)
                    fill(pe.matmul(bank[:, 0:q.stop - q.start], rkT[r, c, kt * P:(kt + 1) * P], rqT[r, c, q], start=True, stop=True), t)
                else:
                    t = ticket0[f"rout{h}_{j // 6}"]
                    if j in (0, 6):
                        claim(pe, t)
                    emptied(pe, ticket0[f"rscore{m}"])
                    last = pe.matmul(ps[t % NBANK][r, 0:q.stop - q.start], rv[:, kt, h * 64:(h + 1) * 64],
                                     decayed[:, m % 4, 0:q.stop - q.start], start=j in (0, 6), stop=j in (5, 7))
                    if j in (5, 7):
                        fill(last, t)
            for c in range(4):
                for b, (lo, hi) in enumerate(TBS):
                    for h in (2 * c, 2 * c + 1):
                        emptied(pe, ticket0[f"rout{h}_{b}"])
                    t = ticket0["rmean"] + 2 * c + b
                    fill(pe.matmul(claim(pe, t)[:, 0:hi - lo], blk64[:, :], mixT[:, 4 + c, lo:hi], start=True, stop=True), t)
            for c in range(4):
                for b, (lo, hi) in enumerate(TBS):
                    pe.wait_ge(S("ret_sq"), 2 * c + b + 1)
                    t = ticket0["rvar"] + 2 * c + b
                    fill(pe.matmul(claim(pe, t)[:, 0:hi - lo], blk64[:, :], rqT[:, c, lo:hi], start=True, stop=True), t)
            for j in range(2):
                w = block(pe, block0["w_out"] + j, 8)
                for m in range(4):
                    for b, (lo, hi) in enumerate(TBS):
                        t = ticket0["w_out"] + 8 * j + 2 * m + b
                        bank = claim(pe, t)
                        for k in range(8):
                            if j == 0 and k >= 4:
                                pe.wait_ge(S("ret_gated"), 2 * (k - 4) + b + 1)
                            last = pe.matmul(bank[:, 0:hi - lo], w[:, k, m * P:(m + 1) * P], mixT[:, k, lo:hi],
                                             start=(k == 0), stop=(k == 7))
                        fill(last, t)
            norm_sums(pe, "l0b", TBS, hT)
            ada1_products(pe, 2)
            pe.wait_ge(S("s5_landed"), 16 * S5_LOADS)
            pe.wait_ge(S("s5_dt_rows"), 2)
            for d in range(2):
                t = ticket0["s5_prm"] + d
                fill(pe.transpose(claim(pe, t)[:, 0:96], prm_rows[0:96, d, :], ident[0:96, 0:96]), t)
            for n in range(8):
                a, half = n // 2, n % 2
                t = ticket0["s5_c"] + n
                bank = claim(pe, t)
                for j in range(4):
                    last = pe.transpose(bank[:, j * P:(j + 1) * P], c_rows[:, a, 4 * half + j, :], ident[:, :])
                fill(last, t)

            for k in range(KD):
                pe.wait_ge(S("l0b_ready"), 2 * k + 2)
            mlp_products(pe, 0, TBS)
            norm_sums(pe, "l1a", TBS, hT)
            ada1_products(pe, 3)
            for k in range(KD):
                pe.wait_ge(S("l1a_ready"), 2 * k + 2)
            def s5_pe_tokens(i, at_):
                pe.wait_ge(S("s5_hs"), i + 1)
                hs = s5_hs[:, 0:NT].rearrange("p (c t) -> p t c", t=8)
                for n in range(4):
                    t, ahead = s5_t(at_, T_U + n)
                    bank = claim(pe, t, ahead)
                    for j in range(2):
                        last = pe.transpose(bank[0:NCH, j * P:(j + 1) * P], hs[:, 2 * n + j, :], ident[:, :])
                    fill(last, t)
                for n in range(4):
                    emptied(pe, *s5_t(at_, T_U + n))
                for n in range(2):
                    t, ahead = s5_t(at_, T_UT + n)
                    bank = claim(pe, t, ahead)
                    for j in range(4):
                        g = 4 * n + j
                        last = pe.transpose(bank[:, j * NCH:(j + 1) * NCH], s5_utok[0:NCH, g * P:(g + 1) * P], ident[0:NCH, 0:NCH])
                    fill(last, t)

            def s5_pe_sums(i):
                pe.wait_ge(S("s5_ucopy"), i + 1)
                for d in range(2):
                    pe.wait_ge(S("s5_F"), 2 * i + d + 1)
                    for c in range(2):
                        t, ahead = s5_t(i, T_FT[d] + c)
                        bank = claim(pe, t, ahead)
                        for r in range(4):
                            last = pe.transpose(bank[:, r * P:(r + 1) * P], s5_F[:, d, c, r, :], ident[:, :])
                        fill(last, t)
                    for c in range(2):
                        emptied(pe, *s5_t(i, T_FT[d] + c))
                    for c in range(2):
                        t, ahead = s5_t(i, T_FI[d] + c)
                        bank = claim(pe, t, ahead)
                        for r in range(4):
                            for par in range(2):
                                last = pe.matmul(bank[64 * par:64 * par + 64, r * NCH:(r + 1) * NCH],
                                                 s5_FT[:, c, r, 64 * par:64 * par + 64], s5_un[:, 2 * r + par, :], start=True, stop=True)
                        fill(last, t)

            def s5_pe_inside(i):
                for d in range(2):
                    if d == 0:
                        pe.wait_ge(S("pool_done"), i * (1 + 7 * 6 + 6) + 4 + 7 * 6 + 6)
                    else:
                        pe.wait_ge(S("s5_E1"), i + 1)
                    for n in range(2):
                        t, ahead = s5_t(i, T_MM[d] + n)
                        bank = claim(pe, t, ahead)
                        for j in range(4):
                            rows = slice(64 * n, 64 * n + 64)
                            for c in range(2):
                                last = pe.matmul(bank[:, j * P:(j + 1) * P], s5_F[rows, d, c, j, :], s5_E[rows, d, c, j, :],
                                                 start=(c == 0), stop=(c == 1))
                        fill(last, t)

            def s5_pe_y(i):
                pe.wait_ge(S("s5_M"), 2 * i + 2)
                pe.wait_ge(S("s5_ucopy"), i + 1)
                pe.wait_ge(S("s5_turned"), 2 * i + 3)
                for n in range(4):
                    t, ahead = s5_t(i, T_Y + n)
                    bank = claim(pe, t, ahead)
                    for j in range(2):
                        g = 2 * (2 * (n // 2) + j) + n % 2
                        rows = slice(64 * (g % 2), 64 * (g % 2) + 64)
                        o = bank[0:LCH, j * P:(j + 1) * P]
                        pe.matmul(o, s5_u[:, g, :], s5_M[:, g, :], start=True, stop=False)
                        for d in range(2):
                            for c in range(2):
                                last = pe.matmul(o, s5_s[rows, d, c, g // 2, :], s5_E[rows, d, c, g // 2, :], start=False,
                                                 stop=(d == 1 and c == 1))
                    fill(last, t)
                for n in range(4):
                    emptied(pe, *s5_t(i, T_Y + n))
                for n in range(2):
                    t, ahead = s5_t(i, T_YB + n)
                    bank = claim(pe, t, ahead)
                    pe.nop(nofuse=True)
                    for j in range(4):
                        tk = 4 * n + j
                        last = pe.transpose(bank[:, j * LCH:(j + 1) * LCH], s5_ytok[0:LCH, tk * P:(tk + 1) * P], ident[0:LCH, 0:LCH])
                    fill(last, t)

            s5_pe_tokens(0, 0)
            with pe.Fori(0, 7) as i:
                s5_pe_sums(i)
                s5_pe_inside(i)
                s5_pe_tokens(i + 1, i)
                s5_pe_y(i)
            s5_pe_sums(7)
            s5_pe_inside(7)
            s5_pe_y(7)
            ada1_products(pe, 4)
            for j in range(2):
                w = [block(pe, block0["glu"] + 2 * j + half, KD) for half in range(2)]
                for m in range(4):
                    for half in range(2):
                        t = ticket0["glu"] + 8 * j + 2 * m + half
                        bank = claim(pe, t)
                        for k in range(KD):
                            pe.wait_ge(S("gelu"), k + 1)
                            last = pe.matmul(bank[:, :], w[half][:, k, m * P:(m + 1) * P], hT[:, k, 0:NL],
                                             start=(k == 0), stop=(k == KD - 1))
                        fill(last, t)

            norm_sums(pe, "l1b", TBL, hT)
            ada1_products(pe, 5)
            for k in range(KD):
                pe.wait_ge(S("l1b_ready"), k + 1)
            mlp_products(pe, 1, TBL)
            norm_sums(pe, "mix", TBL, hT)
            for name, blk, count in (("qkv", "w_in2", 3), ("zg", "w_in2", 1), ("ab", "w_ab", 1), ("xr", "w_xg", 1), ("gate", "w_xg", 1)):
                for j in range(count):
                    bi = block0[blk] + j + (3 if name == "zg" else 1 if name == "gate" else 0)
                    if name == "ab":
                        w = block(pe, bi, KD, n=8)
                        bank = claim(pe, ticket0["ab"])
                        for t in range(NTL):
                            for k in range(KD):
                                last = pe.matmul(bank[:, 8 * t:8 * t + 8], hT[:, k, t * P:(t + 1) * P], w[:, k, :],
                                                 start=(k == 0), stop=(k == KD - 1))
                        fill(last, ticket0["ab"])
                        continue
                    w = block(pe, bi, KD)
                    for m in range(4):
                        t = ticket0[name] + 4 * j + m
                        bank = claim(pe, t)
                        for k in range(KD):
                            pe.wait_ge(S("mix_mul"), k + 1)
                            last = pe.matmul(bank[:, :], w[:, k, m * P:(m + 1) * P], hT[:, k, 0:NL], start=(k == 0), stop=(k == KD - 1))
                        fill(last, t)
            pe.wait_ge(S("mix2_landed"), 16 * MIX2_LOADS)
            for a, name in enumerate(("lru_r", "lru_i")):
                for m in range(4):
                    emptied(pe, ticket0["xr"] + m)
                    t = ticket0[name] + m
                    fill(pe.matmul(claim(pe, t)[:, :], lru_w[:, a, m, :], xrT[:, m, :], start=True, stop=True), t)
            for m in range(8):
                pe.wait_ge(S("gq_sq"), m + 1)
                t = ticket0["gnorm"] + m
                fill(pe.matmul(claim(pe, t)[:, :], ones[:, :], qk_sq[:, m, :], start=True, stop=True), t)
            for name, m0 in (("ktok", 4), ("vtok", 8)):
                if name == "ktok":
                    pe.wait_ge(S("g_normed"), 8)
                else:
                    pe.wait_ge(S("qkv_silu"), 12)
                for t in range(NTL):
                    tk = ticket0[name] + t
                    bank = claim(pe, tk)
                    for h in range(4):
                        last = pe.transpose(bank[:, h * P:(h + 1) * P], qkvT[:, m0 + h, t * P:(t + 1) * P], ident[:, :])
                    fill(last, tk)
            pe.wait_ge(S("g_masks"), 16 * 9)
            pe.wait_ge(S("g_ready"), 1)
            for pair in range(2):
                for tt in (2 * pair, 2 * pair + 1):
                    t0, x = ticket0[f"gpre{tt}"], tt % 2
                    tok = slice(tt * P, (tt + 1) * P)
                    pe.wait_ge(S("g_bcast"), tt + 1)
                    bank = claim(pe, t0)
                    pe.matmul(bank[:, 0:4], tri_incl, gt[:, G_G, tt, :], start=True, stop=True)
                    pe.matmul(bank[:, 4:8], g_suffix, gt[:, G_G, tt, :], start=True, stop=True)
                    for h in range(4):
                        last = pe.matmul(bank[:, 8 + 2 * h:10 + 2 * h], g_bc[:, h, :], g_ind, start=True, stop=True)
                    fill(last, t0)
                    bank = claim(pe, t0 + 1)
                    for h in range(4):
                        last = pe.matmul(bank[:, h * P:(h + 1) * P], g_bc[:, h, :], tri_incl, start=True, stop=True)
                    fill(last, t0 + 1)
                    pe.wait_ge(S("g_kb"), tt + 1)
                    bank = claim(pe, t0 + 2)
                    for h in range(4):
                        last = pe.transpose(bank[:, h * P:(h + 1) * P], g_kw[:, h, :], ident[:, :])
                    fill(last, t0 + 2)
                    emptied(pe, t0 + 2)
                    bank = claim(pe, t0 + 3)
                    for h in range(4):
                        last = pe.matmul(bank[:, h * P:(h + 1) * P], qkvT[:, 4 + h, tok], g_kbT[:, h, :], start=True, stop=True)
                    fill(last, t0 + 3)
                    bank = claim(pe, t0 + 4)
                    for h in range(4):
                        last = pe.matmul(bank[:, h * P:(h + 1) * P], qkvT[:, 4 + h, tok], qkvT[:, h, tok], start=True, stop=True)
                    fill(last, t0 + 4)
                for lv in range(6):
                    t0 = ticket0[f"inv{pair}_{lv}"]
                    for x in range(2):
                        pe.wait_ge(S("g_level"), 12 * pair + 2 * lv + x + 1)
                        if lv > 0:
                            emptied(pe, ticket0[f"inv{pair}_{lv - 1}"] + 2 + 2 * x)
                            emptied(pe, ticket0[f"inv{pair}_{lv - 1}"] + 3 + 2 * x)
                        else:
                            pe.wait_ge(S("g_eye"), pair + 1)
                        bank = claim(pe, t0 + x)
                        for h in range(4):
                            last = pe.matmul(bank[:, h * P:(h + 1) * P], g_lvl[:, x, h, :], inv_x[:, x, h, :], start=True, stop=True)
                        fill(last, t0 + x)
                    for x in range(2):
                        emptied(pe, t0 + x)
                        bank = claim(pe, t0 + 2 + 2 * x)
                        for h in range(4):
                            last = pe.matmul(bank[:, h * P:(h + 1) * P], inv_xt[:, x, h, :], inv_y[:, x, h, :], start=True, stop=True)
                        fill(last, t0 + 2 + 2 * x)
                        bank = claim(pe, t0 + 3 + 2 * x)
                        for h in range(4):
                            last = pe.matmul(bank[:, h * P:(h + 1) * P], inv_y[:, x, h, :], inv_xt[:, x, h, :], start=True, stop=True)
                        fill(last, t0 + 3 + 2 * x)
                for tt in (2 * pair, 2 * pair + 1):
                    t0, x = ticket0[f"uw{tt}"], tt % 2
                    for b in range(4):
                        emptied(pe, ticket0[f"inv{pair}_5"] + 2 + b)
                    emptied(pe, ticket0["vtok"] + tt)
                    bank = claim(pe, t0)
                    for h in range(4):
                        last = pe.matmul(bank[:, h * P:(h + 1) * P], inv_xt[:, x, h, :], u_tok[:, tt, h, :], start=True, stop=True)
                    fill(last, t0)
                    pe.wait_ge(S("g_kw"), tt + 1)
                    bank = claim(pe, t0 + 1)
                    for h in range(4):
                        last = pe.matmul(bank[:, h * P:(h + 1) * P], g_kw[:, h, :], inv_xt[:, x, h, :], start=True, stop=True)
                    fill(last, t0 + 1)
            pe.wait_ge(S("g_qdec"), 4)
            pe.wait_ge(S("g_kdec"), 4)
            for n in range(8):
                tt, r = n // 2, GHALF[n % 2]
                tok = slice(n * GCH, (n + 1) * GCH)
                t0 = ticket0["gscan"] + 3 * n
                pe.wait_ge(S("g_state"), 4 * n + 1)
                if n % 2 == 0:
                    emptied(pe, ticket0[f"uw{tt}"] + 1)
                for h in range(4):
                    pe.wait_ge(S("g_state"), 4 * n + 1 if n == 0 else 4 * (n - 1) + 1 + h + 1)
                bank = claim(pe, t0)
                for h in range(4):
                    last = pe.matmul(bank[r, h * P:(h + 1) * P], wT[:, h, tok], g_state[:, h, :], start=True, stop=True)
                fill(last, t0)
                emptied(pe, t0)
                bank = claim(pe, t0 + 1)
                for h in range(4):
                    o = bank[:, h * GCH:(h + 1) * GCH]
                    pe.matmul(o, g_state[:, h, :], qkvT[:, h, tok], start=True, stop=False)
                    last = pe.matmul(o, v_new[r, h * P:(h + 1) * P], attnT[r, tt, h, r], start=False, stop=True)
                fill(last, t0 + 1)
                bank = claim(pe, t0 + 2)
                for h in range(4):
                    last = pe.matmul(bank[:, h * P:(h + 1) * P], k_tok[r, tt, h, :], v_new[r, h * P:(h + 1) * P], start=True, stop=True)
                fill(last, t0 + 2)
            for m in range(4):
                pe.wait_ge(S("o_sq"), m + 1)
                t = ticket0["norm_o"] + m
                fill(pe.matmul(claim(pe, t)[:, :], ones[:, :], qkvT[:, m, :], start=True, stop=True), t)
            for j in range(2):
                w = block(pe, block0["w_out2"] + j, 8)
                for m in range(4):
                    t = ticket0["w_out2"] + 4 * j + m
                    bank = claim(pe, t)
                    for k in range(8):
                        if j == 0 and m == 0:
                            pe.wait_ge(S("y_gdn"), min(k + 1, 4))
                        last = pe.matmul(bank[:, :], w[:, k, m * P:(m + 1) * P], mix2[:, k, :], start=(k == 0), stop=(k == 7))
                    fill(last, t)
            pe.wait_ge(S("mem_landed"), 32)
            for n in range(4):
                t, g = n // 2, n % 2
                bank = claim(pe, ticket0["mem_in"] + n)
                for j in range(4):
                    last = pe.transpose(bank[:, j * P:(j + 1) * P], mem_in[:, t, (4 * g + j) * P:(4 * g + j + 1) * P], ident[:, :])
                fill(last, ticket0["mem_in"] + n)
            norm_sums(pe, "mem", TBM, mem_h)
            pe.wait_ge(S("mem_mul"), KD)
            for j in range(2):
                w = block(pe, block0["xkv"] + j, KD)
                for n in range(2):
                    t = ticket0["xk"] + 2 * j + n
                    bank = claim(pe, t)
                    for m in range(2):
                        for k in range(KD):
                            last = pe.matmul(bank[:, m * MEM:(m + 1) * MEM], w[:, k, (2 * n + m) * P:(2 * n + m + 1) * P], mem_h[:, k, :],
                                             start=(k == 0), stop=(k == KD - 1))
                    fill(last, t)
            for j in range(2):
                w = block(pe, block0["xkv"] + 2 + j, KD)
                for tt in range(2):
                    t = ticket0["xv"] + 2 * j + tt
                    bank = claim(pe, t)
                    for k in range(KD):
                        last = pe.matmul(bank[:, :], mem_h[:, k, tt * P:(tt + 1) * P], w[:, k, :], start=(k == 0), stop=(k == KD - 1))
                    fill(last, t)
            norm_sums(pe, "xat", TBL, hT)
            for j in range(2):
                w = block(pe, block0["xq"] + j, KD)
                for m in range(4):
                    t = ticket0["xq"] + 4 * j + m
                    bank = claim(pe, t)
                    for k in range(KD):
                        pe.wait_ge(S("xat_mul"), k + 1)
                        last = pe.matmul(bank[:, :], w[:, k, m * P:(m + 1) * P], hT[:, k, 0:NL], start=(k == 0), stop=(k == KD - 1))
                    fill(last, t)
            for step, n in XAT_ORDER:
                t, h, tok = ticket0[f"{step}{n}"], n // 4, slice(n % 4 * P, (n % 4 + 1) * P)
                bank = None
                if step == "xscore":
                    for c in range(2):
                        emptied(pe, ticket0["xq"] + 2 * h + c)
                    emptied(pe, ticket0["xk"] + h)
                    bank = claim(pe, t)
                    for c in range(2):
                        last = pe.matmul(bank[:, 0:MEM], xqT[:, 2 * h + c, tok], xkT[:, 2 * h + c, :], start=(c == 0), stop=(c == 1))
                elif step == "xturn":
                    pe.wait_ge(S("xat_prob"), n + 1)
                    bank = claim(pe, t)
                    for j in range(2):
                        last = pe.transpose(bank[:, j * P:(j + 1) * P], xprob[:, n % 2, j * P:(j + 1) * P], ident[:, :])
                else:
                    emptied(pe, ticket0[f"xturn{n}"])
                    for tt in range(2):
                        emptied(pe, ticket0["xv"] + 2 * (h // 2) + tt)
                    bank = claim(pe, t)
                    for c in range(2):
                        for tt in range(2):
                            last = pe.matmul(bank[:, c * P:(c + 1) * P], xv_tok[:, tt, h * XDH + c * P:h * XDH + (c + 1) * P], xprobT[:, n % 2, tt, :],
                                             start=(tt == 0), stop=(tt == 1))
                fill(last, t)
            for j in range(2):
                w = block(pe, block0["wo"] + j, KD)
                for m in range(4):
                    t = ticket0["wo"] + 4 * j + m
                    bank = claim(pe, t)
                    for k in range(KD):
                        if j == 0 and m == 0:
                            for qt in range(4):
                                emptied(pe, ticket0[f"xout{4 * (k // 2) + qt}"])
                        last = pe.matmul(bank[:, :], w[:, k, m * P:(m + 1) * P], xoT[:, k, :], start=(k == 0), stop=(k == KD - 1))
                    fill(last, t)
            pe.wait_ge(S("peer_landed"), 16 * 3)
            for n in range(4):
                bank = claim(pe, ticket0["subk"] + n)
                for v in range(4):
                    last = pe.transpose(bank[:, v * P:(v + 1) * P], sub_rows[:, 4 * n + v, :], ident[:, :])
                fill(last, ticket0["subk"] + n)
            norm_sums(pe, "ffn", TBL, hT)
            for j in range(4):
                w = block(pe, block0["peer_wq"] + j, KD)
                for v in range(4):
                    t = ticket0[f"pq{j}"] + v
                    bank = claim(pe, t)
                    for k in range(KD):
                        pe.wait_ge(S("ffn_mul"), k + 1)
                        last = pe.matmul(bank[:, :], w[:, k, v * P:(v + 1) * P], hT[:, k, 0:NL], start=(k == 0), stop=(k == KD - 1))
                    fill(last, t)
                emptied(pe, ticket0["subk"] + j)
                for t in range(NTL):
                    tk = ticket0[f"psc{j}"] + t
                    for v in range(4):
                        emptied(pe, ticket0[f"pq{j}"] + v)
                    bank = claim(pe, tk)
                    for v in range(4):
                        last = pe.matmul(bank[:, v * P:(v + 1) * P], pqT[:, j % 2, v, t * P:(t + 1) * P], subT[:, 4 * j + v, :], start=True, stop=True)
                    fill(last, tk)
            for n in range(8):
                tk, t = ticket0["htok"] + n, n // 2
                bank = claim(pe, tk)
                for c in range(4):
                    last = pe.transpose(bank[:, c * P:(c + 1) * P], hT[:, 4 * (n % 2) + c, t * P:(t + 1) * P], ident[:, :])
                fill(last, tk)
            pe.wait_ge(S("wide_ident"), 1)
            for T_ in range(NTL):
                banks = [claim(pe, ticket0["ffn"] + 2 * T_ + g) for g in range(2)]

                def residual(g, c):
                    return pe.matmul(banks[g][:, :], xT[:, 4 * g + c, T_ * P:(T_ + 1) * P], wide_ident[:, (3 - c) * P:(7 - c) * P],
                                     start=(c == 0), stop=(c == 3))

                for g in range(2):
                    for c in range(3):
                        residual(g, c)
                with pe.Fori(0, EGROUPS) as i:
                    for s in range(ERING):
                        pe.wait_ge(S(f"v_landed{s}"), i * 16 + 16 * (EGROUPS * T_ + 1))
                        pe.wait_ge(S("diag_ready"), i * ERING + T_ * EXPERTS + s + 1)
                        pe.matmul(banks[0][:, :], diag[:, s, :], v_row[s][:, 0:512], start=False, stop=False)
                        pe.matmul(banks[1][:, :], diag[:, s, :], v_row[s][:, 512:1024], start=False, stop=False).then_inc(S("v_used"), 1)
                for g in range(2):
                    fill(residual(g, 3), ticket0["ffn"] + 2 * T_ + g)


def kernel(**inputs):
    import numpy as _np
    import concourse.bacc as _bacc
    from concourse import mybir as _mybir
    from concourse.bass_utils import run_bass_kernel_spmd as _run

    nc = _bacc.Bacc("TRN2", target_bir_lowering=False, num_devices=1)
    arrays, aps = {}, {}
    for name, value in inputs.items():
        a = _np.ascontiguousarray(value)
        arrays[f"in_{name}"] = a
        aps[name] = nc.dram_tensor(f"in_{name}", a.shape, _mybir.dt.from_np(a.dtype), kind="ExternalInput").ap()
    table = _np.concatenate(list(shape_constants().values()), axis=1)
    arrays["shape_consts"] = table
    consts = nc.dram_tensor("shape_consts", table.shape, _mybir.dt.float32, kind="ExternalInput").ap()
    out = nc.dram_tensor("out_0", (1, NL, D), _mybir.dt.float32, kind="ExternalOutput").ap()
    build(nc, aps, consts, out)
    r = _run(nc, [arrays], core_ids=[0])
    return r.results[0]["out_0"]
```
